# Optimizing a Trainium2 kernel written in Bass

```python
import math
import jax, jax.numpy as jnp
from jax import lax
import numpy as np

D_MODEL = 2048
BATCH = 1
SEQ = 256
DEPTH = 2
DEC_BATCH = 8
DEC_SEQ = 8
PAST_LEN = 256
PAGE_SIZE = 128

N_A_LAYERS = DEPTH // 2
N_B_LAYERS = DEPTH - N_A_LAYERS
POOL_WINDOWS = (2, 4, 8, 16)
N_POOL_GROUPS = len(POOL_WINDOWS)
POOL_GROUP_DIM = D_MODEL // N_POOL_GROUPS
POOL_BUF = max(POOL_WINDOWS) - 1
HEAD_DIM = 128
N_HEADS = D_MODEL // HEAD_DIM
N_KV_HEADS = 4
GQA_GROUP = N_HEADS // N_KV_HEADS
N_BRANCH = 3
CMP_BLOCK = 32
CMP_STRIDE = 16
CMP_HIDDEN = HEAD_DIM
SLC_BLOCK = 64
N_SELECT = 16
WINDOW = 512
WIN_QBLOCK = 128
SEL_QBLOCK = 16
N_BUCKETS = 32
MAX_DISTANCE = 128
D_FF = -(-8 * D_MODEL // (3 * 256)) * 256
RMS_EPS = 1e-6
SEL_BIG = 1e3
NEG_INF = -1e30

kernel_name = 'yoco_pool_nsa_decoder_step'

def _rmsnorm(x, g):
    xf = x.astype(jnp.float32)
    y = xf * lax.rsqrt(jnp.mean(xf * xf, axis=-1, keepdims=True) + RMS_EPS)
    return (y * g.astype(jnp.float32)).astype(x.dtype)

def _swiglu(x, w_in, w_out):
    g, u = jnp.split(x @ w_in, 2, axis=-1)
    return (jax.nn.silu(g) * u) @ w_out

def _ffn_sublayer(h, norms_l, w_in, w_out):
    return h + _rmsnorm(_swiglu(_rmsnorm(h, norms_l[2]), w_in, w_out), norms_l[3])

def _pool_mix(ext, pos0):
    S = ext.shape[1] - POOL_BUF
    xf = ext.astype(jnp.float32)
    c = jnp.pad(jnp.cumsum(xf, axis=1), ((0, 0), (1, 0), (0, 0)))
    pos = pos0 + jnp.arange(S)
    outs = []
    for g, w in enumerate(POOL_WINDOWS):
        sl = slice(g * POOL_GROUP_DIM, (g + 1) * POOL_GROUP_DIM)
        s = c[:, POOL_BUF + 1:POOL_BUF + 1 + S, sl] - c[:, POOL_BUF + 1 - w:POOL_BUF + 1 - w + S, sl]
        cnt = jnp.minimum(w, pos + 1).astype(jnp.float32)
        outs.append(s / cnt[None, :, None] - xf[:, POOL_BUF:, sl])
    return jnp.concatenate(outs, axis=-1).astype(ext.dtype)

def _pool_layer(h, buf, w_pool_l, scale_l, norms_l, w_in, w_out, pos0):
    B, S, _ = h.shape
    hn = _rmsnorm(h, norms_l[0])
    ext = jnp.concatenate([buf, hn], axis=1)
    mix = _pool_mix(ext, pos0).reshape(B, S, N_POOL_GROUPS, POOL_GROUP_DIM)
    mix = jnp.einsum('bsgc,gcd->bsgd', mix, w_pool_l).reshape(B, S, D_MODEL) * scale_l
    h = h + _rmsnorm(mix, norms_l[1])
    return _ffn_sublayer(h, norms_l, w_in, w_out), ext[:, -POOL_BUF:]

def _rel_bucket(dist):
    n = jnp.maximum(dist, 0)
    max_exact = N_BUCKETS // 2
    nf = jnp.maximum(n, 1).astype(jnp.float32)
    large = max_exact + (jnp.log(nf / max_exact) / math.log(MAX_DISTANCE / max_exact)
                         * (N_BUCKETS - max_exact)).astype(jnp.int32)
    large = jnp.minimum(large, N_BUCKETS - 1)
    return jnp.where(n < max_exact, n, large)

def _attn_probs(q, k, qpos, kpos, rel_bias, mask):
    Tq, Tk = qpos.shape[0], kpos.shape[0]
    logits = jnp.einsum('bqhgd,bkhd->bhgqk', q, k).astype(jnp.float32) * (HEAD_DIM ** -0.5)
    bias = rel_bias.astype(jnp.float32)[_rel_bucket(qpos[:, None] - kpos[None, :])]
    bias = bias.reshape(Tq, Tk, N_KV_HEADS, GQA_GROUP).transpose(2, 3, 0, 1)
    p = jax.nn.softmax(jnp.where(mask, logits + bias, NEG_INF), axis=-1)
    return jnp.where(mask, p, 0.0)

def _window_mask(qpos, kpos):
    d = qpos[:, None] - kpos[None, :]
    return (d >= 0) & (d < WINDOW) & (kpos[None, :] >= 0)

def _shared_kv(h, kv_norm, w_kv):
    B, S, _ = h.shape
    return (_rmsnorm(h, kv_norm) @ w_kv).reshape(B, S, N_BRANCH, 2, N_KV_HEADS, HEAD_DIM)

def _compress(raw, cmp_pos, cmp_w1, cmp_b1, cmp_w2):
    B, T = raw.shape[:2]
    n_sub = T // CMP_STRIDE
    sub = raw[:, :n_sub * CMP_STRIDE].reshape(B, n_sub, CMP_STRIDE, 2, N_KV_HEADS, HEAD_DIM)
    pe = cmp_pos.transpose(1, 0, 2)[:, :, None, :]
    first = jnp.einsum('bnjche,cjef->bnchf', sub + pe[:CMP_STRIDE], cmp_w1[:, :CMP_STRIDE])
    second = jnp.einsum('bnjche,cjef->bnchf', sub + pe[CMP_STRIDE:], cmp_w1[:, CMP_STRIDE:])
    hid = jax.nn.gelu(first[:, :-1] + second[:, 1:] + cmp_b1[:, None, :])
    return jnp.einsum('bnchf,cfe->bnche', hid, cmp_w2)

def _overlap(n_cmp, n_slc):
    cs = jnp.arange(n_cmp) * CMP_STRIDE
    ce = cs + CMP_BLOCK - 1
    ss = jnp.arange(n_slc) * SLC_BLOCK
    se = ss + SLC_BLOCK - 1
    ov = jnp.minimum(ce[:, None], se[None, :]) - jnp.maximum(cs[:, None], ss[None, :]) + 1
    return jnp.maximum(ov, 0).astype(jnp.float32) / CMP_BLOCK

def _select_blocks(p_c, qpos, n_slc):
    imp = jnp.einsum('bhgqk,kj->bqhj', p_c, _overlap(p_c.shape[-1], n_slc))
    j = jnp.arange(n_slc)[None, :]
    qb = (qpos // SLC_BLOCK)[:, None]
    prio = (2 * (j == qb) + (j == qb - 1) + (j == 0)).astype(jnp.float32)
    score = jnp.where((j <= qb)[None, :, None, :], imp + SEL_BIG * prio[None, :, None, :], -SEL_BIG)
    _, sel = lax.top_k(score, min(N_SELECT, n_slc))
    return sel

def _to_blocks(rows):
    B, T = rows.shape[:2]
    n_slc = -(-T // SLC_BLOCK)
    rows = jnp.pad(rows, ((0, 0), (0, n_slc * SLC_BLOCK - T), (0, 0), (0, 0), (0, 0)))
    return rows.reshape(B, n_slc, SLC_BLOCK, 2, N_KV_HEADS, HEAD_DIM).transpose(0, 3, 4, 1, 2, 5)

def _sel_attend(q, kvb, sel, qpos, rel_bias):
    B = q.shape[0]
    bi = jnp.arange(B)[:, None, None, None]
    hi = jnp.arange(N_KV_HEADS)[None, None, :, None]
    k = kvb[:, 0][bi, hi, sel]
    v = kvb[:, 1][bi, hi, sel]
    logits = jnp.einsum('bchgd,bchkld->bchgkl', q, k).astype(jnp.float32) * (HEAD_DIM ** -0.5)
    kpos = sel[..., None] * SLC_BLOCK + jnp.arange(SLC_BLOCK)
    qp = qpos[None, :, None, None, None]
    table = rel_bias.astype(jnp.float32).reshape(N_BUCKETS, N_KV_HEADS, GQA_GROUP)
    bias = jnp.moveaxis(table[_rel_bucket(qp - kpos), hi[..., None]], -1, 3)
    mask = (kpos <= qp)[:, :, :, None]
    shp = logits.shape
    logits = jnp.where(mask, logits + bias, NEG_INF).reshape(*shp[:4], -1)
    p = jax.nn.softmax(logits, axis=-1).reshape(shp)
    return jnp.einsum('bchgkl,bchkld->bchgd', p.astype(v.dtype), v)

def _sel_prompt(q, sel, kvb, rel_bias):
    B, T = q.shape[:2]
    C = SEL_QBLOCK if T % SEL_QBLOCK == 0 else T
    n = T // C
    qc = jnp.swapaxes(q.reshape(B, n, C, *q.shape[2:]), 0, 1)
    sc = jnp.swapaxes(sel.reshape(B, n, C, *sel.shape[2:]), 0, 1)
    pc = jnp.arange(T).reshape(n, C)
    o = lax.map(lambda a: _sel_attend(a[0], kvb, a[1], a[2], rel_bias), (qc, sc, pc))
    return jnp.swapaxes(o, 0, 1).reshape(q.shape)

def _sel_sample(q, sel, new_rows, cache_slc_kv, page_table, qpos, rel_bias):
    def one(a):
        qb, sb, nb, pt = a
        past = cache_slc_kv[pt].reshape(-1, 2, N_KV_HEADS, HEAD_DIM)
        rows = jnp.concatenate([past, nb], axis=0)[None]
        return _sel_attend(qb[None], _to_blocks(rows), sb[None], qpos, rel_bias)[0]
    return lax.map(one, (q, sel, new_rows, page_table))

def _window_prompt(q, kvw, rel_bias):
    B, T = q.shape[:2]
    nb = T // WIN_QBLOCK
    kvp = jnp.pad(kvw, ((0, 0), (WINDOW, 0), (0, 0), (0, 0), (0, 0)))
    qb = jnp.swapaxes(q.reshape(B, nb, WIN_QBLOCK, *q.shape[2:]), 0, 1)

    def block(a):
        c, qc = a
        start = c * WIN_QBLOCK
        kv = lax.dynamic_slice_in_dim(kvp, start, WINDOW + WIN_QBLOCK, axis=1)
        qpos = start + jnp.arange(WIN_QBLOCK)
        kpos = start - WINDOW + jnp.arange(WINDOW + WIN_QBLOCK)
        p = _attn_probs(qc, kv[:, :, 0], qpos, kpos, rel_bias, _window_mask(qpos, kpos))
        return jnp.einsum('bhgqk,bkhd->bqhgd', p.astype(kv.dtype), kv[:, :, 1])

    o = lax.map(block, (jnp.arange(nb), qb))
    return jnp.swapaxes(o, 0, 1).reshape(q.shape)

def _nsa_layer(h, ckv, qpos, n_slc, sel_fn, win_fn, w_q_l, w_o_l, norms_l, rel_bias, w_in, w_out):
    B, S, _ = h.shape
    hn = _rmsnorm(h, norms_l[0])
    proj = hn @ w_q_l
    q = proj[..., :N_HEADS * HEAD_DIM].reshape(B, S, N_KV_HEADS, GQA_GROUP, HEAD_DIM)
    gates = jax.nn.sigmoid(proj[..., N_HEADS * HEAD_DIM:].astype(jnp.float32))
    gates = gates.reshape(B, S, N_BRANCH, N_KV_HEADS, GQA_GROUP, 1)
    kpos_c = jnp.arange(ckv.shape[1]) * CMP_STRIDE + CMP_BLOCK - 1
    p_c = _attn_probs(q, ckv[:, :, 0], qpos, kpos_c, rel_bias, kpos_c[None, :] <= qpos[:, None])
    o_c = jnp.einsum('bhgqk,bkhd->bqhgd', p_c.astype(ckv.dtype), ckv[:, :, 1])
    sel = _select_blocks(p_c, qpos, n_slc)
    o_s = sel_fn(q, sel)
    o_w = win_fn(q)
    o = gates[:, :, 0] * o_c + gates[:, :, 1] * o_s + gates[:, :, 2] * o_w
    out = o.astype(h.dtype).reshape(B, S, N_HEADS * HEAD_DIM) @ w_o_l
    h = h + _rmsnorm(out, norms_l[1])
    return _ffn_sublayer(h, norms_l, w_in, w_out)

def setup_inputs(seed: int = 0) -> dict:
    key = jax.random.key(seed)
    ks = jax.random.split(key, 24)
    f32 = jnp.float32
    n_pages = PAST_LEN // PAGE_SIZE
    n_phys = -(-5 * DEC_BATCH * n_pages // 4)
    win_buf = min(WINDOW, PAST_LEN)
    qcols = N_HEADS * HEAD_DIM + N_BRANCH * N_HEADS
    kvcols = N_BRANCH * 2 * N_KV_HEADS * HEAD_DIM

    def nrm(k, shape, scale=1.0):
        return scale * jax.random.normal(k, shape, f32)

    perm = jax.random.permutation(ks[6], n_phys)
    page_table = perm[:DEC_BATCH * n_pages].reshape(DEC_BATCH, n_pages).astype(jnp.int32)
    return {
        'x_prompt': nrm(ks[0], (BATCH, SEQ, D_MODEL)),
        'x_sample': nrm(ks[1], (DEC_BATCH, DEC_SEQ, D_MODEL)),
        'state_pool': nrm(ks[2], (N_A_LAYERS, DEC_BATCH, POOL_BUF, D_MODEL)),
        'cache_cmp_kv': nrm(ks[3], (n_phys, PAGE_SIZE, 2, N_KV_HEADS, HEAD_DIM)),
        'cache_slc_kv': nrm(ks[4], (n_phys, PAGE_SIZE, 2, N_KV_HEADS, HEAD_DIM)),
        'state_win_kv': nrm(ks[5], (DEC_BATCH, win_buf, 2, N_KV_HEADS, HEAD_DIM)),
        'page_table': page_table,
        'norms': 1.0 + nrm(ks[7], (DEPTH, 4, D_MODEL), 0.05),
        'w_pool': nrm(ks[8], (N_A_LAYERS, N_POOL_GROUPS, POOL_GROUP_DIM, POOL_GROUP_DIM), POOL_GROUP_DIM ** -0.5),
        'pool_scale': 1.0 + nrm(ks[9], (N_A_LAYERS, D_MODEL), 0.1),
        'kv_norm': 1.0 + nrm(ks[10], (D_MODEL,), 0.05),
        'w_kv': nrm(ks[11], (D_MODEL, kvcols), D_MODEL ** -0.5),
        'cmp_pos': nrm(ks[12], (2, CMP_BLOCK, HEAD_DIM), 0.1),
        'cmp_w1': nrm(ks[13], (2, CMP_BLOCK, HEAD_DIM, CMP_HIDDEN), (CMP_BLOCK * HEAD_DIM) ** -0.5),
        'cmp_b1': nrm(ks[14], (2, CMP_HIDDEN), 0.01),
        'cmp_w2': nrm(ks[15], (2, CMP_HIDDEN, HEAD_DIM), CMP_HIDDEN ** -0.5),
        'w_q': nrm(ks[16], (N_B_LAYERS, D_MODEL, qcols), D_MODEL ** -0.5),
        'w_o': nrm(ks[17], (N_B_LAYERS, N_HEADS * HEAD_DIM, D_MODEL), (N_HEADS * HEAD_DIM) ** -0.5),
        'rel_bias': nrm(ks[18], (N_BUCKETS, N_HEADS), 0.2),
        'w_ffn_in': nrm(ks[19], (DEPTH, D_MODEL, 2 * D_FF), D_MODEL ** -0.5),
        'w_ffn_out': nrm(ks[20], (DEPTH, D_FF, D_MODEL), D_FF ** -0.5),
    }

def reference(x_prompt, x_sample, state_pool, cache_cmp_kv, cache_slc_kv, state_win_kv, page_table,
              norms, w_pool, pool_scale, kv_norm, w_kv, cmp_pos, cmp_w1, cmp_b1, cmp_w2,
              w_q, w_o, rel_bias, w_ffn_in, w_ffn_out):
    B, S, _ = x_prompt.shape
    DB, DS, _ = x_sample.shape
    past_len = page_table.shape[1] * cache_slc_kv.shape[1]
    win_buf = state_win_kv.shape[1]

    h = x_prompt
    qpos_p = jnp.arange(S)
    pool_p = []
    for i in range(DEPTH):
        if i < N_A_LAYERS:
            zeros = jnp.zeros((B, POOL_BUF, D_MODEL), h.dtype)
            h, st = _pool_layer(h, zeros, w_pool[i], pool_scale[i], norms[i], w_ffn_in[i], w_ffn_out[i], 0)
            pool_p.append(st)
        else:
            if i == N_A_LAYERS:
                kv_p = _shared_kv(h, kv_norm, w_kv)
                ckv_p = _compress(kv_p[:, :, 0], cmp_pos, cmp_w1, cmp_b1, cmp_w2)
                kvb_p = _to_blocks(kv_p[:, :, 1])
                kvw_p = kv_p[:, :, 2]
            j = i - N_A_LAYERS
            h = _nsa_layer(h, ckv_p, qpos_p, kvb_p.shape[3],
                           lambda q, sel: _sel_prompt(q, sel, kvb_p, rel_bias),
                           lambda q: _window_prompt(q, kvw_p, rel_bias),
                           w_q[j], w_o[j], norms[i], rel_bias, w_ffn_in[i], w_ffn_out[i])
    y_prompt = h
    pad_front = max(win_buf - S, 0)
    win_state_p = jnp.pad(kvw_p, ((0, 0), (pad_front, 0), (0, 0), (0, 0), (0, 0)))[:, -win_buf:]

    h = x_sample
    qpos_s = past_len + jnp.arange(DS)
    pool_s = []
    for i in range(DEPTH):
        if i < N_A_LAYERS:
            h, st = _pool_layer(h, state_pool[i], w_pool[i], pool_scale[i], norms[i],
                                w_ffn_in[i], w_ffn_out[i], past_len)
            pool_s.append(st)
        else:
            if i == N_A_LAYERS:
                kv_s = _shared_kv(h, kv_norm, w_kv)

                def _cmp_one(a):
                    pt, new = a
                    past = cache_cmp_kv[pt].reshape(-1, 2, N_KV_HEADS, HEAD_DIM)
                    rows = jnp.concatenate([past, new], axis=0)[None]
                    return _compress(rows, cmp_pos, cmp_w1, cmp_b1, cmp_w2)[0]

                ckv_s = lax.map(_cmp_one, (page_table, kv_s[:, :, 0]))
                n_slc_s = -(-(past_len + DS) // SLC_BLOCK)
                win_rows = jnp.concatenate([state_win_kv, kv_s[:, :, 2]], axis=1)
                kpos_w = past_len - win_buf + jnp.arange(win_buf + DS)
                wmask = _window_mask(qpos_s, kpos_w)
            j = i - N_A_LAYERS
            h = _nsa_layer(h, ckv_s, qpos_s, n_slc_s,
                           lambda q, sel: _sel_sample(q, sel, kv_s[:, :, 1], cache_slc_kv, page_table, qpos_s, rel_bias),
                           lambda q: jnp.einsum('bhgqk,bkhd->bqhgd',
                                                _attn_probs(q, win_rows[:, :, 0], qpos_s, kpos_w, rel_bias, wmask).astype(win_rows.dtype),
                                                win_rows[:, :, 1]),
                           w_q[j], w_o[j], norms[i], rel_bias, w_ffn_in[i], w_ffn_out[i])
    y_sample = h
    win_state_s = win_rows[:, -win_buf:]

    return (y_prompt, y_sample, jnp.stack(pool_p), jnp.stack(pool_s),
            kv_p[:, :, 0], kv_s[:, :, 0], kv_p[:, :, 1], kv_s[:, :, 1],
            win_state_p, win_state_s)


_drawn_inputs = setup_inputs


def setup_inputs(seed=0):
    import zlib

    import numpy as np

    out = dict(_drawn_inputs(seed))
    spreads = {}
    factors = {'cmp_b1': 8.0}
    for name, (base, spread) in spreads.items():
        noise = np.random.default_rng([zlib.crc32(name.encode()), seed]).standard_normal(out[name].shape)
        drawn = base * np.exp(spread * noise) if base else spread * noise
        out[name] = __import__('jax').numpy.asarray(drawn.astype(out[name].dtype))
    for name, factor in factors.items():
        out[name] = (out[name] * factor).astype(out[name].dtype)
    return out
```

```python
from contextlib import ExitStack

import numpy as np

import concourse.bass as bass
from concourse import mybir

F32 = mybir.dt.float32
F32R = mybir.dt.float32r
I32 = mybir.dt.int32
ALU = mybir.AluOpType
ACT = mybir.ActivationFunctionType
AX = mybir.AxisListType

P = 128
D = 2048
KT = D // P
SEQ, DB, DS = 256, 8, 8
NS = DB * DS
NT = SEQ + NS
PAST = 256
PAGE = 128
NPG = PAST // PAGE
DFF = 5632
HT = DFF // P
NQ = 4
HQ = HT // NQ
BUF = 15
EXT_P = BUF + SEQ
EXT_B = BUF + DS
EXT = EXT_P + DB * EXT_B
NG = 4
GC = KT // NG
NH, NKV, HD = 16, 4, 128
GQ = NH // NKV
NBR = 3
NBUCK = 32
CB, CS = 32, 16
NCMP = (PAST - CB) // CS + 1
NSUB = PAST // CS
EPS = 1e-6
SCALE = HD ** -0.5
NEG = -1e30
NEW = NS

PW = KT * P
PO = HQ * P
P_POOL, P_FFN0 = 0, NG
PER_Q = 2 * HQ + KT
P_KV = P_FFN0 + NQ * PER_Q
N_KVT = NBR * 2 * NKV
P_Q = P_KV + N_KVT
N_QT = NH + 1
P_WO = P_Q + N_QT
P_FFN1 = P_WO + KT
TOFF = KT - NG

C_ID, C_IM, C_HS, C_INV, C_RV = 0, 128, 192, 192 + 3 * 128, 192 + 3 * 128 + NG * NT
C_N = C_RV + 1
G_POOL, G_KV = 8, 9
NE = SEQ + PAST + DS - 1


def plan_sbuf(nc):
    lo = (nc.sbuf_base + 31) // 32 * 32
    region = {}
    for name, size in (("H", KT * NT * 4), ("Y", KT * NT * 4), ("HID", 32768), ("X", 2 * KT * NT * 4),
                       ("RAW", 2 * PW * 4), ("LO", 2 * PW * 4), ("HI", 2 * PW * 4), ("Z", 19712), ("S", 0)):
        region[name] = lo
        lo += size
    used = {}

    def at(name, where, shape, dt=F32, off=None):
        n = int(np.prod(shape[1:])) * 4
        start = used.get(where, 0) if off is None else off
        used[where] = start + (n + 31) // 32 * 32
        return nc.alloc_sbuf_tensor_at(name, list(shape), dt, offset=region[where] + start)

    return at


SW_S = PAST + NEW
SPANS_P = ((0, NCMP), (16, P), (144, P), (272, NCMP), (288, SEQ), (544, SEQ))
SPANS_S = ((0, NCMP), (16, SW_S), (16 + SW_S, SW_S))


def rep(ap, n):
    return ap.unsqueeze(1).broadcast_to([ap.shape[0], n, ap.shape[1]])


def spread(ap, n):
    return ap.unsqueeze(2).broadcast_to([ap.shape[0], ap.shape[1], n])


def pick(ap, off, step, n, w):
    return ap[:, off:off + n * step].rearrange("p (n s) -> p n s", n=n)[:, :, 0:w]


def build(nc, x, st, gains, consts, onehot, rel, w_pool, w_in0, w_in1, w_out0, w_out1, w_kv, w_q, w_o,
          cmp_data, cmp_w1, cmp_pos, cmp_b1, cmp_w2, slc_k, slc_kv, win_k, win_kv, pages,
          y_out, pool_p_out, pool_s_out, kv_out, win_out):
    at = plan_sbuf(nc)
    h = at("h", "H", [P, KT, NT])
    y = at("y", "Y", [P, KT, NT])
    qT = at("qT", "Y", [P, KT, NT], off=0)
    hid_hi = at("hid_hi", "HID", [P, HQ, NT], F32R)
    hid_lo = at("hid_lo", "HID", [P, HQ, NT], F32R)
    ext = at("ext", "HID", [P, KT, EXT], off=0)
    kvT = at("kvT", "HID", [P, N_KVT, NT], off=0)
    bias_s = at("bias_s", "HID", [P, PAST])
    bias_n = at("bias_n", "HID", [P, 2 * DB - 1, DS])
    x_hi = at("x_hi", "X", [P, KT, NT], F32R)
    x_lo = at("x_lo", "X", [P, KT, NT], F32R)
    w_raw = at("w_raw", "RAW", [P, 2, PW])
    w_lo = at("w_lo", "LO", [P, 2, PW], F32R)
    w_hi = at("w_hi", "HI", [P, 2, PW], F32R)
    NP_ALL = DB * NPG
    rowsK = at("rowsK", "RAW", [P, NP_ALL, CS, 32], off=0)
    w1K = at("w1K", "HI", [P, CB, P], off=0)
    rowsV = at("rowsV", "X", [P, NP_ALL, CS, 32], off=0)
    w1V = at("w1V", "Y", [P, CB, P], off=0)
    sub1 = at("sub1", "Y", [P, DB * NKV, NSUB])
    inv = at("inv", "Z", [P, NG, NT], off=0)
    winA = at("winA", "Z", [P, GC, EXT])
    winB = at("winB", "Z", [P, GC, EXT])
    w1Kp = at("w1Kp", "RAW", [P, CB, P], off=0)
    w1Vp = at("w1Vp", "LO", [P, CB, P], off=0)
    oh = at("oh", "X", [NBUCK + 1, 2, NE], off=0)
    tabL = at("tabL", "X", [NBUCK + 1, DS, P])
    vP = at("vP", "RAW", [P, 2, 2, NKV * HD], off=0)
    vN = at("vN", "RAW", [NS, 2, NKV * HD])
    vC = at("vC", "RAW", [NCMP, 2, NKV * HD])
    pastK = at("pastK", "LO", [P, 2, NKV, PAST], off=0)
    pastV = at("pastV", "LO", [P, 2, 2, NKV * HD])
    biasP = at("biasP", "HI", [P, NH, SEQ], off=0)
    SW = 816
    sc = at("sc", "Z", [P, 3, SW], off=0)
    pT = at("pT", "Z", [P, 2, 1024])
    cst = at("cst", "S", [P, C_INV])
    rv = at("rv", "S", [P, 1])
    ones = at("ones", "S", [P, P])
    gn = at("gn", "S", [P, 10, KT])
    acc = at("acc", "S", [P, NT])
    r = at("r", "S", [P, NT])
    root = acc
    sq = at("sq", "S", [P, 2, NT])
    xf = at("xf", "Z", [P, 2, NT], off=0)
    sg = at("sg", "Z", [P, NT])
    hb = at("hb", "Z", [P, NT])
    epsc = at("epsc", "S", [P, 1])
    pos = at("pos", "S", [P, 2, CB])
    b1 = at("b1", "S", [P, 2])
    b1e = at("b1e", "S", [P, 2])
    w2 = at("w2", "S", [P, 2, P])
    hcS = at("hcS", "S", [P, 2, DB * NKV * NCMP])
    kcS = at("kcS", "S", [P, DB * NKV * NCMP])
    sub0 = at("sub0", "S", [P, DB * NKV, NSUB])
    hcP = at("hcP", "S", [P, 2, NKV * NCMP])
    kcP = at("kcP", "S", [P, NKV * NCMP])
    vCP = at("vCP", "S", [NCMP, NKV * HD])
    tab = at("tab", "S", [NBUCK + 1, NH])
    biasC = at("biasC", "S", [P, 2, NH, NCMP])
    biasSC = at("biasSC", "S", [P, NCMP])
    gT = at("gT", "S", [P, NT])
    gP = at("gP", "S", [P, 2, 3 * NH])
    gtmp = at("gtmp", "Z", [P, 3, NS], off=0)
    qS = at("qS", "S", [P, DB, NH, DS])
    gS = at("gS", "S", [P, 3, DB])
    neg = at("neg", "S", [P, 3, 6])
    tot = at("tot", "S", [P, 3, 6])
    rec = at("rec", "S", [P, 3, 6])
    pgs = at("pgs", "S", [1, NP_ALL], I32)
    ident = cst[:, C_ID:C_ID + P]

    ps = nc.alloc_psum_tensor("ps", [P, 8, 512], F32)
    STAT = 7

    sem = nc.alloc_semaphore
    x_in, const_in, ext_in = sem("x_in"), sem("const_in"), sem("ext_in")
    pages_in, cmpK_in, cmpV_in = sem("pages_in"), sem("cmpK_in"), sem("cmpV_in")
    raw_in = [sem("raw_in0"), sem("raw_in1")]
    w1p_in, oh_in = sem("w1p_in"), sem("oh_in")
    pastK_in, pastV_in = [sem("pastK_in0"), sem("pastK_in1")], [sem("pastV_in0"), sem("pastV_in1")]
    states_out, rows_out, win_stored, y_stored = sem("states_out"), sem("rows_out"), sem("win_stored"), sem("y_stored")
    hi_made, lo_made, tile_made = sem("hi_made"), sem("lo_made"), sem("tile_made")
    bank_read = [sem("bank_read0"), sem("bank_read1")]
    hid_hi_made, hid_made, y_zero = sem("hid_hi_made"), sem("hid_made"), sem("y_zero")
    set_made, acc_made = sem("set_made"), sem("acc_made")
    sq_made, sq_used, stat_made, root_made, r_made = (sem(n) for n in ("sq_made", "sq_used", "stat_made",
                                                                       "root_made", "r_made"))
    yn_made, h_made = sem("yn_made"), sem("h_made")
    xf_made, xhi_made, x_made = sem("xf_made"), sem("xhi_made"), sem("x_made")
    ext_made, mix_made, mixhi_made = sem("ext_made"), sem("mix_made"), sem("mixhi_made")
    mix_ready = sem("mix_ready")
    cmp_sum, cmp_pre, cmp_hid, kc_sum, kc_made = (sem(n) for n in ("cmp_sum", "cmp_pre", "cmp_hid", "kc_sum",
                                                                   "kc_made"))
    b1_sum, b1_made = sem("b1_sum"), sem("b1_made")
    tab_made, tabL_made, bias_sum, bias_made = (sem(n) for n in ("tab_made", "tabL_made", "bias_sum", "bias_made"))
    vt_sum, vt_made = sem("vt_sum"), sem("vt_made")
    g_sum, g_made, gates_made = sem("g_sum"), sem("g_made"), sem("gates_made")
    s_made, s_read, max_made, exp_made, rec_made, p_made = (sem(n) for n in ("s_made", "s_read", "max_made",
                                                                             "exp_made", "rec_made", "p_made"))
    t_made, pTa_made, pTb_made, o_made, ohi_made, o_read = (sem(n) for n in ("t_made", "pTa_made", "pTb_made",
                                                                             "o_made", "ohi_made", "o_read"))
    vc_sum, vc_made, qS_made = sem("vc_sum"), sem("vc_made"), sem("qS_made")
    dve_chain, pool_chain = sem("dve_chain"), sem("pool_chain")

    block = nc.Block()
    block_ctx = ExitStack()
    block_ctx.enter_context(block)

    UNITS = NH + DB
    sub1p = sub0[:, 8:8 + NKV, :]

    def mix(i):
        return (winA if (i // GC) % 2 else winB)[:, i % GC, 0:NT]

    def tiles_before(c, half):
        if isinstance(half, int):
            n = c + 2 * half
            return n * GC if n <= NG else n + TOFF
        return half * 2 + (c + TOFF)

    @block.sync
    def _(sp):
        def panel(c, half, src, width):
            slot = c % 2
            if not isinstance(half, int) or c + 2 * half >= 2:
                sp.wait_ge(lo_made, half * 2 + (c - 1))
            sp.dma_start(w_raw[:, slot, 0:width], src).then_inc(raw_in[slot], 16)

        def section(c, n, src, width):
            with sp.Fori(0, n // 2) as i:
                for j in range(2):
                    panel(c + j, i, src[i * 2 + j], width)
            if n % 2:
                panel(c + n - 1, 0, src[n - 1], width)

        def ffn(c, w_in, w_out):
            with sp.Fori(0, NQ) as q:
                with sp.Fori(0, HQ) as i:
                    for j in range(2):
                        panel(c + j, q * (PER_Q // 2) + i, w_in[q * (2 * HQ) + i * 2 + j], PW)
                with sp.Fori(0, KT // 2) as i:
                    for j in range(2):
                        panel(c + 2 * HQ + j, q * (PER_Q // 2) + i, w_out[q * KT + i * 2 + j], PO)

        def page(p):
            return sp.value_load(pgs[0:1, p:p + 1], min_val=0, max_val=cmp_data.shape[1] - 1)

        sp.dma_start(h[:, :, :], x[:, :, :]).then_inc(x_in, 16)
        sp.dma_start(pgs[:, :], pages[:, :]).then_inc(pages_in, 16)
        sp.dma_start(gn[:, :, :], gains[:, :, :]).then_inc(const_in, 16)
        sp.dma_start(cst[:, :], consts[:, 0:C_INV]).then_inc(const_in, 16)
        sp.dma_start(rv[:, :], consts[:, C_RV:C_RV + 1], allow_slow_non_contiguous=True).then_inc(const_in, 16)
        sp.dma_start(inv[:, :, :], consts[:, C_INV:C_RV].rearrange("p (g t) -> p g t", g=NG)).then_inc(const_in, 16)
        sp.dma_start(pos[:, :, :], cmp_pos[:, :, :]).then_inc(const_in, 16)
        sp.dma_start(b1[:, :], cmp_b1[:, :]).then_inc(const_in, 16)
        sp.dma_start(w2[:, :, :], cmp_w2[:, :, :]).then_inc(const_in, 16)
        sp.dma_start(tab[0:NBUCK, :], rel[:, :]).then_inc(const_in, 16)
        for b in range(DB):
            o = EXT_P + b * EXT_B
            sp.dma_start(ext[:, :, o:o + BUF], st[:, :, b, :]).then_inc(ext_in, 16)
        sp.dma_start(w1K[:, :, :], cmp_w1[0]).then_inc(cmpK_in, 16)
        sp.wait_ge(pages_in, 16)
        for p in range(NP_ALL):
            sp.dma_start(rowsK[:, p, :, :], cmp_data[0, page(p)]).then_inc(cmpK_in, 16)
        sp.dma_start(w1V[:, :, :], cmp_w1[1]).then_inc(cmpV_in, 16)
        for p in range(NP_ALL):
            sp.dma_start(rowsV[:, p, :, :], cmp_data[1, page(p)]).then_inc(cmpV_in, 16)

        sp.wait_ge(cmp_sum, 1)
        for g in range(NG):
            panel(g, 0, w_pool[g], PW)
        ffn(P_FFN0, w_in0, w_out0)
        section(P_KV, N_KVT, w_kv, PW)
        section(P_Q, N_QT, w_q, PW)
        sp.wait_ge(bank_read[(P_Q - 1) % 2], (P_Q - 1 + TOFF) // 2 + 1)
        sp.wait_ge(bank_read[P_Q % 2], (P_Q - 2 + TOFF) // 2 + 1)
        sp.dma_start(kv_out[:, :, :], kvT[:, :, :]).then_inc(rows_out, 16)

        sp.wait_ge(lo_made, P_WO)
        sp.dma_start(w1Kp[:, :, :], cmp_w1[0]).then_inc(w1p_in, 16)
        sp.wait_ge(tile_made, P_WO + TOFF)
        sp.dma_start(w1Vp[:, :, :], cmp_w1[1]).then_inc(w1p_in, 16)
        sp.dma_start(oh[:, :, :], onehot[:, :, :]).then_inc(oh_in, 16)
        sp.wait_ge(cmp_sum, 4)

        def load_keys(b):
            if b:
                sp.wait_ge(s_made, NH + b)
            for p in range(NPG):
                sp.dma_start(pastK[:, 0, :, p * PAGE:(p + 1) * PAGE], slc_k[page(b * NPG + p)]).then_inc(pastK_in[b % 2], 16)
            sp.dma_start(pastK[:, 1, :, :], win_k[b]).then_inc(pastK_in[b % 2], 16)

        def load_values(b):
            if b:
                sp.wait_ge(o_made, NH + b)
            for p in range(NPG):
                sp.dma_start(pastV[:, 0, p, :], slc_kv[page(b * NPG + p), :, 1, :]).then_inc(pastV_in[b % 2], 16)
            sp.dma_start(pastV[:, 1, :, :], win_kv[b, :, 1, :].rearrange("(t p) n -> p t n", p=P)).then_inc(pastV_in[b % 2], 16)

        load_keys(0)
        load_values(0)
        for b in range(1, DB + 2):
            if b < DB:
                load_keys(b)
            if b >= 3:
                load_values(b - 2)

        sp.wait_ge(o_made, UNITS)
        section(P_WO, KT, w_o, PW)
        ffn(P_FFN1, w_in1, w_out1)
        sp.wait_ge(h_made, 4 * KT)
        sp.dma_start(y_out[:, :, :], h[:, :, :]).then_inc(y_stored, 16)
        sp.wait_ge(states_out, 16 * (1 + DB))
        sp.wait_ge(rows_out, 16)
        sp.wait_ge(win_stored, 16 * DB)
        sp.wait_ge(y_stored, 16)

    @block.scalar
    def _(act):
        A = nc.scalar.activation

        def hi_split(c, half, width=PW):
            slot = c % 2
            act.wait_ge(raw_in[slot], half * 16 + 16 * (c // 2 + 1))
            if not isinstance(half, int) or c + 2 * half >= 2:
                act.wait_ge(tile_made, tiles_before(c - 1, half))
            nc.scalar.copy(w_hi[:, slot, 0:width], w_raw[:, slot, 0:width]).then_inc(hi_made, 1)

        def tile_wait(c, half):
            act.wait_ge(tile_made, half * 2 + (c + TOFF + 1))

        def squares(m, src, ready, after=lambda i: None):
            for i in range(KT):
                ready(i)
                if i >= 2 and m % 2 == 0:
                    act.wait_ge(sq_used, (KT - 1) * (m // 2) + i - 1)
                if i >= 2 and m % 2:
                    act.wait_ge(acc_made, (KT + 1) * (m // 2) + i)
                nc.scalar.square(sq[:, i % 2, :], src[:, i, :]).then_inc(sq_made, 1)
                after(i)

        def rms_root(m):
            act.wait_ge(stat_made, m + 1)
            A(root[:, :], ps[:, STAT, 0:NT], ACT.Sqrt, bias=epsc[:, 0:1], scale=1.0 / D).then_inc(root_made, 1)

        def x_high(k):
            for i in range(KT):
                act.wait_ge(xf_made, 16 * k + i + 1)
                nc.scalar.copy(x_hi[:, i, :], xf[:, i % 2, :]).then_inc(xhi_made, 1)

        def gelu(n, c, dst):
            act.wait_ge(cmp_pre, n + 1)
            if n == 0:
                act.wait_ge(b1_made, 1)
            A(dst.rearrange("p (a s) -> p a s", s=NCMP), sub0[:, 0:dst.shape[1] // NCMP, 0:NCMP],
              ACT.Gelu_apprx_tanh, bias=b1e[:, c:c + 1]).then_inc(cmp_hid, 1)

        def ffn(c, m, next_width, free):
            def pair(q19, i, w):
                half = q19 + i
                tile_wait(c, half)
                act.wait_ge(bank_read[(c + 1) % 2], half + (c + 1 + TOFF) // 2)
                A(sg[:, :], ps[:, c % 2, 0:NT], ACT.Silu).then_inc(bank_read[c % 2], 1)
                hi_split(c + 2, half, w)
                act.wait_ge(bank_read[(c + 1) % 2], half + ((c + 1 + TOFF) // 2 + 1))
                nc.scalar.copy(hid_hi[:, i, :], hb[:, :]).then_inc(hid_hi_made, 1)
                hi_split(c + 3, half, w)

            def out_steps(q19, w_last):
                with act.Fori(0, KT // 2 - 1) as i:
                    for j in range(2):
                        hi_split(c + 2 * HQ + 2 + j, q19 + i, PO)
                if w_last:
                    for j in range(2):
                        hi_split(c + 2 * HQ + KT + j, q19, w_last)

            free()
            with act.Fori(0, NQ - 1) as q:
                with act.Fori(0, HQ - 1) as i:
                    pair(q * (PER_Q // 2), i, PW)
                pair(q * (PER_Q // 2), HQ - 1, PO)
                out_steps(q * (PER_Q // 2), PW)
            q19 = (NQ - 1) * (PER_Q // 2)
            with act.Fori(0, HQ - 1) as i:
                pair(q19, i, PW)
            pair(q19, HQ - 1, PO)
            o = c + 2 * HQ + 2 * q19

            def next_split(i):
                if i < KT - 2:
                    hi_split(o + i + 2, 0, PO)
                elif next_width:
                    hi_split(o + i + 2, 0, next_width)
            squares(m, y, lambda i: act.wait_ge(bank_read[(o + i) % 2], (o + i + TOFF) // 2 + 1), next_split)

        def post_and_pre(a, m):
            rms_root(m)

            def ready(i):
                act.wait_ge(h_made, 16 * a + i + 1)
            squares(m + 1, h, ready)
            rms_root(m + 1)

        act.wait_ge(x_in, 16)
        act.wait_ge(set_made, 1)
        squares(0, h, lambda i: None)
        rms_root(0)
        gelu(0, 0, hcS[:, 0, :])
        hi_split(0, 0)
        hi_split(1, 0)
        gelu(1, 1, hcS[:, 1, :])
        act.wait_ge(cmp_sum, 2)
        for i in range(KT):
            act.wait_ge(mix_made, i // GC + 1)
            nc.scalar.copy(x_hi[:, i, :], mix(i)).then_inc(mixhi_made, 1)
        hi_split(2, 0)
        hi_split(3, 0)
        hi_split(4, 0)
        hi_split(5, 0)
        squares(1, y, lambda i: act.wait_ge(bank_read[i % 2], i // 2 + 1))
        post_and_pre(0, 1)
        x_high(0)
        ffn(P_FFN0, 3, PW, lambda: act.wait_ge(states_out, 16 * (1 + DB)))
        post_and_pre(1, 3)
        x_high(1)

        def tiles_out(c, n, dst, more):
            with act.Fori(0, n // 2 - 1) as i:
                for j in range(2):
                    tile_wait(c + j, i)
                    nc.scalar.copy(dst[:, i * 2 + j, :], ps[:, (c + j) % 2, 0:NT]).then_inc(bank_read[(c + j) % 2], 1)
                    hi_split(c + j + 2, i)
            for j in range(2):
                k = n - 2 + j
                tile_wait(c + k, 0)
                nc.scalar.copy(dst[:, k, :], ps[:, (c + k) % 2, 0:NT]).then_inc(bank_read[(c + k) % 2], 1)
                if more > j:
                    hi_split(c + k + 2, 0)

        tiles_out(P_KV, N_KVT, kvT, 2)
        x_high(2)
        tiles_out(P_Q, NH, qT, 1)
        tile_wait(P_Q + NH, 0)
        A(gT[:, :], ps[:, (P_Q + NH) % 2, 0:NT], ACT.Sigmoid).then_inc(bank_read[(P_Q + NH) % 2], 1)

        gelu(2, 0, hcP[:, 0, :])
        gelu(3, 1, hcP[:, 1, :])

        def exps(u):
            act.wait_ge(max_made, u + 1)
            if u >= 3:
                act.wait_ge(rec_made, u - 2)
            s3 = u % 3
            for n, (lo, w) in enumerate(SPANS_P if u < NH else SPANS_S):
                last = A(sc[:, s3, lo:lo + w], sc[:, s3, lo:lo + w], ACT.Exp, bias=neg[:, s3, n:n + 1],
                         accum_out=tot[:, s3, n:n + 1])
            last.then_inc(exp_made, 1)

        def copy_p(u):
            act.wait_ge(t_made, u + 1)
            if u >= 2:
                act.wait_ge(o_made, u - 1)
            nc.scalar.copy(pT[:, u % 2, 0:512], ps[:, 4, :]).then_inc(pTa_made, 1)

        def out_high(u):
            act.wait_ge(o_made, u + 1)
            nc.scalar.copy(*o_pair(u, x_hi)).then_inc(ohi_made, 1)

        def o_pair(u, dst):
            if u < NH:
                return dst[:, u, 0:SEQ], ps[:, 6, 0:SEQ]
            b = u - NH
            o = SEQ + b * DS
            return dst[:, :, o:o + DS], ps[:, 6, 0:P].rearrange("p (h i) -> p h i", h=NH)

        for s in range(UNITS + 3):
            if s < UNITS:
                exps(s)
            if 2 <= s < UNITS + 2:
                copy_p(s - 2)
            if s >= 3:
                out_high(s - 3)

        act.wait_ge(tile_made, P_WO + TOFF)
        act.wait_ge(s_read, UNITS)
        hi_split(P_WO, 0)
        hi_split(P_WO + 1, 0)
        squares(5, y, lambda i: act.wait_ge(bank_read[(P_WO + i) % 2], (P_WO + i + TOFF) // 2 + 1),
                lambda i: hi_split(P_WO + i + 2, 0))
        post_and_pre(2, 5)
        x_high(3)
        ffn(P_FFN1, 7, None, lambda: act.wait_ge(rows_out, 16))
        rms_root(7)

    @block.vector
    def _(dve):
        V = nc.vector
        chain = [0]

        def link(ins):
            chain[0] += 1
            ins.then_inc(dve_chain, 1)
            dve.wait_ge(dve_chain, chain[0])

        def lo_split(c, half, width=PW):
            slot = c % 2
            dve.wait_ge(hi_made, half * 2 + (c + 1))
            V.tensor_tensor(w_lo[:, slot, 0:width], w_raw[:, slot, 0:width],
                            w_hi[:, slot, 0:width].bitcast(F32), ALU.subtract).then_inc(lo_made, 1)

        def tile_wait(c, half):
            dve.wait_ge(tile_made, half * 2 + (c + TOFF + 1))

        def rms_recip(m):
            dve.wait_ge(root_made, m + 1)
            link(V.reciprocal(r[:, :], root[:, :]))

        def x_norm(k, g):
            for i in range(KT):
                if 16 * k + i >= 2:
                    dve.wait_ge(x_made, 16 * k + i - 1)
                V.scalar_tensor_tensor(out=xf[:, i % 2, :], in0=h[:, i, :], scalar=gn[:, g, i:i + 1], in1=r[:, :],
                                       op0=ALU.mult, op1=ALU.mult).then_inc(xf_made, 1)

        def post_norm(a, m, g):
            rms_recip(m)
            for i in range(KT):
                V.scalar_tensor_tensor(out=y[:, i, :], in0=y[:, i, :], scalar=gn[:, g, i:i + 1], in1=r[:, :],
                                       op0=ALU.mult, op1=ALU.mult).then_inc(yn_made, 1)

        V.memset(tab[NBUCK:NBUCK + 1, :], NEG).then_inc(tab_made, 1)
        dve.wait_ge(const_in, 16 * 8)
        dve.wait_ge(x_in, 16)
        rms_recip(0)
        for i in range(KT):
            V.scalar_tensor_tensor(out=ext[:, i, BUF:EXT_P], in0=h[:, i, 0:SEQ], scalar=gn[:, 0, i:i + 1],
                                   in1=r[:, 0:SEQ], op0=ALU.mult, op1=ALU.mult)
            es = ext[:, i, EXT_P:EXT].rearrange("p (b j) -> p b j", b=DB)[:, :, BUF:EXT_B]
            last = V.scalar_tensor_tensor(out=es, in0=h[:, i, SEQ:NT].rearrange("p (b j) -> p b j", b=DB),
                                          scalar=gn[:, 0, i:i + 1],
                                          in1=r[:, SEQ:NT].rearrange("p (b j) -> p b j", b=DB),
                                          op0=ALU.mult, op1=ALU.mult)
        last.then_inc(ext_made, 1)
        dve.wait_ge(ext_made, 1)
        dve.wait_ge(ext_in, 16 * DB)
        dve.wait_ge(set_made, 1)

        def window_sums(g):
            e = ext[:, g * GC:(g + 1) * GC, :]
            src, at_, bufs = e, 0, (winA, winB)
            if g:
                dve.wait_ge(mix_ready, GC * g)
            for n in range(g + 1):
                w = 2 ** n
                dst = bufs[n % 2]
                o = at_ + w
                link(V.tensor_tensor(dst[:, :, o:EXT], src[:, :, o:EXT], src[:, :, o - w:EXT - w], ALU.add))
                src, at_ = dst, o
            out = bufs[(g + 1) % 2]
            V.tensor_tensor(out[:, :, 0:SEQ], src[:, :, BUF:EXT_P], rep(inv[:, g, 0:SEQ], GC), ALU.mult)
            for k in range(GC):
                last = V.tensor_tensor(out[:, k, SEQ:NT].rearrange("p (b j) -> p b j", b=DB),
                                       src[:, k, EXT_P:EXT].rearrange("p (b j) -> p b j", b=DB)[:, :, BUF:EXT_B],
                                       inv[:, g, SEQ:NT].rearrange("p (b j) -> p b j", b=DB), ALU.mult)
            link(last)
            V.tensor_tensor(out[:, :, 0:SEQ], out[:, :, 0:SEQ], e[:, :, BUF:EXT_P], ALU.subtract)
            for k in range(GC):
                last = V.tensor_tensor(out[:, k, SEQ:NT].rearrange("p (b j) -> p b j", b=DB),
                                       out[:, k, SEQ:NT].rearrange("p (b j) -> p b j", b=DB),
                                       ext[:, g * GC + k, EXT_P:EXT].rearrange("p (b j) -> p b j", b=DB)[:, :, BUF:EXT_B],
                                       ALU.subtract)
            last.then_inc(mix_made, 1)

        def cmp_join(n, bank, nseq, pages_apart):
            dve.wait_ge(cmp_sum, n + 1)
            if n:
                dve.wait_ge(cmp_hid, n)
            if pages_apart:
                for dst, b_ in ((sub0, bank), (sub1, bank + 1)):
                    for p in range(NPG):
                        d_ = dst[:, :, :].rearrange("p (b h) s -> p b h s", h=NKV)[:, :, :, p * 8:p * 8 + 8]
                        s_ = ps[:, b_, :].rearrange("p (b g h s) -> p b g h s", b=DB, g=NPG, h=NKV)[:, :, p, :, :]
                        last = V.tensor_copy(d_, s_)
            else:
                V.tensor_copy(sub0[:, 0:nseq, :], ps[:, bank, 0:NKV * NSUB].rearrange("p (h s) -> p h s", h=NKV))
                last = V.tensor_copy(sub1p[:, 0:nseq, :], ps[:, bank, 64:64 + NKV * NSUB].rearrange("p (h s) -> p h s", h=NKV))
            link(last)
            s1 = sub1 if pages_apart else sub1p
            V.tensor_tensor(sub0[:, 0:nseq, 0:NCMP], sub0[:, 0:nseq, 0:NCMP], s1[:, 0:nseq, 1:NSUB],
                            ALU.add).then_inc(cmp_pre, 1)

        dve.wait_ge(b1_sum, 1)
        V.tensor_tensor(b1e[:, :], b1[:, :], ps[:, 6, 0:2], ALU.add).then_inc(b1_made, 1)
        window_sums(0)
        cmp_join(0, 2, DB * NKV, True)
        lo_split(0, 0)
        lo_split(1, 0)
        cmp_join(1, 4, DB * NKV, True)
        for g in range(1, NG):
            window_sums(g)
        dve.wait_ge(kc_sum, 1)
        V.tensor_copy(kcS[:, :], ps[:, 6, 0:DB * NKV * NCMP]).then_inc(kc_made, 1)

        dve.wait_ge(cmp_sum, 2)
        def pool_tiles(g):
            for n in range(g * GC, (g + 1) * GC):
                dve.wait_ge(tile_made, n + 1)
                V.tensor_scalar(y[:, n, :], ps[:, n % 2, 0:NT], gn[:, G_POOL, n:n + 1], None,
                                ALU.mult).then_inc(bank_read[n % 2], 1)
        for g in range(NG):
            pool_tiles(g)
            lo_split(g + 2, 0)
        post_norm(0, 1, 1)
        rms_recip(2)
        x_norm(0, 2)

        def ffn(c, next_width):
            def pair(q19, i, w):
                half = q19 + i
                lo_split(c + 2, half, w)
                tile_wait(c + 1, half)
                dve.wait_ge(bank_read[c % 2], half + ((c + TOFF) // 2 + 1))
                dve.wait_ge(hid_made, pairs_before(c, q19, i))
                V.tensor_tensor(hb[:, :], sg[:, :], ps[:, (c + 1) % 2, 0:NT], ALU.mult).then_inc(bank_read[(c + 1) % 2], 1)
                lo_split(c + 3, half, w)

            def pairs_before(c_, q19, i):
                base = 1 if c_ == P_FFN0 else 1 + HT
                if isinstance(q19, int):
                    return i + (base + (q19 // (PER_Q // 2)) * HQ)
                return i + q_reg[0] * HQ + base

            def outs(q19, w_last):
                o = c + 2 * HQ

                def one(j, i, n):
                    tile_wait(o + j, q19 + i)
                    V.tensor_tensor(y[:, n, :], y[:, n, :], ps[:, (o + j) % 2, 0:NT], ALU.add).then_inc(bank_read[(o + j) % 2], 1)
                with dve.Fori(0, KT // 2 - 1) as i:
                    for j in range(2):
                        one(j, i, i * 2 + j)
                        lo_split(o + 2 + j, q19 + i, PO)
                for j in range(2):
                    one(j, KT // 2 - 1, KT - 2 + j)
                    if w_last:
                        lo_split(o + 2 + j, q19 + (KT // 2 - 1), w_last)

            q_reg = [0]
            dve.wait_ge(y_zero, 1 if c == P_FFN0 else 2)
            with dve.Fori(0, NQ - 1) as q:
                q_reg[0] = q
                with dve.Fori(0, HQ - 1) as i:
                    pair(q * (PER_Q // 2), i, PW)
                pair(q * (PER_Q // 2), HQ - 1, PO)
                outs(q * (PER_Q // 2), PW)
            q19 = (NQ - 1) * (PER_Q // 2)
            with dve.Fori(0, HQ - 1) as i:
                pair(q19, i, PW)
            pair(q19, HQ - 1, PO)
            outs(q19, next_width)

        ffn(P_FFN0, PW)
        post_norm(1, 3, 3)
        rms_recip(4)
        x_norm(1, G_KV)
        with dve.Fori(0, N_KVT // 2) as i:
            for j in range(2):
                lo_split(P_KV + 2 + j, i)
        dve.wait_ge(tile_made, P_Q + TOFF)
        x_norm(2, 4)
        with dve.Fori(0, NH // 2 - 1) as i:
            for j in range(2):
                lo_split(P_Q + 2 + j, i)
        lo_split(P_Q + NH, 0)

        for n in (2, 3):
            cmp_join(n, n, NKV, False)
        for br in range(2):
            for t in range(2):
                n = br * 2 + t
                dve.wait_ge(vt_sum, n + 1)
                V.tensor_copy(vP[:, br, t, :], ps[:, 4 + n % 2, :]).then_inc(vt_made, 1)
        for br in range(2):
            dve.wait_ge(vt_sum, 5 + br)
            V.tensor_copy(vN[:, br, :], ps[0:NS, 4 + br, :]).then_inc(vt_made, 1)

        dve.wait_ge(g_sum, 1)
        V.tensor_copy(gP[:, :, :], ps[:, 6, 0:2 * 3 * NH].rearrange("p (t n) -> p t n", t=2))
        link(V.tensor_tensor(gtmp[:, :, :], ps[:, 7, 0:3 * NS].rearrange("p (r n) -> p r n", r=3),
                             rep(cst[:, C_IM:C_IM + NS], 3), ALU.mult))
        V.tensor_scalar(gP[:, 0, 0:NH], gP[:, 0, 0:NH], rv[:, 0:1], None, ALU.mult)
        V.tensor_reduce(gS[:, :, :], gtmp[:, :, :].rearrange("p r (b i) -> p r b i", b=DB), AX.X,
                        ALU.add).then_inc(gates_made, 1)
        dve.wait_ge(gates_made, 1)

        for n in range(8):
            dve.wait_ge(bias_sum, n + 1)
            V.tensor_copy(biasP[:, :, n * 32:(n + 1) * 32],
                          ps[:, n % 2, :].rearrange("p (k h) -> p h k", h=NH)).then_inc(bias_made, 1)
        dve.wait_ge(bias_sum, 9)
        for t in range(2):
            V.tensor_copy(biasC[:, t, :, :], ps[:, 2, t * NCMP * NH:(t + 1) * NCMP * NH].rearrange("p (m h) -> p h m", h=NH))
        V.tensor_copy(bias_s[:, :], ps[:, 3, 0:PAST])
        V.tensor_copy(biasSC[:, :], ps[:, 3, PAST + DS:PAST + DS + NCMP])
        dve.wait_ge(tabL_made, 1)
        V.tensor_copy(bias_n[:, DB - 1, :], ps[:, 3, PAST:PAST + DS]).then_inc(bias_made, 1)
        dve.wait_ge(bias_made, 9)

        dve.wait_ge(kc_sum, 2)
        V.tensor_copy(kcP[:, :], ps[:, 4, 0:NKV * NCMP])
        V.tensor_copy(vCP[:, :], ps[0:NCMP, 5, :]).then_inc(kc_made, 1)

        def scores_p(u):
            s3, a = u % 3, 2 * (u % 2)
            dve.wait_ge(s_made, u + 1)
            if u >= 3:
                dve.wait_ge(t_made, u - 2)
            o = sc[:, s3, :]
            V.scalar_tensor_tensor(out=o[:, 16:272].rearrange("p (r k) -> p r k", r=2),
                                   in0=ps[:, a, 0:256].rearrange("p (r k) -> p r k", r=2), scalar=SCALE,
                                   in1=rep(biasP[:, u, P:SEQ], 2), op0=ALU.mult, op1=ALU.add)
            V.scalar_tensor_tensor(out=pick(o, 0, 272, 2, NCMP), in0=pick(ps[:, a, :], 256, 16, 2, NCMP), scalar=SCALE,
                                   in1=biasC[:, :, u, :], op0=ALU.mult, op1=ALU.add)
            link(V.scalar_tensor_tensor(out=o[:, 288:800].rearrange("p (r k) -> p r k", r=2),
                                        in0=ps[:, a + 1, :].rearrange("p (r k) -> p r k", r=2), scalar=SCALE,
                                        in1=rep(biasP[:, u, :], 2), op0=ALU.mult, op1=ALU.add))
            V.tensor_reduce(pick(neg[:, s3, :], 0, 3, 2, 1)[:, :, 0], pick(o, 0, 272, 2, NCMP), AX.X, ALU.max,
                            negate=True).then_inc(s_read, 1)
            V.tensor_reduce(neg[:, s3, 1:3], o[:, 16:272].rearrange("p (r k) -> p r k", r=2), AX.X, ALU.max, negate=True)
            V.tensor_reduce(neg[:, s3, 4:6], o[:, 288:800].rearrange("p (r k) -> p r k", r=2), AX.X, ALU.max,
                            negate=True).then_inc(max_made, 1)

        def scores_s(u):
            b, s3, a = u - NH, u % 3, 2 * (u % 2)
            W = PAST + NEW
            dve.wait_ge(s_made, u + 1)
            dve.wait_ge(t_made, u - 2)
            o = sc[:, s3, :]
            two = ps[:, a:a + 2, :]
            ob = o[:, 16:16 + 2 * W].rearrange("p (r k) -> p r k", r=2)
            V.scalar_tensor_tensor(out=ob[:, :, 0:PAST], in0=two[:, :, 0:PAST], scalar=SCALE,
                                   in1=rep(bias_s[:, :], 2), op0=ALU.mult, op1=ALU.add)
            bn = bias_n[:, DB - 1 - b:2 * DB - 1 - b, :].rearrange("p a j -> p (a j)")
            V.scalar_tensor_tensor(out=ob[:, :, PAST:W], in0=two[:, :, PAST:W], scalar=SCALE,
                                   in1=rep(bn, 2), op0=ALU.mult, op1=ALU.add)
            link(V.scalar_tensor_tensor(out=o[:, 0:NCMP], in0=ps[:, a, W:W + NCMP], scalar=SCALE,
                                        in1=biasSC[:, :], op0=ALU.mult, op1=ALU.add))
            V.tensor_reduce(neg[:, s3, 0:1], o[:, 0:NCMP], AX.X, ALU.max, negate=True).then_inc(s_read, 1)
            V.tensor_reduce(neg[:, s3, 1:3], ob, AX.X, ALU.max, negate=True).then_inc(max_made, 1)

        def recips(u):
            s3 = u % 3
            dve.wait_ge(exp_made, u + 1)
            if u >= 3:
                dve.wait_ge(p_made, u - 2)
            n = 6 if u < NH else 3
            link(V.reciprocal(rec[:, s3, 0:n], tot[:, s3, 0:n]))
            if u < NH:
                V.tensor_tensor(rec[:, s3, :].rearrange("p (t r) -> p t r", t=2), rec[:, s3, :].rearrange("p (t r) -> p t r", t=2),
                                gP[:, :, :].rearrange("p t (r h) -> p t r h", h=NH)[:, :, :, u], ALU.mult).then_inc(rec_made, 1)
            else:
                V.tensor_tensor(rec[:, s3, 0:3], rec[:, s3, 0:3], gS[:, :, u - NH], ALU.mult).then_inc(rec_made, 1)

        def copy_p(u):
            dve.wait_ge(t_made, u + 1)
            if u >= 2:
                dve.wait_ge(o_made, u - 1)
            if u < NH:
                V.tensor_copy(pT[:, u % 2, 512:768], ps[:, 5, 0:256])
                V.tensor_copy(pT[0:NCMP, u % 2, 768:1024], ps[0:NCMP, 5, 256:512]).then_inc(pTb_made, 1)
            else:
                V.tensor_copy(pT[0:NS, u % 2, 512:768], ps[0:NS, 5, 0:256])
                V.tensor_copy(pT[0:NCMP, u % 2, 768:896], ps[0:NCMP, 5, 256:384]).then_inc(pTb_made, 1)
            if u >= NH:
                dve.wait_ge(vc_sum, u - NH + 1)
                V.tensor_copy(vC[:, u % 2, :], ps[0:NCMP, 7, :]).then_inc(vc_made, 1)

        def out_low(u):
            dve.wait_ge(ohi_made, u + 1)
            if u < NH:
                V.tensor_tensor(x_lo[:, u, 0:SEQ], ps[:, 6, 0:SEQ], x_hi[:, u, 0:SEQ].bitcast(F32),
                                ALU.subtract).then_inc(o_read, 1)
            else:
                o = SEQ + (u - NH) * DS
                V.tensor_tensor(x_lo[:, :, o:o + DS], ps[:, 6, 0:P].rearrange("p (h i) -> p h i", h=NH),
                                x_hi[:, :, o:o + DS].bitcast(F32), ALU.subtract).then_inc(o_read, 1)

        for s in range(UNITS + 3):
            if s < UNITS:
                scores_p(s) if s < NH else scores_s(s)
            if 1 <= s < UNITS + 1:
                recips(s - 1)
            if 2 <= s < UNITS + 2:
                copy_p(s - 2)
            if s >= 3:
                out_low(s - 3)

        lo_split(P_WO, 0)
        lo_split(P_WO + 1, 0)
        for i in range(KT):
            dve.wait_ge(tile_made, P_WO + TOFF + i + 1)
            V.tensor_copy(y[:, i, :], ps[:, (P_WO + i) % 2, 0:NT]).then_inc(bank_read[(P_WO + i) % 2], 1)
            lo_split(P_WO + i + 2, 0)
        post_norm(2, 5, 5)
        rms_recip(6)
        x_norm(3, 6)
        ffn(P_FFN1, None)
        post_norm(3, 7, 7)

    @block.gpsimd
    def _(pool):
        G = nc.gpsimd

        def x_low(k):
            for i in range(KT):
                pool.wait_ge(xhi_made, 16 * k + i + 1)
                G.tensor_tensor(x_lo[:, i, :], xf[:, i % 2, :], x_hi[:, i, :].bitcast(F32),
                                ALU.subtract).then_inc(x_made, 1)

        def add_squares(a, m):
            if a:
                pool.wait_ge(stat_made, m - 1)
            G.memset(acc[:, :], 0.0).then_inc(acc_made, 1)
            for i in range(KT):
                pool.wait_ge(sq_made, 16 * m + i + 1)
                pool.wait_ge(acc_made, 17 * a + i + 1)
                G.tensor_tensor(acc[:, :], acc[:, :], sq[:, i % 2, :], ALU.add).then_inc(acc_made, 1)

        def residual(a):
            for i in range(KT):
                pool.wait_ge(yn_made, 16 * a + i + 1)
                G.tensor_tensor(h[:, i, :], h[:, i, :], y[:, i, :], ALU.add).then_inc(h_made, 1)

        def ffn(a, m):
            base = a_pairs[0]

            def pair(i, before):
                pool.wait_ge(hid_hi_made, i + before + 1)
                G.tensor_tensor(hid_lo[:, i, :], hb[:, :], hid_hi[:, i, :].bitcast(F32),
                                ALU.subtract).then_inc(hid_made, 1)
            with pool.Fori(0, NQ) as q:
                with pool.Fori(0, HQ) as i:
                    pair(i, q * HQ + base)
            a_pairs[0] += HT
            add_squares(a, m)

        a_pairs = [0]
        G.memset(epsc[:, :], EPS).then_inc(hid_made, 1)
        G.memset(ones[:, :], 1.0)
        G.memset(ext[:, :, 0:BUF], 0.0).then_inc(set_made, 1)
        pool.wait_ge(ext_made, 1)
        pool.wait_ge(ext_in, 16 * DB)
        pool.dma_start(pool_p_out[:, :, :], ext[:, :, SEQ:EXT_P]).then_inc(states_out, 16)
        for b in range(DB):
            o = EXT_P + b * EXT_B
            pool.dma_start(pool_s_out[:, :, b, :], ext[:, :, o + DS:o + EXT_B]).then_inc(states_out, 16)
        for b in range(DB):
            pool.dma_start(win_out[b], win_kv[b, DS:PAST].rearrange("t c n -> t (c n)")).then_inc(win_stored, 16)
        for i in range(KT):
            pool.wait_ge(mixhi_made, i + 1)
            G.tensor_tensor(x_lo[:, i, :], mix(i), x_hi[:, i, :].bitcast(F32), ALU.subtract).then_inc(mix_ready, 1)
        add_squares(0, 1)
        residual(0)
        pool.wait_ge(h_made, KT)
        G.memset(y[:, :, :], 0.0).then_inc(y_zero, 1)
        x_low(0)
        ffn(1, 3)
        residual(1)
        x_low(1)
        x_low(2)
        pool.wait_ge(tile_made, P_WO + TOFF)
        G.memset(bias_n[:, :, :], NEG)
        G.memset(tabL[:, :, :], 0.0).then_inc(pool_chain, 1)
        pool.wait_ge(pool_chain, 1)
        pool.wait_ge(const_in, 16 * 8)
        pool.wait_ge(tab_made, 1)
        for i in range(DS):
            last = G.tensor_copy(tabL[:, i, :].rearrange("p (h j) -> p h j", h=NH)[:, :, i], tab[:, :])
        last.then_inc(tabL_made, 1)
        pool.wait_ge(bank_read[(P_WO - 1) % 2], (P_WO - 1 + TOFF) // 2 + 1)
        for b in range(DB):
            last = G.tensor_copy(qS[:, b, :, :], qT[:, :, SEQ + b * DS:SEQ + (b + 1) * DS])
        last.then_inc(qS_made, 1)

        for u in range(UNITS):
            s3 = u % 3
            pool.wait_ge(rec_made, u + 1)
            o, f = sc[:, s3, :], rec[:, s3, :]
            if u < NH:
                v = pick(o, 0, 272, 2, NCMP)
                G.tensor_tensor(v, v, spread(pick(f, 0, 3, 2, 1)[:, :, 0], NCMP), ALU.mult)
                v = o[:, 16:272].rearrange("p (r k) -> p r k", r=2)
                G.tensor_tensor(v, v, spread(f[:, 1:3], P), ALU.mult)
                v = o[:, 288:800].rearrange("p (r k) -> p r k", r=2)
                G.tensor_tensor(v, v, spread(f[:, 4:6], SEQ), ALU.mult).then_inc(p_made, 1)
            else:
                W = PAST + NEW
                v = o[:, 0:NCMP]
                G.tensor_tensor(v, v, f[:, 0:1].broadcast_to([P, NCMP]), ALU.mult)
                v = o[:, 16:16 + 2 * W].rearrange("p (r k) -> p r k", r=2)
                G.tensor_tensor(v, v, spread(f[:, 1:3], W), ALU.mult).then_inc(p_made, 1)
        add_squares(2, 5)
        residual(2)
        pool.wait_ge(h_made, 3 * KT)
        G.memset(y[:, :, :], 0.0).then_inc(y_zero, 1)
        x_low(3)
        ffn(3, 7)
        residual(3)

    @block.tensor
    def _(pe):
        M = nc.tensor.matmul
        T = nc.tensor.transpose

        def tile(c, half, kt, xh, xl, ready=None):
            slot = c % 2
            pe.wait_ge(lo_made, half * 2 + (c + 1))
            if not isinstance(half, int) or c + TOFF + 2 * half >= 2:
                pe.wait_ge(bank_read[slot], half + (c + TOFF) // 2)
            out = ps[:, slot, 0:NT]
            for k in range(kt):
                if ready:
                    ready(k)
                wh, wl = w_hi[:, slot, k * P:(k + 1) * P], w_lo[:, slot, k * P:(k + 1) * P]
                M(out, wh, xh[:, k, :], start=(k == 0), stop=False)
                M(out, wh, xl[:, k, :], start=False, stop=False)
                last = M(out, wl, xh[:, k, :], start=False, stop=(k == kt - 1))
            last.then_inc(tile_made, 1)

        def section(c, n, kt, ready):
            tile(c, 0, kt, x_hi, x_lo, ready)
            tile(c + 1, 0, kt, x_hi, x_lo)
            with pe.Fori(1, n // 2) as i:
                for j in range(2):
                    tile(c + j, i, kt, x_hi, x_lo)
            if n % 2:
                tile(c + n - 1, 0, kt, x_hi, x_lo)

        def squares_sum(m):
            for i in range(KT):
                pe.wait_ge(sq_made, 16 * m + i + 1)
                M(ps[:, STAT, 0:NT], ones[:, :], sq[:, i % 2, :], start=(i == 0),
                  stop=(i == KT - 1)).then_inc(sq_used if i < KT - 1 else stat_made, 1)

        def acc_sum(a, m):
            pe.wait_ge(acc_made, 17 * (a + 1))
            M(ps[:, STAT, 0:NT], ones[:, :], acc[:, :], start=True, stop=True).then_inc(stat_made, 1)

        def x_ready(k):
            return lambda i: pe.wait_ge(x_made, 16 * k + i + 1)

        def ffn(c, k, hid_before):
            def quarter(q19, hid_need):
                def hidden(k):
                    if k == 0:
                        pe.wait_ge(hid_made, hid_need)
                    if k == HQ - 1:
                        pe.wait_ge(hid_made, hid_need + 1)
                with pe.Fori(0, KT // 2) as i:
                    for j in range(2):
                        tile(c + 2 * HQ + j, q19 + i, HQ, hid_hi, hid_lo, None if j else hidden)
            tile(c, 0, KT, x_hi, x_lo, x_ready(k))
            tile(c + 1, 0, KT, x_hi, x_lo)
            with pe.Fori(1, HQ) as i:
                for j in range(2):
                    tile(c + j, i, KT, x_hi, x_lo)
            quarter(0, hid_before + HQ)
            with pe.Fori(1, NQ) as q:
                with pe.Fori(0, HQ) as i:
                    for j in range(2):
                        tile(c + j, q * (PER_Q // 2) + i, KT, x_hi, x_lo)
                quarter(q * (PER_Q // 2), q * HQ + (hid_before + HQ))

        def compress(bank, w1, rows, c):
            for j in range(CB):
                last = M(ps[:, bank + j // CS, :], w1[:, j, :], rows[:, :, j % CS, :],
                         start=(j % CS == 0), stop=(j % CS == CS - 1))
            return last

        def pos_bias(c, w1):
            for j in range(CB):
                last = M(ps[:, 6, c:c + 1], w1[:, j, :], pos[:, c, j:j + 1], start=(j == 0), stop=(j == CB - 1))
            return last

        pe.wait_ge(set_made, 1)
        squares_sum(0)
        pe.wait_ge(const_in, 16 * 8)
        pe.wait_ge(cmpK_in, 16 * (1 + NP_ALL))
        pos_bias(0, w1K)
        compress(2, w1K, rowsK, 0).then_inc(cmp_sum, 1)
        pe.wait_ge(cmpV_in, 16 * (1 + NP_ALL))
        pos_bias(1, w1V).then_inc(b1_sum, 1)
        compress(4, w1V, rowsV, 1).then_inc(cmp_sum, 1)
        pe.wait_ge(cmp_hid, 1)
        pe.wait_ge(b1_made, 1)
        M(ps[:, 6, 0:DB * NKV * NCMP], w2[:, 0, :], hcS[:, 0, :], start=True, stop=True).then_inc(kc_sum, 1)

        for g in range(NG):
            pe.wait_ge(lo_made, g + 1)
            pe.wait_ge(mix_ready, GC * (g + 1))
            for n in range(GC):
                t = g * GC + n
                if t >= 2:
                    pe.wait_ge(bank_read[t % 2], t // 2)
                for k in range(GC):
                    o = (n * GC + k) * P
                    wh, wl = w_hi[:, g % 2, o:o + P], w_lo[:, g % 2, o:o + P]
                    M(ps[:, t % 2, 0:NT], wh, x_hi[:, g * GC + k, :], start=(k == 0), stop=False)
                    M(ps[:, t % 2, 0:NT], wh, x_lo[:, g * GC + k, :], start=False, stop=False)
                    last = M(ps[:, t % 2, 0:NT], wl, x_hi[:, g * GC + k, :], start=False, stop=(k == GC - 1))
                last.then_inc(tile_made, 1)
        acc_sum(0, 1)
        squares_sum(2)
        ffn(P_FFN0, 0, 0)
        acc_sum(1, 3)
        squares_sum(4)
        section(P_KV, N_KVT, KT, x_ready(1))
        section(P_Q, N_QT, KT, x_ready(2))

        pe.wait_ge(w1p_in, 32)
        pe.wait_ge(bank_read[(P_WO - 1) % 2], (P_WO - 1 + TOFF) // 2 + 1)
        for c, w1 in ((0, w1Kp), (1, w1Vp)):
            for j in range(CB):
                rows = kvT[:, c * NKV:(c + 1) * NKV, j % CS:SEQ:CS]
                last = M(ps[:, 2 + c, 64 * (j // CS):64 * (j // CS) + 64], w1[:, j, :], rows,
                         start=(j % CS == 0), stop=(j % CS == CS - 1))
            last.then_inc(cmp_sum, 1)
        for br in range(2):
            for t in range(2):
                n = br * 2 + t
                if n >= 2:
                    pe.wait_ge(vt_made, n - 1)
                for v in range(NKV):
                    src = kvT[:, (br + 1) * 2 * NKV + NKV + v, t * P:(t + 1) * P]
                    last = T(ps[:, 4 + n % 2, v * HD:(v + 1) * HD], src, ident)
                last.then_inc(vt_sum, 1)
        for br in range(2):
            pe.wait_ge(vt_made, 3 + br)
            for v in range(NKV):
                src = kvT[:, (br + 1) * 2 * NKV + NKV + v, SEQ:NT]
                last = T(ps[0:NS, 4 + br, v * HD:(v + 1) * HD], src, ident)
            last.then_inc(vt_sum, 1)
        for t in range(2):
            T(ps[:, 6, t * 3 * NH:(t + 1) * 3 * NH], gT[0:3 * NH, t * P:(t + 1) * P], ident[0:3 * NH, 0:3 * NH])
        for br in range(NBR):
            last = M(ps[:, 7, br * NS:(br + 1) * NS], cst[0:3 * NH, C_HS + br * P:C_HS + (br + 1) * P],
                     gT[0:3 * NH, SEQ:NT], start=True, stop=True)
        last.then_inc(g_sum, 1)

        pe.wait_ge(oh_in, 16)
        pe.wait_ge(tabL_made, 1)
        for n in range(8):
            if n >= 2:
                pe.wait_ge(bias_made, n - 1)
            for k in range(32):
                key = n * 32 + k
                a = (SEQ - 1) + P - key
                last = M(ps[:, n % 2, k * NH:(k + 1) * NH], oh[:, 0, a:a + P], tab[:, :], start=True, stop=True)
            last.then_inc(bias_sum, 1)
        pe.wait_ge(cmp_hid, 4)
        for t in range(2):
            for m in range(NCMP):
                a = (SEQ - 1) + t * P - (CS * m + CB - 1)
                o = (t * NCMP + m) * NH
                M(ps[:, 2, o:o + NH], oh[:, 0, a:a + P], tab[:, :], start=True, stop=True)
        d_max = PAST + DS - 1
        for lo, w, start_, step in ((0, PAST, d_max - PAST, 1), (PAST, DS, d_max, 1),
                                    (PAST + DS, NCMP, d_max - (PAST - CB + 1), CS)):
            for i in range(DS):
                a = start_ - i
                last = M(ps[:, 3, lo:lo + w], tabL[:, i, :], oh[:, 1, a:a + (w - 1) * step + 1:step],
                         start=(i == 0), stop=(i == DS - 1))
        last.then_inc(bias_sum, 1)
        pe.wait_ge(vt_made, 6)
        M(ps[:, 4, 0:NKV * NCMP], w2[:, 0, :], hcP[:, 0, :], start=True, stop=True)
        for v in range(NKV):
            last = M(ps[0:NCMP, 5, v * HD:(v + 1) * HD], hcP[:, 1, v * NCMP:(v + 1) * NCMP], w2[:, 1, :],
                     start=True, stop=True)
        last.then_inc(kc_sum, 1)
        pe.wait_ge(kc_made, 2)
        pe.wait_ge(gates_made, 1)
        pe.wait_ge(bias_made, 9)
        pe.wait_ge(qS_made, 1)

        def kT(br, v):
            return kvT[:, (br + 1) * 2 * NKV + v, :]

        def scores(u):
            a = 2 * (u % 2)
            if u >= 2:
                pe.wait_ge(s_read, u - 1)
            if u < NH:
                v = u // GQ
                q0, q1 = qT[:, u, 0:P], qT[:, u, P:SEQ]
                M(ps[:, a, 0:P], q0, kT(0, v)[:, 0:P], start=True, stop=True)
                M(ps[:, a, P:SEQ], q0, kT(1, v)[:, 0:P], start=True, stop=True)
                M(ps[:, a, 256:256 + NCMP], q0, kcP[:, v * NCMP:(v + 1) * NCMP], start=True, stop=True)
                M(ps[:, a, 272:272 + NCMP], q1, kcP[:, v * NCMP:(v + 1) * NCMP], start=True, stop=True)
                M(ps[:, a + 1, 0:256], q1, kT(0, v)[:, 0:SEQ], start=True, stop=True)
                M(ps[:, a + 1, 256:512], q1, kT(1, v)[:, 0:SEQ], start=True, stop=True).then_inc(s_made, 1)
                return
            b = u - NH
            pe.wait_ge(pastK_in[b % 2], 48 * (b // 2 + 1))
            for v in range(NKV):
                q = qS[:, b, v * GQ:(v + 1) * GQ, :].rearrange("p h i -> p (h i)")
                rows = slice(32 * v, 32 * v + 32)
                for br in range(2):
                    M(ps[rows, a + br, 0:PAST], q, pastK[:, br, v, :], start=True, stop=True)
                    M(ps[rows, a + br, PAST:PAST + NEW], q, kT(br, v)[:, SEQ:NT], start=True, stop=True)
                o = (b * NKV + v) * NCMP
                last = M(ps[rows, a, PAST + NEW:PAST + NEW + NCMP], q, kcS[:, o:o + NCMP], start=True, stop=True)
            last.then_inc(s_made, 1)

        def transposes(u):
            pe.wait_ge(p_made, u + 1)
            if u:
                pe.wait_ge(pTa_made, u)
                pe.wait_ge(pTb_made, u)
            o = sc[:, u % 3, :]
            if u < NH:
                for n, lo in enumerate((16, 288, 144, 544)):
                    T(ps[:, 4, n * P:(n + 1) * P], o[:, lo:lo + P], ident)
                for n, lo in enumerate((416, 672)):
                    T(ps[:, 5, n * P:(n + 1) * P], o[:, lo:lo + P], ident)
                T(ps[0:NCMP, 5, 256:384], o[:, 0:NCMP], ident)
                T(ps[0:NCMP, 5, 384:512], o[:, 272:272 + NCMP], ident).then_inc(t_made, 1)
                return
            W = PAST + NEW
            for br in range(2):
                for t in range(2):
                    n = br * 2 + t
                    lo = 16 + br * W + t * P
                    T(ps[:, 4, n * P:(n + 1) * P], o[:, lo:lo + P], ident)
            for br in range(2):
                lo = 16 + br * W + PAST
                T(ps[0:NS, 5, br * P:(br + 1) * P], o[:, lo:lo + NEW], ident)
            T(ps[0:NCMP, 5, 256:384], o[:, 0:NCMP], ident).then_inc(t_made, 1)
            b = u - NH
            if b:
                pe.wait_ge(vc_made, b)
            for v in range(NKV):
                o_ = (b * NKV + v) * NCMP
                last = M(ps[0:NCMP, 7, v * HD:(v + 1) * HD], hcS[:, 1, o_:o_ + NCMP], w2[:, 1, :], start=True, stop=True)
            last.then_inc(vc_sum, 1)

        def outputs(u):
            pe.wait_ge(pTa_made, u + 1)
            pe.wait_ge(pTb_made, u + 1)
            if u:
                pe.wait_ge(o_read, u)
            p = pT[:, u % 2, :]
            if u < NH:
                v = slice((u // GQ) * HD, (u // GQ + 1) * HD)
                O = ps[:, 6, 0:SEQ]
                M(O, vP[:, 0, 0, v], p[:, 0:256], start=True, stop=False)
                M(O, vP[:, 1, 0, v], p[:, 256:512], start=False, stop=False)
                M(O, vCP[:, v], p[0:NCMP, 768:1024], start=False, stop=False)
                M(O[:, P:SEQ], vP[:, 0, 1, v], p[:, 512:640], start=False, stop=False)
                M(O[:, P:SEQ], vP[:, 1, 1, v], p[:, 640:768], start=False, stop=True).then_inc(o_made, 1)
                return
            b = u - NH
            pe.wait_ge(pastV_in[b % 2], 48 * (b // 2 + 1))
            pe.wait_ge(vc_made, b + 1)
            for n in range(NKV):
                v = slice(n * HD, (n + 1) * HD)
                O = ps[:, 6, 32 * n:32 * n + 32]
                for br in range(2):
                    for t in range(2):
                        c0 = (br * 2 + t) * P + 32 * n
                        M(O, pastV[:, br, t, v], p[:, c0:c0 + 32], start=(br == 0 and t == 0), stop=False)
                for br in range(2):
                    c0 = 512 + br * P + 32 * n
                    M(O, vN[:, br, v], p[0:NS, c0:c0 + 32], start=False, stop=False)
                last = M(O, vC[:, u % 2, v], p[0:NCMP, 768 + 32 * n:800 + 32 * n], start=False, stop=True)
            last.then_inc(o_made, 1)

        for s in range(UNITS + 3):
            if s < UNITS:
                scores(s)
            if 2 <= s < UNITS + 2:
                transposes(s - 2)
            if s >= 3:
                outputs(s - 3)

        pe.wait_ge(o_read, UNITS)
        section(P_WO, KT, KT, None)
        acc_sum(2, 5)
        squares_sum(6)
        ffn(P_FFN1, 3, HT)
        acc_sum(3, 7)

    block_ctx.close()


_IN_NAMES = ("x", "st", "gains", "consts", "onehot", "rel", "w_pool", "w_in0", "w_in1", "w_out0", "w_out1", "w_kv", "w_q",
             "w_o", "cmp_data", "cmp_w1", "cmp_pos", "cmp_b1", "cmp_w2", "slc_k", "slc_kv", "win_k", "win_kv", "pages")
_OUTS = (("y_out", (P, KT, NT)), ("pool_p_out", (P, KT, BUF)), ("pool_s_out", (P, KT, DB, BUF)),
         ("kv_out", (P, N_KVT, NT)), ("win_out", (DB, PAST - DS, 2 * NKV * HD)))


def bucket(dist):
    n = np.maximum(dist, 0)
    exact = NBUCK // 2
    big = exact + (np.log(np.maximum(n, 1).astype(np.float32) / exact) / np.log(np.float32(128 / exact)) * (NBUCK - exact)).astype(np.int32)
    return np.where(n < exact, n, np.minimum(big, NBUCK - 1))


def shape_constants():
    c = np.zeros((P, C_N), np.float32)
    c[:, C_ID:C_ID + P] = np.eye(P)
    row, col = np.arange(P)[:, None], np.arange(NS)[None, :]
    c[:, C_IM:C_IM + NS] = row % DS == col % DS
    for br in range(NBR):
        c[:3 * NH, C_HS + br * P:C_HS + (br + 1) * P] = np.arange(3 * NH)[:, None] == br * NH + np.arange(P)[None, :] // DS
    for g in range(NG):
        w = 2 ** (g + 1)
        c[:, C_INV + g * NT:C_INV + g * NT + SEQ] = np.float32(1) / np.minimum(w, np.arange(SEQ) + 1).astype(np.float32)
        c[:, C_INV + g * NT + SEQ:C_INV + (g + 1) * NT] = np.float32(1) / w
    c[:, C_RV] = np.arange(P) >= CB - 1
    hot = np.zeros((NBUCK + 1, 2, NE), np.float32)
    d = np.arange(NE) - (SEQ - 1)
    hot[np.where(d < 0, NBUCK, bucket(d)), 0, np.arange(NE)] = 1
    hot[:, 1] = hot[:, 0, ::-1]
    return c, hot


def kernel(**inputs):
    import concourse.bacc as bacc
    from concourse.bass_utils import run_bass_kernel_spmd

    a = {k: np.asarray(v) for k, v in inputs.items()}

    def chunks(m):
        t = m.reshape(-1, KT, P).transpose(2, 1, 0)
        return t.reshape(P, KT, *m.shape[:-1])

    def panels(w, kt):
        k, n = w.shape
        return w.reshape(kt, P, n // P, P).transpose(2, 1, 0, 3).reshape(n // P, P, kt * P)

    def ffn_in(w):
        gate, up = panels(w[:, :DFF], KT), panels(w[:, DFF:], KT)
        return np.stack([gate, up], 1).reshape(2 * HT, P, PW)

    def ffn_out(w):
        return np.concatenate([panels(w[q * HQ * P:(q + 1) * HQ * P], HQ) for q in range(NQ)])

    consts, hot = shape_constants()
    x_all = np.concatenate([a["x_prompt"].reshape(SEQ, D), a["x_sample"].reshape(NS, D)])
    norms = a["norms"].reshape(8, D)
    gains = np.concatenate([norms, a["pool_scale"].reshape(1, D), a["kv_norm"].reshape(1, D)])
    w_q = a["w_q"][0]
    w_q = np.concatenate([w_q, np.zeros((D, N_QT * P - w_q.shape[1]), w_q.dtype)], 1)
    cmp_rows = a["cache_cmp_kv"]
    n_pages = cmp_rows.shape[0]
    arrays = {
        "x": chunks(x_all),
        "st": chunks(a["state_pool"][0].reshape(DB * BUF, D)).reshape(P, KT, DB, BUF),
        "gains": gains.reshape(10, KT, P).transpose(2, 0, 1),
        "consts": consts, "onehot": hot, "rel": a["rel_bias"],
        "w_pool": a["w_pool"][0].reshape(NG, GC, P, GC, P).transpose(0, 2, 3, 1, 4).reshape(NG, P, PW),
        "w_in0": ffn_in(a["w_ffn_in"][0]), "w_in1": ffn_in(a["w_ffn_in"][1]),
        "w_out0": ffn_out(a["w_ffn_out"][0]), "w_out1": ffn_out(a["w_ffn_out"][1]),
        "w_kv": panels(a["w_kv"], KT), "w_q": panels(w_q, KT), "w_o": panels(a["w_o"][0], KT),
        "cmp_data": cmp_rows.reshape(n_pages, PAGE // CS, CS, 2, NKV, HD).transpose(3, 0, 5, 2, 4, 1).reshape(
            2, n_pages, P, CS, NKV * PAGE // CS),
        "cmp_w1": a["cmp_w1"].transpose(0, 2, 1, 3), "cmp_pos": a["cmp_pos"].transpose(2, 0, 1),
        "cmp_b1": a["cmp_b1"].T, "cmp_w2": a["cmp_w2"].transpose(1, 0, 2),
        "slc_k": a["cache_slc_kv"][:, :, 0].transpose(0, 3, 2, 1),
        "slc_kv": a["cache_slc_kv"].reshape(n_pages, PAGE, 2, NKV * HD),
        "win_k": a["state_win_kv"][:, :, 0].transpose(0, 3, 2, 1),
        "win_kv": a["state_win_kv"].reshape(DB, PAST, 2, NKV * HD),
        "pages": a["page_table"].reshape(1, DB * NPG),
    }
    nc = bacc.Bacc("TRN2", target_bir_lowering=False, num_devices=1)
    args, sent = [], {}
    for name in _IN_NAMES:
        v = np.ascontiguousarray(arrays[name])
        sent[name + "_dram"] = v
        args.append(nc.dram_tensor(name + "_dram", v.shape, mybir.dt.from_np(v.dtype), kind="ExternalInput").ap())
    for name, shape in _OUTS:
        args.append(nc.dram_tensor(name + "_dram", shape, F32, kind="ExternalOutput").ap())
    build(nc, *args)
    got = run_bass_kernel_spmd(nc, [sent], core_ids=[0]).results[0]
    yt, pool_p, pool_s, kv, win = (got[name + "_dram"] for name, _ in _OUTS)

    y_all = yt.transpose(2, 1, 0).reshape(NT, D)
    kv = kv.transpose(2, 1, 0).reshape(NT, NBR, 2, NKV, HD)
    kv_p, kv_s = kv[:SEQ].reshape(1, SEQ, NBR, 2, NKV, HD), kv[SEQ:].reshape(DB, DS, NBR, 2, NKV, HD)
    win_s = np.concatenate([win.reshape(DB, PAST - DS, 2, NKV, HD), kv_s[:, :, 2]], 1)
    return (y_all[:SEQ].reshape(1, SEQ, D), y_all[SEQ:].reshape(DB, DS, D),
            pool_p.transpose(2, 1, 0).reshape(1, 1, BUF, D), pool_s.transpose(2, 3, 1, 0).reshape(1, DB, BUF, D),
            kv_p[:, :, 0], kv_s[:, :, 0], kv_p[:, :, 1], kv_s[:, :, 1], kv_p[:, :, 2], win_s)
```

```python
from contextlib import ExitStack

import numpy as np

import concourse.bass as bass
from concourse import mybir

F32 = mybir.dt.float32
F32R = mybir.dt.float32r
I32 = mybir.dt.int32
ALU = mybir.AluOpType
ACT = mybir.ActivationFunctionType
AX = mybir.AxisListType

P = 128
D = 2048
KT = D // P
SEQ, DB, DS = 256, 8, 8
NS = DB * DS
NT = SEQ + NS
PAST = 256
PAGE = 128
NPG = PAST // PAGE
DFF = 5632
HT = DFF // P
NQ = 4
HQ = HT // NQ
BUF = 15
EXT_P = BUF + SEQ
EXT_B = BUF + DS
EXT = EXT_P + DB * EXT_B
NG = 4
GC = KT // NG
NH, NKV, HD = 16, 4, 128
GQ = NH // NKV
NBR = 3
NBUCK = 32
CB, CS = 32, 16
NCMP = (PAST - CB) // CS + 1
NSUB = PAST // CS
EPS = 1e-6
SCALE = HD ** -0.5
NEG = -1e30
NEW = NS

PW = KT * P
PO = HQ * P
P_POOL, P_FFN0 = 0, NG
PER_Q = 2 * HQ + KT
P_KV = P_FFN0 + NQ * PER_Q
N_KVT = NBR * 2 * NKV
P_Q = P_KV + N_KVT
N_QT = NH + 1
P_WO = P_Q + N_QT
P_FFN1 = P_WO + KT
TOFF = KT - NG

C_ID, C_IM, C_HS, C_INV, C_RV = 0, 128, 192, 192 + 3 * 128, 192 + 3 * 128 + NG * NT
C_N = C_RV + 1
G_POOL, G_KV = 8, 9
NE = SEQ + PAST + DS - 1


def plan_sbuf(nc):
    lo = (nc.sbuf_base + 31) // 32 * 32
    region = {}
    for name, size in (("H", KT * NT * 4), ("Y", KT * NT * 4), ("HID", 32768), ("X", 2 * KT * NT * 4),
                       ("RAW", 2 * PW * 4), ("LO", 2 * PW * 4), ("HI", 2 * PW * 4), ("Z", 19712), ("S", 0)):
        region[name] = lo
        lo += size
    used = {}

    def at(name, where, shape, dt=F32, off=None):
        n = int(np.prod(shape[1:])) * 4
        start = used.get(where, 0) if off is None else off
        used[where] = start + (n + 31) // 32 * 32
        return nc.alloc_sbuf_tensor_at(name, list(shape), dt, offset=region[where] + start)

    return at


SW_S = PAST + NEW
SPANS_P = ((0, NCMP), (16, P), (144, P), (272, NCMP), (288, SEQ), (544, SEQ))
SPANS_S = ((0, NCMP), (16, SW_S), (16 + SW_S, SW_S))


def rep(ap, n):
    return ap.unsqueeze(1).broadcast_to([ap.shape[0], n, ap.shape[1]])


def spread(ap, n):
    return ap.unsqueeze(2).broadcast_to([ap.shape[0], ap.shape[1], n])


def pick(ap, off, step, n, w):
    return ap[:, off:off + n * step].rearrange("p (n s) -> p n s", n=n)[:, :, 0:w]


def build(nc, x, st, gains, consts, onehot, rel, w_pool, w_in0, w_in1, w_out0, w_out1, w_kv, w_q, w_o, flips,
          cmp_data, cmp_w1, cmp_pos, cmp_b1, cmp_w2, slc_k, slc_kv, win_k, win_kv, pages,
          y_out, pool_p_out, pool_s_out, kv_out, win_out):
    at = plan_sbuf(nc)
    h = at("h", "H", [P, KT, NT])
    y = at("y", "Y", [P, KT, NT])
    qT = at("qT", "Y", [P, KT, NT], off=0)
    hid_hi = at("hid_hi", "HID", [P, HQ, NT], F32R)
    hid_lo = at("hid_lo", "HID", [P, HQ, NT], F32R)
    ext = at("ext", "HID", [P, KT, EXT], off=0)
    kvT = at("kvT", "HID", [P, N_KVT, NT], off=0)
    stP = at("stP", "HID", [P, KT, BUF], off=KT * EXT * 4)
    bias_s = at("bias_s", "HID", [P, PAST + DS], off=N_KVT * NT * 4)
    bias_n = at("bias_n", "HID", [P, 2 * DB - 1, DS])
    x_hi = at("x_hi", "X", [P, KT, NT], F32R)
    x_lo = at("x_lo", "X", [P, KT, NT], F32R)
    w_raw = at("w_raw", "RAW", [P, 2, PW])
    w_lo = at("w_lo", "LO", [P, 2, PW], F32R)
    w_hi = at("w_hi", "HI", [P, 2, PW], F32R)
    NP_ALL = DB * NPG
    rowsK = at("rowsK", "RAW", [P, NP_ALL, CS, 32], off=0)
    w1K = at("w1K", "HI", [P, CB, P], off=0)
    rowsV = at("rowsV", "X", [P, NP_ALL, CS, 32], off=0)
    stS = at("stS", "X", [P, KT, DB, BUF])
    w1V = at("w1V", "Y", [P, CB, P], off=0)
    sub1 = at("sub1", "Y", [P, DB * NKV, NSUB])
    inv = at("inv", "Z", [P, NG, NT], off=0)
    winA = at("winA", "Z", [P, GC, EXT])
    winB = at("winB", "Z", [P, GC, EXT])
    w1Kp = at("w1Kp", "RAW", [P, CB, P], off=0)
    w1Vp = at("w1Vp", "LO", [P, CB, P], off=0)
    revP = at("revP", "X", [P, NH, SEQ], off=0)
    revS = at("revS", "X", [P, PAST + DS])
    vP = at("vP", "RAW", [P, 2, 2, NKV * HD], off=0)
    vN = at("vN", "RAW", [NS, 2, NKV * HD])
    vC = at("vC", "RAW", [NCMP, 2, NKV * HD])
    pastK = at("pastK", "LO", [P, 2, NKV, PAST], off=0)
    pastV = at("pastV", "LO", [P, 2, 2, NKV * HD])
    biasP = at("biasP", "HI", [P, NH, SEQ], off=0)
    SW = 816
    sc = at("sc", "Z", [P, 3, SW], off=0)
    pT = at("pT", "Z", [P, 2, 1024])
    cst = at("cst", "S", [P, C_INV])
    rv = at("rv", "S", [P, 1])
    ones = at("ones", "S", [P, P])
    gn = at("gn", "S", [P, 10, KT])
    acc = at("acc", "S", [P, NT])
    r = at("r", "S", [P, NT])
    root = acc
    sq = at("sq", "S", [P, 2, NT])
    sg = at("sg", "Z", [P, NT], off=0)
    hb = at("hb", "Z", [P, NT])
    oh = at("oh", "Z", [NBUCK + 1, NE])
    trow = at("trow", "Z", [NH, NE])
    flip = at("flip", "Z", [P, 2, P])
    epsc = at("epsc", "S", [P, 1])
    epsr = at("epsr", "S", [P, 1])
    pos = at("pos", "S", [P, 2, CB])
    b1 = at("b1", "S", [P, 2])
    b1e = at("b1e", "S", [P, 2])
    brow = at("brow", "HID", [1, 2 * P], off=KT * EXT * 4 + 992)
    w2 = at("w2", "S", [P, 2, P])
    hcS = at("hcS", "S", [P, 2, DB * NKV * NCMP])
    kcS = at("kcS", "S", [P, DB * NKV * NCMP])
    sub0 = at("sub0", "S", [P, DB * NKV, NSUB])
    hcP = at("hcP", "S", [P, 2, NKV * NCMP])
    kcP = at("kcP", "S", [P, NKV * NCMP])
    vCP = at("vCP", "S", [NCMP, NKV * HD])
    tab = at("tab", "S", [NBUCK + 1, NH])
    biasC = at("biasC", "S", [P, 2, NH, NCMP])
    biasSC = at("biasSC", "S", [P, NCMP])
    gT = at("gT", "S", [P, NT])
    gP = at("gP", "S", [P, 2, 3 * NH])
    gtmp = at("gtmp", "Z", [P, 3, NS], off=0)
    oN = at("oN", "S", [P, P])
    qS = at("qS", "S", [P, DB, NH, DS])
    gS = at("gS", "S", [P, 3, DB])
    neg = at("neg", "S", [P, 3, 6])
    tot = at("tot", "S", [P, 3, 6])
    rec = at("rec", "S", [P, 3, 6])
    pgs = at("pgs", "HID", [1, NP_ALL], I32, off=N_KVT * NT * 4 + 1056 + 480)
    ident = cst[:, C_ID:C_ID + P]

    bias_dram = nc.dram_tensor("bias_by_distance", (NH, NE), F32, kind="Internal").ap()

    ps = nc.alloc_psum_tensor("ps", [P, 8, 512], F32)
    STAT = 7

    sem = nc.alloc_semaphore
    x_in, const_in, st_in = sem("x_in"), sem("const_in"), sem("st_in")
    gain_in, pos_in = sem("gain_in"), sem("pos_in")
    pages_in, cmpK_in, cmpV_in = sem("pages_in"), sem("cmpK_in"), sem("cmpV_in")
    raw_in = [sem("raw_in0"), sem("raw_in1")]
    w1p_in, oh_in, rev_in, trow_out = sem("w1p_in"), sem("oh_in"), sem("rev_in"), sem("trow_out")
    pastK_in, pastV_in = [sem("pastK_in0"), sem("pastK_in1")], [sem("pastV_in0"), sem("pastV_in1")]
    states_out, rows_out, win_stored, y_stored = sem("states_out"), sem("rows_out"), sem("win_stored"), sem("y_stored")
    hi_made, lo_made, tile_made = sem("hi_made"), sem("lo_made"), sem("tile_made")
    bank_read = [sem("bank_read0"), sem("bank_read1")]
    hid_hi_made, hid_made, y_zero = sem("hid_hi_made"), sem("hid_made"), sem("y_zero")
    set_made, acc_made = sem("set_made"), sem("acc_made")
    sq_made, sq_used, stat_made, root_made, r_made = (sem(n) for n in ("sq_made", "sq_used", "stat_made",
                                                                       "root_made", "r_made"))
    yn_made, h_made = sem("yn_made"), sem("h_made")
    y_even, y_odd = sem("y_even"), sem("y_odd")
    xhi_made, x_made, x_used = sem("xhi_made"), sem("x_made"), sem("x_used")
    silu_made, sgr_made = sem("silu_made"), sem("sgr_made")
    st_set, ext_made, ext_saved = sem("st_set"), sem("ext_made"), sem("ext_saved")
    mix_made, mixhi_made, mix_ready = sem("mix_made"), sem("mixhi_made"), sem("mix_ready")
    cmp_sum, cmp_pre, cmp_hid, kc_sum, kc_made = (sem(n) for n in ("cmp_sum", "cmp_pre", "cmp_hid", "kc_sum",
                                                                   "kc_made"))
    brow_sum, brow_made, b1_sum, b1_made = sem("brow_sum"), sem("brow_made"), sem("b1_sum"), sem("b1_made")
    tab_made, trow_sum, trow_made, mask_set, bias_sum, bias_made = (
        sem(n) for n in ("tab_made", "trow_sum", "trow_made", "mask_set", "bias_sum", "bias_made"))
    vt_sum, vt_made = sem("vt_sum"), sem("vt_made")
    g_sum, sig_made, gates_made = sem("g_sum"), sem("sig_made"), sem("gates_made")
    s_made, s_read, max_made, exp_made, rec_made, p_made = (sem(n) for n in ("s_made", "s_read", "max_made",
                                                                             "exp_made", "rec_made", "p_made"))
    t_made, pTa_made, pTb_made, o_made, ohi_made, o_read = (sem(n) for n in ("t_made", "pTa_made", "pTb_made",
                                                                             "o_made", "ohi_made", "o_read"))
    oN_sum, oN_made = sem("oN_sum"), sem("oN_made")
    vc_sum, vc_made, qS_made = sem("vc_sum"), sem("vc_made"), sem("qS_made")
    dve_chain, pool_chain = sem("dve_chain"), sem("pool_chain")

    block = nc.Block()
    block_ctx = ExitStack()
    block_ctx.enter_context(block)

    UNITS = NH + DB
    sub1p = sub0[:, 8:8 + NKV, :]

    def by_tokens(t, g):
        t = t[:, g * GC:(g + 1) * GC, :] if t.shape[1] == KT else t
        return t[:, :, 0:SEQ], t[:, :, SEQ:NT].rearrange("p c (b j) -> p c b j", b=DB)

    def by_positions(t, g):
        t = t[:, g * GC:(g + 1) * GC, :] if t.shape[1] == KT else t
        return t[:, :, BUF:EXT_P], t[:, :, EXT_P:EXT].rearrange("p c (b j) -> p c b j", b=DB)[:, :, :, BUF:EXT_B]

    ext_s = ext[:, :, EXT_P:EXT].rearrange("p c (b j) -> p c b j", b=DB)

    def tiles_before(c, half):
        if isinstance(half, int):
            n = c + 2 * half
            return n * GC if n <= NG else n + TOFF
        return half * 2 + (c + TOFF)

    @block.sync
    def _(sp):
        def panel(c, half, src, width):
            slot = c % 2
            if not isinstance(half, int) or c + 2 * half >= 2:
                sp.wait_ge(lo_made, half * 2 + (c - 1))
            sp.dma_start(w_raw[:, slot, 0:width], src).then_inc(raw_in[slot], 16)

        def section(c, n, src, width):
            with sp.Fori(0, n // 2) as i:
                for j in range(2):
                    panel(c + j, i, src[i * 2 + j], width)
            if n % 2:
                panel(c + n - 1, 0, src[n - 1], width)

        def ffn(c, w_in, w_out):
            with sp.Fori(0, NQ) as q:
                with sp.Fori(0, HQ) as i:
                    for j in range(2):
                        panel(c + j, q * (PER_Q // 2) + i, w_in[q * (2 * HQ) + i * 2 + j], PW)
                with sp.Fori(0, KT // 2) as i:
                    for j in range(2):
                        panel(c + 2 * HQ + j, q * (PER_Q // 2) + i, w_out[q * KT + i * 2 + j], PO)

        def page(p):
            return sp.value_load(pgs[0:1, p:p + 1], min_val=0, max_val=cmp_data.shape[1] - 1)

        sp.dma_start(pgs[:, :], pages[:, :]).then_inc(pages_in, 16)
        sp.dma_start(h[:, :, :], x[:, :, :]).then_inc(x_in, 16)
        sp.dma_start(gn[:, :, :], gains[:, :, :]).then_inc(gain_in, 16)
        sp.dma_start(pos[:, :, :], cmp_pos[:, :, :]).then_inc(pos_in, 16)
        sp.dma_start(w1K[:, :, :], cmp_w1[0]).then_inc(cmpK_in, 16)
        sp.wait_ge(pages_in, 16)
        for p in range(NP_ALL):
            sp.dma_start(rowsK[:, p, :, :], cmp_data[0, page(p)]).then_inc(cmpK_in, 16)
            if p == 3:
                sp.dma_start(stS[:, :, :, :], st[:, :, :, :]).then_inc(st_in, 16)
                sp.dma_start(inv[:, :, :], consts[:, C_INV:C_RV].rearrange("p (g t) -> p g t", g=NG)).then_inc(const_in, 16)
        sp.dma_start(cst[:, :], consts[:, 0:C_INV]).then_inc(const_in, 16)
        sp.dma_start(rv[:, :], consts[:, C_RV:C_RV + 1], allow_slow_non_contiguous=True).then_inc(const_in, 16)
        sp.dma_start(b1[:, :], cmp_b1[:, :]).then_inc(const_in, 16)
        sp.dma_start(w2[:, :, :], cmp_w2[:, :, :]).then_inc(const_in, 16)
        sp.dma_start(tab[0:NBUCK, :], rel[:, :]).then_inc(const_in, 16)
        sp.dma_start(w1V[:, :, :], cmp_w1[1]).then_inc(cmpV_in, 16)
        for p in range(NP_ALL):
            sp.dma_start(rowsV[:, p, :, :], cmp_data[1, page(p)]).then_inc(cmpV_in, 16)

        sp.wait_ge(cmp_sum, 1)
        for g in range(NG):
            panel(g, 0, w_pool[g], PW)
        ffn(P_FFN0, w_in0, w_out0)
        section(P_KV, N_KVT, w_kv, PW)
        section(P_Q, N_QT, w_q, PW)
        sp.wait_ge(bank_read[(P_Q - 1) % 2], (P_Q - 1 + TOFF) // 2 + 1)
        sp.wait_ge(bank_read[P_Q % 2], (P_Q - 2 + TOFF) // 2 + 1)
        sp.dma_start(kv_out[:, :, :], kvT[:, :, :]).then_inc(rows_out, 16)

        sp.wait_ge(lo_made, P_WO)
        sp.dma_start(w1Kp[:, :, :], cmp_w1[0]).then_inc(w1p_in, 16)
        sp.wait_ge(tile_made, P_WO + TOFF)
        sp.dma_start(w1Vp[:, :, :], cmp_w1[1]).then_inc(w1p_in, 16)
        sp.wait_ge(trow_out, 16)
        t = bias_dram.tensor
        sp.dma_start(revP[:, :, :], bass.AP(t, DS, [[1, P], [NE, NH], [1, SEQ]])).then_inc(rev_in, 16)
        sp.dma_start(revS[:, :], bass.AP(t, 0, [[NE, NH], [1, DS], [1, PAST + DS]])).then_inc(rev_in, 16)
        sp.wait_ge(cmp_sum, 4)

        def load_keys(b):
            if b:
                sp.wait_ge(s_made, NH + b)
            for p in range(NPG):
                sp.dma_start(pastK[:, 0, :, p * PAGE:(p + 1) * PAGE], slc_k[page(b * NPG + p)]).then_inc(pastK_in[b % 2], 16)
            sp.dma_start(pastK[:, 1, :, :], win_k[b]).then_inc(pastK_in[b % 2], 16)

        def load_values(b):
            if b:
                sp.wait_ge(o_made, NH + b)
            for p in range(NPG):
                sp.dma_start(pastV[:, 0, p, :], slc_kv[page(b * NPG + p), :, 1, :]).then_inc(pastV_in[b % 2], 16)
            sp.dma_start(pastV[:, 1, :, :], win_kv[b, :, 1, :].rearrange("(t p) n -> p t n", p=P)).then_inc(pastV_in[b % 2], 16)

        load_keys(0)
        load_values(0)
        for b in range(1, DB + 3):
            if b < DB:
                load_keys(b)
            if b >= 4:
                load_values(b - 3)

        sp.wait_ge(o_made, UNITS)
        section(P_WO, KT, w_o, PW)
        ffn(P_FFN1, w_in1, w_out1)
        for i in range(0, KT, GC):
            sp.wait_ge(y_even, (i + GC) // 2)
            sp.wait_ge(y_odd, (i + GC) // 2)
            sp.dma_start(y_out[:, i:i + GC, :], h[:, i:i + GC, :]).then_inc(y_stored, 16)
        sp.wait_ge(states_out, 32)
        sp.wait_ge(rows_out, 16)
        sp.wait_ge(win_stored, 16 * DB)
        sp.wait_ge(y_stored, 16 * KT // GC)

    @block.scalar
    def _(act):
        A = nc.scalar.activation

        def hi_split(c, half, width=PW):
            slot = c % 2
            act.wait_ge(raw_in[slot], half * 16 + 16 * (c // 2 + 1))
            if not isinstance(half, int) or c + 2 * half >= 2:
                act.wait_ge(tile_made, tiles_before(c - 1, half))
            nc.scalar.copy(w_hi[:, slot, 0:width], w_raw[:, slot, 0:width]).then_inc(hi_made, 1)

        def tile_wait(c, half):
            act.wait_ge(tile_made, half * 2 + (c + TOFF + 1))

        def squares(m, src, ready, after=lambda i: None):
            for i in range(KT):
                ready(i)
                if i >= 2 and m % 2 == 0:
                    act.wait_ge(sq_used, (KT - 1) * (m // 2) + i - 1)
                if i >= 2 and m % 2:
                    act.wait_ge(acc_made, (KT + 1) * (m // 2) + i)
                nc.scalar.square(sq[:, i % 2, :], src[:, i, :]).then_inc(sq_made, 1)
                after(i)

        def sqrt_table():
            A(epsr[:, :], epsc[:, :], ACT.Sqrt)

        def rms_root(m):
            act.wait_ge(stat_made, m + 1)
            A(root[:, :], ps[:, STAT, 0:NT], ACT.Sqrt, bias=epsc[:, 0:1], scale=1.0 / D).then_inc(root_made, 1)

        def x_high(k, g, i):
            A(x_hi[:, i, :], h[:, i, :], ACT.Copy, scale=gn[:, g, i:i + 1]).then_inc(xhi_made, 1)

        def gelu(n, c, dst):
            act.wait_ge(cmp_pre, n + 1)
            act.wait_ge(b1_made, 1)
            A(dst.rearrange("p (a s) -> p a s", s=NCMP), sub0[:, 0:dst.shape[1] // NCMP, 0:NCMP],
              ACT.Gelu_apprx_tanh, bias=b1e[:, c:c + 1]).then_inc(cmp_hid, 1)

        def ffn(c, m, next_width, free=lambda: None):
            def pair(q19, i, w):
                half = q19 + i
                act.wait_ge(bank_read[c % 2], half + ((c + TOFF) // 2 + 1))
                A(sg[:, :], sg[:, :], ACT.Silu).then_inc(silu_made, 1)
                hi_split(c + 2, half, w)
                act.wait_ge(bank_read[(c + 1) % 2], half + ((c + 1 + TOFF) // 2 + 1))
                nc.scalar.copy(hid_hi[:, i, :], hb[:, :]).then_inc(hid_hi_made, 1)
                hi_split(c + 3, half, w)

            def out_steps(q19, w_last):
                with act.Fori(0, KT // 2 - 1) as i:
                    for j in range(2):
                        hi_split(c + 2 * HQ + 2 + j, q19 + i, PO)
                if w_last:
                    for j in range(2):
                        hi_split(c + 2 * HQ + KT + j, q19, w_last)

            free()
            with act.Fori(0, NQ - 1) as q:
                with act.Fori(0, HQ - 1) as i:
                    pair(q * (PER_Q // 2), i, PW)
                pair(q * (PER_Q // 2), HQ - 1, PO)
                out_steps(q * (PER_Q // 2), PW)
            q19 = (NQ - 1) * (PER_Q // 2)
            with act.Fori(0, HQ - 1) as i:
                pair(q19, i, PW)
            pair(q19, HQ - 1, PO)
            o = c + 2 * HQ + 2 * q19

            def next_split(i):
                if i < KT - 2:
                    hi_split(o + i + 2, 0, PO)
                elif next_width:
                    hi_split(o + i + 2, 0, next_width)
            sqrt_table()
            squares(m, y, lambda i: act.wait_ge(bank_read[(o + i) % 2], (o + i + TOFF) // 2 + 1), next_split)

        def post_and_pre(a, m, k, g):
            rms_root(m)

            def ready(i):
                act.wait_ge(h_made, KT * a + i + 1)
            squares(m + 1, h, ready, lambda i: x_high(k, g, i))
            rms_root(m + 1)

        act.wait_ge(x_in, 16)
        act.wait_ge(set_made, 1)
        sqrt_table()
        squares(0, h, lambda i: None)
        rms_root(0)
        hi_split(0, 0)
        hi_split(1, 0)
        act.wait_ge(cmp_sum, 2)
        for g in range(NG):
            act.wait_ge(mix_made, g + 1)
            for dst, src in zip(by_tokens(x_hi, g), by_positions(ext, g)):
                last = nc.scalar.copy(dst, src)
            last.then_inc(mixhi_made, 1)
            if g < 2:
                gelu(g, g, hcS[:, g, :])

        def pool_ready(i):
            if i % GC == 0:
                hi_split(i // GC + 2, 0)
            act.wait_ge(bank_read[i % 2], i // 2 + 1)
        sqrt_table()
        squares(1, y, pool_ready)
        post_and_pre(0, 1, 0, 2)
        ffn(P_FFN0, 3, PW)
        post_and_pre(1, 3, 1, G_KV)
        with act.Fori(0, N_KVT // 2 - 1) as i:
            for j in range(2):
                hi_split(P_KV + 2 + j, i)
        hi_split(P_Q, 0)
        for i in range(KT):
            if i < KT - 1:
                act.wait_ge(x_used, i + 1)
            else:
                act.wait_ge(tile_made, P_Q + TOFF)
            x_high(2, 4, i)
        hi_split(P_Q + 1, 0)
        with act.Fori(0, NH // 2 - 1) as i:
            for j in range(2):
                hi_split(P_Q + 2 + j, i)
        hi_split(P_Q + NH, 0)
        act.wait_ge(bank_read[(P_Q + NH) % 2], (P_Q + NH + TOFF) // 2 + 1)
        A(gT[:, :], gT[:, :], ACT.Sigmoid).then_inc(sig_made, 1)

        gelu(2, 0, hcP[:, 0, :])
        gelu(3, 1, hcP[:, 1, :])

        def exps(u):
            act.wait_ge(max_made, u + 1)
            if u >= 3:
                act.wait_ge(rec_made, u - 2)
            s3 = u % 3
            for n, (lo, w) in enumerate(SPANS_P if u < NH else SPANS_S):
                last = A(sc[:, s3, lo:lo + w], sc[:, s3, lo:lo + w], ACT.Exp, bias=neg[:, s3, n:n + 1],
                         accum_out=tot[:, s3, n:n + 1])
            last.then_inc(exp_made, 1)

        def copy_p(u):
            act.wait_ge(t_made, u + 1)
            if u >= 2:
                act.wait_ge(o_made, u - 1)
            nc.scalar.copy(pT[:, u % 2, 0:512], ps[:, 4, :]).then_inc(pTa_made, 1)

        def out_high(u):
            if u < NH:
                act.wait_ge(o_made, u + 1)
                nc.scalar.copy(x_hi[:, u, 0:SEQ], ps[:, 6, 0:SEQ]).then_inc(ohi_made, 1)
            else:
                o = SEQ + (u - NH) * DS
                act.wait_ge(oN_sum, u - NH + 1)
                nc.scalar.copy(x_hi[:, :, o:o + DS], ps[:, 6, P:2 * P].rearrange("p (h i) -> p h i", h=NH)).then_inc(ohi_made, 1)

        def out_rows(u):
            act.wait_ge(o_made, u + 1)
            nc.scalar.copy(oN[:, :], ps[:, 6, 0:P]).then_inc(oN_made, 1)

        for s in range(UNITS + 4):
            if s >= 4:
                out_high(s - 4)
            if s < UNITS:
                exps(s)
            if 2 <= s < UNITS + 2:
                copy_p(s - 2)
            if NH + 3 <= s < UNITS + 3:
                out_rows(s - 3)

        act.wait_ge(tile_made, P_WO + TOFF)
        act.wait_ge(s_read, UNITS)
        hi_split(P_WO, 0)
        hi_split(P_WO + 1, 0)
        sqrt_table()
        squares(5, y, lambda i: act.wait_ge(bank_read[(P_WO + i) % 2], (P_WO + i + TOFF) // 2 + 1),
                lambda i: hi_split(P_WO + i + 2, 0))
        post_and_pre(2, 5, 3, 6)
        ffn(P_FFN1, 7, None, lambda: act.wait_ge(rows_out, 16))
        rms_root(7)

    @block.vector
    def _(dve):
        V = nc.vector
        chain = [0]

        def link(ins):
            chain[0] += 1
            ins.then_inc(dve_chain, 1)
            dve.wait_ge(dve_chain, chain[0])

        def lo_split(c, half, width=PW):
            slot = c % 2
            dve.wait_ge(hi_made, half * 2 + (c + 1))
            V.tensor_tensor(w_lo[:, slot, 0:width], w_raw[:, slot, 0:width],
                            w_hi[:, slot, 0:width].bitcast(F32), ALU.subtract).then_inc(lo_made, 1)

        def tile_wait(c, half):
            dve.wait_ge(tile_made, half * 2 + (c + TOFF + 1))

        def rms_recip(m):
            dve.wait_ge(root_made, m + 1)
            V.reciprocal(r[:, :], root[:, :]).then_inc(r_made, 1)
            dve.wait_ge(r_made, m + 1)

        def x_low(k, g, i):
            dve.wait_ge(xhi_made, 16 * k + i + 1)
            V.scalar_tensor_tensor(out=x_lo[:, i, :], in0=h[:, i, :], scalar=gn[:, g, i:i + 1],
                                   in1=x_hi[:, i, :].bitcast(F32), op0=ALU.mult, op1=ALU.subtract).then_inc(x_made, 1)

        def post_norm(a, m, g, lows=lambda i: None):
            rms_recip(m)
            for i in range(KT + 3):
                if i < KT:
                    V.scalar_tensor_tensor(out=y[:, i, :], in0=y[:, i, :], scalar=gn[:, g, i:i + 1], in1=r[:, :],
                                           op0=ALU.mult, op1=ALU.mult).then_inc(yn_made, 1)
                if a == 3 and i % 2 and i < KT:
                    dve.wait_ge(yn_made, 16 * a + i + 1)
                    V.tensor_tensor(h[:, i, :], h[:, i, :], y[:, i, :], ALU.add).then_inc(y_odd, 1)
                if i >= 3:
                    lows(i - 3)

        V.memset(tab[NBUCK:NBUCK + 1, :], NEG).then_inc(tab_made, 1)
        dve.wait_ge(gain_in, 16)
        dve.wait_ge(x_in, 16)
        rms_recip(0)
        for i in range(KT):
            V.scalar_tensor_tensor(out=ext[:, i, BUF:EXT_P], in0=h[:, i, 0:SEQ], scalar=gn[:, 0, i:i + 1],
                                   in1=r[:, 0:SEQ], op0=ALU.mult, op1=ALU.mult)
            es = ext[:, i, EXT_P:EXT].rearrange("p (b j) -> p b j", b=DB)[:, :, BUF:EXT_B]
            last = V.scalar_tensor_tensor(out=es, in0=h[:, i, SEQ:NT].rearrange("p (b j) -> p b j", b=DB),
                                          scalar=gn[:, 0, i:i + 1],
                                          in1=r[:, SEQ:NT].rearrange("p (b j) -> p b j", b=DB),
                                          op0=ALU.mult, op1=ALU.mult)
        last.then_inc(ext_made, 1)
        dve.wait_ge(ext_made, 1)
        dve.wait_ge(const_in, 16 * 6)
        dve.wait_ge(st_set, 1)

        def window_sums(g):
            e = ext[:, g * GC:(g + 1) * GC, :]
            src, at_, bufs = e, 0, (winA, winB)
            if g:
                dve.wait_ge(mix_made, g)
            for n in range(g + 1):
                w = 2 ** n
                dst = bufs[n % 2]
                o = at_ + w
                link(V.tensor_tensor(dst[:, :, o:EXT], src[:, :, o:EXT], src[:, :, o - w:EXT - w], ALU.add))
                src, at_ = dst, o
            mean = bufs[(g + 1) % 2]
            counts = (rep(inv[:, g, 0:SEQ], GC),
                      rep(inv[:, g, SEQ:NT], GC).rearrange("p c (b j) -> p c b j", b=DB))
            for dst, total, c in zip(by_tokens(mean, g), by_positions(src, g), counts):
                last = V.tensor_tensor(dst, total, c, ALU.mult)
            link(last)
            if g == 0:
                dve.wait_ge(ext_saved, 1)
            for m_, x_ in zip(by_tokens(mean, g), by_positions(ext, g)):
                last = V.tensor_tensor(x_, m_, x_, ALU.subtract)
            last.then_inc(mix_made, 1)

        def cmp_join(n, bank, nseq, pages_apart):
            dve.wait_ge(cmp_sum, n + 1)
            if n:
                dve.wait_ge(cmp_hid, n)
            if pages_apart:
                for dst, b_ in ((sub0, bank), (sub1, bank + 1)):
                    for p in range(NPG):
                        d_ = dst[:, :, :].rearrange("p (b h) s -> p b h s", h=NKV)[:, :, :, p * 8:p * 8 + 8]
                        s_ = ps[:, b_, :].rearrange("p (b g h s) -> p b g h s", b=DB, g=NPG, h=NKV)[:, :, p, :, :]
                        last = V.tensor_copy(d_, s_)
            else:
                V.tensor_copy(sub0[:, 0:nseq, :], ps[:, bank, 0:NKV * NSUB].rearrange("p (h s) -> p h s", h=NKV))
                last = V.tensor_copy(sub1p[:, 0:nseq, :], ps[:, bank, 64:64 + NKV * NSUB].rearrange("p (h s) -> p h s", h=NKV))
            link(last)
            s1 = sub1 if pages_apart else sub1p
            V.tensor_tensor(sub0[:, 0:nseq, 0:NCMP], sub0[:, 0:nseq, 0:NCMP], s1[:, 0:nseq, 1:NSUB],
                            ALU.add).then_inc(cmp_pre, 1)

        for g in range(NG):
            window_sums(g)
        dve.wait_ge(brow_sum, 1)
        V.tensor_copy(brow[:, :], ps[0:1, 6, 0:2 * P]).then_inc(brow_made, 1)
        cmp_join(0, 2, DB * NKV, True)
        lo_split(0, 0)
        lo_split(1, 0)
        dve.wait_ge(b1_sum, 1)
        V.tensor_tensor(b1e[:, :], b1[:, :], ps[:, 6, 2 * P:2 * P + 2], ALU.add).then_inc(b1_made, 1)
        cmp_join(1, 4, DB * NKV, True)

        dve.wait_ge(cmp_sum, 2)
        def pool_tiles(g):
            for n in range(g * GC, (g + 1) * GC):
                dve.wait_ge(tile_made, n + 1)
                V.tensor_scalar(y[:, n, :], ps[:, n % 2, 0:NT], gn[:, G_POOL, n:n + 1], None,
                                ALU.mult).then_inc(bank_read[n % 2], 1)
        for g in range(NG):
            pool_tiles(g)
            lo_split(g + 2, 0)
        dve.wait_ge(kc_sum, 1)
        V.tensor_copy(kcS[:, :], ps[:, 6, 0:DB * NKV * NCMP]).then_inc(kc_made, 1)
        post_norm(0, 1, 1, lambda i: x_low(0, 2, i))
        rms_recip(2)

        def ffn(c, next_width):
            def pair(q19, i, w):
                half = q19 + i
                n = pairs_before(c, q19, i)
                tile_wait(c, half)
                V.tensor_tensor(sg[:, :], ps[:, c % 2, 0:NT], r[:, :], ALU.mult).then_inc(bank_read[c % 2], 1)
                lo_split(c + 2, half, w)
                dve.wait_ge(silu_made, n)
                V.tensor_tensor(sg[:, :], sg[:, :], r[:, :], ALU.mult).then_inc(sgr_made, 1)
                tile_wait(c + 1, half)
                dve.wait_ge(sgr_made, n)
                dve.wait_ge(hid_made, n)
                V.tensor_tensor(hb[:, :], sg[:, :], ps[:, (c + 1) % 2, 0:NT], ALU.mult).then_inc(bank_read[(c + 1) % 2], 1)
                lo_split(c + 3, half, w)

            def pairs_before(c_, q19, i):
                base = 1 if c_ == P_FFN0 else 1 + HT
                if isinstance(q19, int):
                    return i + (base + (q19 // (PER_Q // 2)) * HQ)
                return i + q_reg[0] * HQ + base

            def outs(q19, w_last):
                o = c + 2 * HQ

                def one(j, i, n):
                    tile_wait(o + j, q19 + i)
                    V.tensor_tensor(y[:, n, :], y[:, n, :], ps[:, (o + j) % 2, 0:NT], ALU.add).then_inc(bank_read[(o + j) % 2], 1)
                with dve.Fori(0, KT // 2 - 1) as i:
                    for j in range(2):
                        one(j, i, i * 2 + j)
                        lo_split(o + 2 + j, q19 + i, PO)
                for j in range(2):
                    one(j, KT // 2 - 1, KT - 2 + j)
                    if w_last:
                        lo_split(o + 2 + j, q19 + (KT // 2 - 1), w_last)

            q_reg = [0]
            dve.wait_ge(y_zero, 1 if c == P_FFN0 else 2)
            with dve.Fori(0, NQ - 1) as q:
                q_reg[0] = q
                with dve.Fori(0, HQ - 1) as i:
                    pair(q * (PER_Q // 2), i, PW)
                pair(q * (PER_Q // 2), HQ - 1, PO)
                outs(q * (PER_Q // 2), PW)
            q19 = (NQ - 1) * (PER_Q // 2)
            with dve.Fori(0, HQ - 1) as i:
                pair(q19, i, PW)
            pair(q19, HQ - 1, PO)
            outs(q19, next_width)

        ffn(P_FFN0, PW)
        post_norm(1, 3, 3, lambda i: x_low(1, G_KV, i))
        rms_recip(4)

        def scaled(c, half, dst):
            tile_wait(c, half)
            V.tensor_tensor(dst, ps[:, c % 2, 0:NT], r[:, :], ALU.mult).then_inc(bank_read[c % 2], 1)

        with dve.Fori(0, N_KVT // 2 - 1) as i:
            for j in range(2):
                scaled(P_KV + j, i, kvT[:, i * 2 + j, :])
                lo_split(P_KV + 2 + j, i)
        scaled(P_Q - 2, 0, kvT[:, N_KVT - 2, :])
        lo_split(P_Q, 0)
        for i in range(KT):
            x_low(2, 4, i)
        scaled(P_Q - 1, 0, kvT[:, N_KVT - 1, :])
        lo_split(P_Q + 1, 0)
        dve.wait_ge(trow_sum, 1)
        V.tensor_copy(trow[:, 0:512], ps[0:NH, 2, :])
        V.tensor_copy(trow[:, 512:NE], ps[0:NH, 3, 0:NE - 512]).then_inc(trow_made, 1)
        with dve.Fori(0, NH // 2 - 1) as i:
            for j in range(2):
                scaled(P_Q + j, i, qT[:, i * 2 + j, :])
                lo_split(P_Q + 2 + j, i)
        scaled(P_Q + NH - 2, 0, qT[:, NH - 2, :])
        lo_split(P_Q + NH, 0)
        scaled(P_Q + NH - 1, 0, qT[:, NH - 1, :])
        scaled(P_Q + NH, 0, gT[:, :])

        for n in (2, 3):
            cmp_join(n, n, NKV, False)
        for br in range(2):
            for t in range(2):
                n = br * 2 + t
                dve.wait_ge(vt_sum, n + 1)
                V.tensor_copy(vP[:, br, t, :], ps[:, 4 + n % 2, :]).then_inc(vt_made, 1)
        for br in range(2):
            dve.wait_ge(vt_sum, 5 + br)
            V.tensor_copy(vN[:, br, :], ps[0:NS, 4 + br, :]).then_inc(vt_made, 1)

        dve.wait_ge(g_sum, 1)
        V.tensor_copy(gP[:, :, :], ps[:, 6, 0:2 * 3 * NH].rearrange("p (t n) -> p t n", t=2))
        link(V.tensor_tensor(gtmp[:, :, :], ps[:, 7, 0:3 * NS].rearrange("p (r n) -> p r n", r=3),
                             rep(cst[:, C_IM:C_IM + NS], 3), ALU.mult))
        V.tensor_scalar(gP[:, 0, 0:NH], gP[:, 0, 0:NH], rv[:, 0:1], None, ALU.mult)
        V.tensor_reduce(gS[:, :, :], gtmp[:, :, :].rearrange("p r (b i) -> p r b i", b=DB), AX.X,
                        ALU.add).then_inc(gates_made, 1)
        dve.wait_ge(gates_made, 1)

        for n in range(NH // 2):
            dve.wait_ge(bias_sum, n + 1)
            V.tensor_copy(biasP[:, 2 * n:2 * n + 2, :], ps[:, n % 2, :].rearrange("p (h k) -> p h k", h=2)).then_inc(bias_made, 1)
        dve.wait_ge(bias_sum, NH // 2 + 1)
        dve.wait_ge(mask_set, 1)
        V.tensor_copy(bias_s[:, :], ps[:, 2, 0:PAST + DS])
        link(V.tensor_copy(bias_n[:, DB - 1, :], ps[:, 2, PAST:PAST + DS]))
        V.tensor_copy(biasC[:, 1, :, :], biasP[:, :, CB - 1:SEQ:CS])
        n0 = len(range(P + CB - 1, SEQ, CS))
        V.tensor_copy(biasC[:, 0, :, 0:n0], biasP[:, :, P + CB - 1:SEQ:CS])
        V.tensor_copy(biasSC[:, :], bias_s[:, CB - 1:PAST:CS]).then_inc(bias_made, 1)
        dve.wait_ge(bias_made, NH // 2 + 1)

        dve.wait_ge(kc_sum, 2)
        V.tensor_copy(kcP[:, :], ps[:, 4, 0:NKV * NCMP])
        V.tensor_copy(vCP[:, :], ps[0:NCMP, 5, :]).then_inc(kc_made, 1)

        def scores_p(u):
            s3, a = u % 3, 2 * (u % 2)
            dve.wait_ge(s_made, u + 1)
            if u >= 3:
                dve.wait_ge(t_made, u - 2)
            o = sc[:, s3, :]
            V.scalar_tensor_tensor(out=o[:, 16:272].rearrange("p (r k) -> p r k", r=2),
                                   in0=ps[:, a, 0:256].rearrange("p (r k) -> p r k", r=2), scalar=SCALE,
                                   in1=rep(biasP[:, u, P:SEQ], 2), op0=ALU.mult, op1=ALU.add)
            V.scalar_tensor_tensor(out=pick(o, 0, 272, 2, NCMP), in0=pick(ps[:, a, :], 256, 16, 2, NCMP), scalar=SCALE,
                                   in1=biasC[:, :, u, :], op0=ALU.mult, op1=ALU.add)
            link(V.scalar_tensor_tensor(out=o[:, 288:800].rearrange("p (r k) -> p r k", r=2),
                                        in0=ps[:, a + 1, :].rearrange("p (r k) -> p r k", r=2), scalar=SCALE,
                                        in1=rep(biasP[:, u, :], 2), op0=ALU.mult, op1=ALU.add))
            V.tensor_reduce(pick(neg[:, s3, :], 0, 3, 2, 1)[:, :, 0], pick(o, 0, 272, 2, NCMP), AX.X, ALU.max,
                            negate=True).then_inc(s_read, 1)
            V.tensor_reduce(neg[:, s3, 1:3], o[:, 16:272].rearrange("p (r k) -> p r k", r=2), AX.X, ALU.max, negate=True)
            V.tensor_reduce(neg[:, s3, 4:6], o[:, 288:800].rearrange("p (r k) -> p r k", r=2), AX.X, ALU.max,
                            negate=True).then_inc(max_made, 1)

        def scores_s(u):
            b, s3, a = u - NH, u % 3, 2 * (u % 2)
            W = PAST + NEW
            dve.wait_ge(s_made, u + 1)
            dve.wait_ge(t_made, u - 2)
            o = sc[:, s3, :]
            two = ps[:, a:a + 2, :]
            ob = o[:, 16:16 + 2 * W].rearrange("p (r k) -> p r k", r=2)
            V.scalar_tensor_tensor(out=ob[:, :, 0:PAST], in0=two[:, :, 0:PAST], scalar=SCALE,
                                   in1=rep(bias_s[:, 0:PAST], 2), op0=ALU.mult, op1=ALU.add)
            bn = bias_n[:, DB - 1 - b:2 * DB - 1 - b, :].rearrange("p a j -> p (a j)")
            V.scalar_tensor_tensor(out=ob[:, :, PAST:W], in0=two[:, :, PAST:W], scalar=SCALE,
                                   in1=rep(bn, 2), op0=ALU.mult, op1=ALU.add)
            link(V.scalar_tensor_tensor(out=o[:, 0:NCMP], in0=ps[:, a, W:W + NCMP], scalar=SCALE,
                                        in1=biasSC[:, :], op0=ALU.mult, op1=ALU.add))
            V.tensor_reduce(neg[:, s3, 0:1], o[:, 0:NCMP], AX.X, ALU.max, negate=True).then_inc(s_read, 1)
            V.tensor_reduce(neg[:, s3, 1:3], ob, AX.X, ALU.max, negate=True).then_inc(max_made, 1)

        def recips(u):
            s3 = u % 3
            dve.wait_ge(exp_made, u + 1)
            if u >= 3:
                dve.wait_ge(p_made, u - 2)
            n = 6 if u < NH else 3
            link(V.reciprocal(rec[:, s3, 0:n], tot[:, s3, 0:n]))
            if u < NH:
                V.tensor_tensor(rec[:, s3, :].rearrange("p (t r) -> p t r", t=2), rec[:, s3, :].rearrange("p (t r) -> p t r", t=2),
                                gP[:, :, :].rearrange("p t (r h) -> p t r h", h=NH)[:, :, :, u], ALU.mult).then_inc(rec_made, 1)
            else:
                V.tensor_tensor(rec[:, s3, 0:3], rec[:, s3, 0:3], gS[:, :, u - NH], ALU.mult).then_inc(rec_made, 1)

        def copy_p(u):
            dve.wait_ge(t_made, u + 1)
            if u >= 2:
                dve.wait_ge(o_made, u - 1)
            if u < NH:
                V.tensor_copy(pT[:, u % 2, 512:768], ps[:, 5, 0:256])
                V.tensor_copy(pT[0:NCMP, u % 2, 768:1024], ps[0:NCMP, 5, 256:512]).then_inc(pTb_made, 1)
            else:
                V.tensor_copy(pT[0:NS, u % 2, 512:768], ps[0:NS, 5, 0:256])
                V.tensor_copy(pT[0:NCMP, u % 2, 768:896], ps[0:NCMP, 5, 256:384]).then_inc(pTb_made, 1)
            if u >= NH:
                dve.wait_ge(vc_sum, u - NH + 1)
                V.tensor_copy(vC[:, u % 2, :], ps[0:NCMP, 7, :]).then_inc(vc_made, 1)

        def out_low(u):
            dve.wait_ge(ohi_made, u + 1)
            if u < NH:
                V.tensor_tensor(x_lo[:, u, 0:SEQ], ps[:, 6, 0:SEQ], x_hi[:, u, 0:SEQ].bitcast(F32),
                                ALU.subtract).then_inc(o_read, 1)
            else:
                o = SEQ + (u - NH) * DS
                V.tensor_tensor(x_lo[:, :, o:o + DS], ps[:, 6, P:2 * P].rearrange("p (h i) -> p h i", h=NH),
                                x_hi[:, :, o:o + DS].bitcast(F32), ALU.subtract).then_inc(o_read, 1)

        for s in range(UNITS + 4):
            if s >= 4:
                out_low(s - 4)
            if s < UNITS:
                scores_p(s) if s < NH else scores_s(s)
            if 1 <= s < UNITS + 1:
                recips(s - 1)
            if 2 <= s < UNITS + 2:
                copy_p(s - 2)

        lo_split(P_WO, 0)
        lo_split(P_WO + 1, 0)
        for i in range(KT):
            dve.wait_ge(tile_made, P_WO + TOFF + i + 1)
            V.tensor_copy(y[:, i, :], ps[:, (P_WO + i) % 2, 0:NT]).then_inc(bank_read[(P_WO + i) % 2], 1)
            lo_split(P_WO + i + 2, 0)
        post_norm(2, 5, 5, lambda i: x_low(3, 6, i))
        rms_recip(6)
        ffn(P_FFN1, None)
        post_norm(3, 7, 7)

    @block.gpsimd
    def _(pool):
        G = nc.gpsimd

        def add_squares(m):
            pool.wait_ge(r_made, m)
            G.memset(acc[:, :], 0.0).then_inc(acc_made, 1)
            for i in range(KT):
                pool.wait_ge(sq_made, 16 * m + i + 1)
                pool.wait_ge(acc_made, 17 * (m // 2) + i + 1)
                G.tensor_tensor(acc[:, :], acc[:, :], sq[:, i % 2, :], ALU.add).then_inc(acc_made, 1)

        def residual(a):
            for i in range(KT):
                pool.wait_ge(yn_made, 16 * a + i + 1)
                G.tensor_tensor(h[:, i, :], h[:, i, :], y[:, i, :], ALU.add).then_inc(h_made, 1)

        def clear_y(n):
            pool.wait_ge(h_made, KT * n)
            G.memset(y[:, :, :], 0.0).then_inc(y_zero, 1)

        def ffn(m):
            base = a_pairs[0]

            def pair(i, before):
                pool.wait_ge(hid_hi_made, i + before + 1)
                G.tensor_tensor(hid_lo[:, i, :], hb[:, :], hid_hi[:, i, :].bitcast(F32),
                                ALU.subtract).then_inc(hid_made, 1)
            with pool.Fori(0, NQ) as q:
                with pool.Fori(0, HQ) as i:
                    pair(i, q * HQ + base)
            a_pairs[0] += HT
            add_squares(m)

        a_pairs = [0]
        G.memset(epsc[:, :], EPS).then_inc(hid_made, 1)
        G.memset(ones[:, :], 1.0)
        G.memset(ext[:, :, 0:BUF], 0.0).then_inc(set_made, 1)
        pool.wait_ge(st_in, 16)
        G.tensor_copy(ext_s[:, :, :, 0:BUF], stS[:, :, :, :]).then_inc(st_set, 1)
        pool.wait_ge(ext_made, 1)
        pool.wait_ge(st_set, 1)
        G.tensor_copy(stP[:, :, :], ext[:, :, SEQ:EXT_P])
        G.tensor_copy(stS[:, :, :, :], ext_s[:, :, :, DS:EXT_B]).then_inc(ext_saved, 1)
        pool.wait_ge(ext_saved, 1)
        pool.dma_start(pool_p_out[:, :, :], stP[:, :, :]).then_inc(states_out, 16)
        pool.dma_start(pool_s_out[:, :, :, :], stS[:, :, :, :]).then_inc(states_out, 16)
        pool.wait_ge(states_out, 32)
        for g in range(NG):
            pool.wait_ge(mixhi_made, g + 1)
            for dst, high, src in zip(by_tokens(x_lo, g), by_tokens(x_hi, g), by_positions(ext, g)):
                last = G.tensor_tensor(dst, src, high.bitcast(F32), ALU.subtract)
            last.then_inc(mix_ready, 1)
        for b in range(DB):
            pool.dma_start(win_out[b], win_kv[b, DS:PAST].rearrange("t c n -> t (c n)")).then_inc(win_stored, 16)
        add_squares(1)
        residual(0)
        clear_y(1)
        pool.dma_start(oh[:, :], onehot[:, :]).then_inc(oh_in, 16)
        pool.dma_start(flip[:, :, :], flips[:, :, :]).then_inc(oh_in, 16)
        ffn(3)
        residual(1)
        pool.wait_ge(trow_made, 1)
        pool.dma_start(bias_dram[:, :], trow[:, :]).then_inc(trow_out, 16)
        pool.wait_ge(tile_made, P_WO + TOFF)
        G.memset(bias_n[:, :, :], NEG)
        G.memset(biasC[:, :, :, :], NEG).then_inc(mask_set, 1)
        pool.wait_ge(bank_read[(P_WO - 1) % 2], (P_WO - 1 + TOFF) // 2 + 1)
        for b in range(DB):
            last = G.tensor_copy(qS[:, b, :, :], qT[:, :, SEQ + b * DS:SEQ + (b + 1) * DS])
        last.then_inc(qS_made, 1)

        for u in range(UNITS):
            s3 = u % 3
            pool.wait_ge(rec_made, u + 1)
            o, f = sc[:, s3, :], rec[:, s3, :]
            if u < NH:
                v = pick(o, 0, 272, 2, NCMP)
                G.tensor_tensor(v, v, spread(pick(f, 0, 3, 2, 1)[:, :, 0], NCMP), ALU.mult)
                v = o[:, 16:272].rearrange("p (r k) -> p r k", r=2)
                G.tensor_tensor(v, v, spread(f[:, 1:3], P), ALU.mult)
                v = o[:, 288:800].rearrange("p (r k) -> p r k", r=2)
                G.tensor_tensor(v, v, spread(f[:, 4:6], SEQ), ALU.mult).then_inc(p_made, 1)
            else:
                W = PAST + NEW
                v = o[:, 0:NCMP]
                G.tensor_tensor(v, v, f[:, 0:1].broadcast_to([P, NCMP]), ALU.mult)
                v = o[:, 16:16 + 2 * W].rearrange("p (r k) -> p r k", r=2)
                G.tensor_tensor(v, v, spread(f[:, 1:3], W), ALU.mult).then_inc(p_made, 1)
        add_squares(5)
        residual(2)
        clear_y(3)
        ffn(7)
        for i in range(0, KT, 2):
            pool.wait_ge(yn_made, 16 * 3 + i + 1)
            G.tensor_tensor(h[:, i, :], h[:, i, :], y[:, i, :], ALU.add).then_inc(y_even, 1)

    @block.tensor
    def _(pe):
        M = nc.tensor.matmul
        T = nc.tensor.transpose

        def tile(c, half, kt, xh, xl, ready=None, used=None):
            slot = c % 2
            pe.wait_ge(lo_made, half * 2 + (c + 1))
            if not isinstance(half, int) or c + TOFF + 2 * half >= 2:
                pe.wait_ge(bank_read[slot], half + (c + TOFF) // 2)
            out = ps[:, slot, 0:NT]
            for k in range(kt):
                if ready:
                    ready(k)
                wh, wl = w_hi[:, slot, k * P:(k + 1) * P], w_lo[:, slot, k * P:(k + 1) * P]
                M(out, wh, xh[:, k, :], start=(k == 0), stop=False)
                M(out, wh, xl[:, k, :], start=False, stop=False)
                last = M(out, wl, xh[:, k, :], start=False, stop=(k == kt - 1))
                if used and k < kt - 1:
                    last.then_inc(used, 1)
            last.then_inc(tile_made, 1)

        def first_tile(c, ready, m):
            slot = c % 2
            pe.wait_ge(lo_made, c + 1)
            pe.wait_ge(bank_read[slot], (c + TOFF) // 2)
            for k in range(KT):
                square_sum(m, k)
                ready(k)
                wh, wl = w_hi[:, slot, k * P:(k + 1) * P], w_lo[:, slot, k * P:(k + 1) * P]
                M(ps[:, slot, 0:NT], wh, x_hi[:, k, :], start=(k == 0), stop=False)
                M(ps[:, slot, 0:NT], wh, x_lo[:, k, :], start=False, stop=False)
                last = M(ps[:, slot, 0:NT], wl, x_hi[:, k, :], start=False, stop=(k == KT - 1))
            last.then_inc(tile_made, 1)

        def square_sum(m, i):
            pe.wait_ge(sq_made, 16 * m + i + 1)
            M(ps[:, STAT, 0:NT], ones[:, :], sq[:, i % 2, :], start=(i == 0),
              stop=(i == KT - 1)).then_inc(sq_used if i < KT - 1 else stat_made, 1)

        def acc_sum(m):
            pe.wait_ge(acc_made, 17 * (m // 2 + 1))
            M(ps[:, STAT, 0:NT], ones[:, :], acc[:, :], start=True, stop=True).then_inc(stat_made, 1)

        def x_ready(k):
            return lambda i: pe.wait_ge(x_made, 16 * k + i + 1)

        def ffn(c, k, m, hid_before):
            def quarter(q19, hid_need):
                def hidden(k):
                    if k == 0:
                        pe.wait_ge(hid_made, hid_need)
                    if k == HQ - 1:
                        pe.wait_ge(hid_made, hid_need + 1)
                with pe.Fori(0, KT // 2) as i:
                    for j in range(2):
                        tile(c + 2 * HQ + j, q19 + i, HQ, hid_hi, hid_lo, None if j else hidden)
            first_tile(c, x_ready(k), m)
            tile(c + 1, 0, KT, x_hi, x_lo)
            with pe.Fori(1, HQ) as i:
                for j in range(2):
                    tile(c + j, i, KT, x_hi, x_lo)
            quarter(0, hid_before + HQ)
            with pe.Fori(1, NQ) as q:
                with pe.Fori(0, HQ) as i:
                    for j in range(2):
                        tile(c + j, q * (PER_Q // 2) + i, KT, x_hi, x_lo)
                quarter(q * (PER_Q // 2), q * HQ + (hid_before + HQ))

        def compress(bank, w1, rows, c):
            for j in range(CB):
                last = M(ps[:, bank + j // CS, :], w1[:, j, :], rows[:, :, j % CS, :],
                         start=(j % CS == 0), stop=(j % CS == CS - 1))
            return last

        def pos_bias(c, w1):
            for j in range(CB):
                last = M(ps[0:1, 6, c * P:(c + 1) * P], pos[:, c, j:j + 1], w1[:, j, :], start=(j == 0), stop=(j == CB - 1))
            return last

        pe.wait_ge(set_made, 1)
        for i in range(KT):
            square_sum(0, i)
        pe.wait_ge(pos_in, 16)
        pe.wait_ge(cmpK_in, 16 * (1 + NP_ALL))
        pos_bias(0, w1K)
        compress(2, w1K, rowsK, 0).then_inc(cmp_sum, 1)
        pe.wait_ge(cmpV_in, 16 * (1 + NP_ALL))
        pos_bias(1, w1V).then_inc(brow_sum, 1)
        compress(4, w1V, rowsV, 1).then_inc(cmp_sum, 1)
        pe.wait_ge(brow_made, 1)
        for c in range(2):
            last = M(ps[:, 6, 2 * P + c:2 * P + c + 1], brow[0:1, c * P:(c + 1) * P], ones[0:1, 0:1], start=True, stop=True)
        last.then_inc(b1_sum, 1)

        for g in range(NG):
            pe.wait_ge(lo_made, g + 1)
            pe.wait_ge(mix_ready, g + 1)
            for n in range(GC):
                t = g * GC + n
                if t >= 2:
                    pe.wait_ge(bank_read[t % 2], t // 2)
                for k in range(GC):
                    o = (n * GC + k) * P
                    wh, wl = w_hi[:, g % 2, o:o + P], w_lo[:, g % 2, o:o + P]
                    M(ps[:, t % 2, 0:NT], wh, x_hi[:, g * GC + k, :], start=(k == 0), stop=False)
                    M(ps[:, t % 2, 0:NT], wh, x_lo[:, g * GC + k, :], start=False, stop=False)
                    last = M(ps[:, t % 2, 0:NT], wl, x_hi[:, g * GC + k, :], start=False, stop=(k == GC - 1))
                last.then_inc(tile_made, 1)
        pe.wait_ge(const_in, 16 * 6)
        pe.wait_ge(cmp_hid, 1)
        M(ps[:, 6, 0:DB * NKV * NCMP], w2[:, 0, :], hcS[:, 0, :], start=True, stop=True).then_inc(kc_sum, 1)
        acc_sum(1)
        ffn(P_FFN0, 0, 2, 0)
        acc_sum(3)
        first_tile(P_KV, x_ready(1), 4)
        tile(P_KV + 1, 0, KT, x_hi, x_lo)
        with pe.Fori(1, N_KVT // 2 - 1) as i:
            for j in range(2):
                tile(P_KV + j, i, KT, x_hi, x_lo)
        tile(P_Q - 2, 0, KT, x_hi, x_lo)
        tile(P_Q - 1, 0, KT, x_hi, x_lo, used=x_used)
        pe.wait_ge(oh_in, 32)
        pe.wait_ge(tab_made, 1)
        M(ps[0:NH, 2, :], tab[:, :], oh[:, 0:512], start=True, stop=True)
        M(ps[0:NH, 3, 0:NE - 512], tab[:, :], oh[:, 512:NE], start=True, stop=True).then_inc(trow_sum, 1)
        tile(P_Q, 0, KT, x_hi, x_lo, x_ready(2))
        tile(P_Q + 1, 0, KT, x_hi, x_lo)
        with pe.Fori(1, NH // 2) as i:
            for j in range(2):
                tile(P_Q + j, i, KT, x_hi, x_lo)
        tile(P_Q + NH, 0, KT, x_hi, x_lo)

        pe.wait_ge(w1p_in, 32)
        pe.wait_ge(bank_read[(P_WO - 1) % 2], (P_WO - 1 + TOFF) // 2 + 1)
        for c, w1 in ((0, w1Kp), (1, w1Vp)):
            for j in range(CB):
                rows = kvT[:, c * NKV:(c + 1) * NKV, j % CS:SEQ:CS]
                last = M(ps[:, 2 + c, 64 * (j // CS):64 * (j // CS) + 64], w1[:, j, :], rows,
                         start=(j % CS == 0), stop=(j % CS == CS - 1))
            last.then_inc(cmp_sum, 1)
        for br in range(2):
            for t in range(2):
                n = br * 2 + t
                if n >= 2:
                    pe.wait_ge(vt_made, n - 1)
                for v in range(NKV):
                    src = kvT[:, (br + 1) * 2 * NKV + NKV + v, t * P:(t + 1) * P]
                    last = T(ps[:, 4 + n % 2, v * HD:(v + 1) * HD], src, ident)
                last.then_inc(vt_sum, 1)
        for br in range(2):
            pe.wait_ge(vt_made, 3 + br)
            for v in range(NKV):
                src = kvT[:, (br + 1) * 2 * NKV + NKV + v, SEQ:NT]
                last = T(ps[0:NS, 4 + br, v * HD:(v + 1) * HD], src, ident)
            last.then_inc(vt_sum, 1)
        pe.wait_ge(sig_made, 1)
        for t in range(2):
            T(ps[:, 6, t * 3 * NH:(t + 1) * 3 * NH], gT[0:3 * NH, t * P:(t + 1) * P], ident[0:3 * NH, 0:3 * NH])
        for br in range(NBR):
            last = M(ps[:, 7, br * NS:(br + 1) * NS], cst[0:3 * NH, C_HS + br * P:C_HS + (br + 1) * P],
                     gT[0:3 * NH, SEQ:NT], start=True, stop=True)
        last.then_inc(g_sum, 1)

        pe.wait_ge(rev_in, 32)
        for n in range(NH // 2):
            if n >= 2:
                pe.wait_ge(bias_made, n - 1)
            M(ps[:, n % 2, :], flip[:, 0, :], revP[:, 2 * n:2 * n + 2, :], start=True, stop=True).then_inc(bias_sum, 1)
        pe.wait_ge(cmp_hid, 4)
        M(ps[:, 2, 0:PAST + DS], flip[:, 1, :], revS[:, :], start=True, stop=True).then_inc(bias_sum, 1)
        pe.wait_ge(vt_made, 6)
        M(ps[:, 4, 0:NKV * NCMP], w2[:, 0, :], hcP[:, 0, :], start=True, stop=True)
        for v in range(NKV):
            last = M(ps[0:NCMP, 5, v * HD:(v + 1) * HD], hcP[:, 1, v * NCMP:(v + 1) * NCMP], w2[:, 1, :],
                     start=True, stop=True)
        last.then_inc(kc_sum, 1)
        pe.wait_ge(kc_made, 2)
        pe.wait_ge(gates_made, 1)
        pe.wait_ge(bias_made, NH // 2 + 1)
        pe.wait_ge(qS_made, 1)

        def kT(br, v):
            return kvT[:, (br + 1) * 2 * NKV + v, :]

        def scores(u):
            a = 2 * (u % 2)
            if u >= 2:
                pe.wait_ge(s_read, u - 1)
            if u < NH:
                v = u // GQ
                q0, q1 = qT[:, u, 0:P], qT[:, u, P:SEQ]
                both = kvT[:, 2 * NKV:, :].rearrange("p (r c v) t -> p r c v t", r=2, c=2)[:, :, 0, v, :]
                M(ps[:, a, 0:SEQ], q0, both[:, :, 0:P], start=True, stop=True)
                M(ps[:, a, 256:256 + NCMP], q0, kcP[:, v * NCMP:(v + 1) * NCMP], start=True, stop=True)
                M(ps[:, a, 272:272 + NCMP], q1, kcP[:, v * NCMP:(v + 1) * NCMP], start=True, stop=True)
                M(ps[:, a + 1, :], q1, both[:, :, 0:SEQ], start=True, stop=True).then_inc(s_made, 1)
                return
            b = u - NH
            pe.wait_ge(pastK_in[b % 2], 48 * (b // 2 + 1))
            for v in range(NKV):
                q = qS[:, b, v * GQ:(v + 1) * GQ, :].rearrange("p h i -> p (h i)")
                rows = slice(32 * v, 32 * v + 32)
                for br in range(2):
                    M(ps[rows, a + br, 0:PAST], q, pastK[:, br, v, :], start=True, stop=True)
                    M(ps[rows, a + br, PAST:PAST + NEW], q, kT(br, v)[:, SEQ:NT], start=True, stop=True)
                o = (b * NKV + v) * NCMP
                last = M(ps[rows, a, PAST + NEW:PAST + NEW + NCMP], q, kcS[:, o:o + NCMP], start=True, stop=True)
            last.then_inc(s_made, 1)

        def transposes(u):
            pe.wait_ge(p_made, u + 1)
            if u:
                pe.wait_ge(pTa_made, u)
                pe.wait_ge(pTb_made, u)
            o = sc[:, u % 3, :]
            if u < NH:
                for n, lo in enumerate((16, 288, 144, 544)):
                    T(ps[:, 4, n * P:(n + 1) * P], o[:, lo:lo + P], ident)
                for n, lo in enumerate((416, 672)):
                    T(ps[:, 5, n * P:(n + 1) * P], o[:, lo:lo + P], ident)
                T(ps[0:NCMP, 5, 256:384], o[:, 0:NCMP], ident)
                T(ps[0:NCMP, 5, 384:512], o[:, 272:272 + NCMP], ident).then_inc(t_made, 1)
                return
            W = PAST + NEW
            for br in range(2):
                for t in range(2):
                    n = br * 2 + t
                    lo = 16 + br * W + t * P
                    T(ps[:, 4, n * P:(n + 1) * P], o[:, lo:lo + P], ident)
            for br in range(2):
                lo = 16 + br * W + PAST
                T(ps[0:NS, 5, br * P:(br + 1) * P], o[:, lo:lo + NEW], ident)
            T(ps[0:NCMP, 5, 256:384], o[:, 0:NCMP], ident).then_inc(t_made, 1)
            b = u - NH
            if b:
                pe.wait_ge(vc_made, b)
            for v in range(NKV):
                o_ = (b * NKV + v) * NCMP
                last = M(ps[0:NCMP, 7, v * HD:(v + 1) * HD], hcS[:, 1, o_:o_ + NCMP], w2[:, 1, :], start=True, stop=True)
            last.then_inc(vc_sum, 1)

        def outputs(u):
            pe.wait_ge(pTa_made, u + 1)
            pe.wait_ge(pTb_made, u + 1)
            if u:
                pe.wait_ge(o_read, u)
            p = pT[:, u % 2, :]
            if u < NH:
                v = slice((u // GQ) * HD, (u // GQ + 1) * HD)
                O = ps[:, 6, 0:SEQ]
                M(O, vP[:, 0, 0, v], p[:, 0:256], start=True, stop=False)
                M(O, vP[:, 1, 0, v], p[:, 256:512], start=False, stop=False)
                M(O, vCP[:, v], p[0:NCMP, 768:1024], start=False, stop=False)
                M(O[:, P:SEQ], vP[:, 0, 1, v], p[:, 512:640], start=False, stop=False)
                M(O[:, P:SEQ], vP[:, 1, 1, v], p[:, 640:768], start=False, stop=True).then_inc(o_made, 1)
                return
            b = u - NH
            pe.wait_ge(pastV_in[b % 2], 48 * (b // 2 + 1))
            pe.wait_ge(vc_made, b + 1)
            for n in range(NKV):
                v = slice(n * HD, (n + 1) * HD)
                O = ps[32 * n:32 * n + 32, 6, 0:HD]
                for br in range(2):
                    for t in range(2):
                        c0 = (br * 2 + t) * P + 32 * n
                        M(O, p[:, c0:c0 + 32], pastV[:, br, t, v], start=(br == 0 and t == 0), stop=False)
                for br in range(2):
                    c0 = 512 + br * P + 32 * n
                    M(O, p[0:NS, c0:c0 + 32], vN[:, br, v], start=False, stop=False)
                last = M(O, p[0:NCMP, 768 + 32 * n:800 + 32 * n], vC[:, u % 2, v], start=False, stop=True)
            last.then_inc(o_made, 1)

        def turn_outputs(b):
            pe.wait_ge(oN_made, b + 1)
            T(ps[:, 6, P:2 * P], oN[:, :], ident).then_inc(oN_sum, 1)

        for s in range(UNITS + 4):
            if s >= NH + 4:
                turn_outputs(s - 4 - NH)
            if s < UNITS:
                scores(s)
            if 2 <= s < UNITS + 2:
                transposes(s - 2)
            if 3 <= s < UNITS + 3:
                outputs(s - 3)

        pe.wait_ge(o_read, UNITS)
        with pe.Fori(0, KT // 2) as i:
            for j in range(2):
                tile(P_WO + j, i, KT, x_hi, x_lo)
        acc_sum(5)
        ffn(P_FFN1, 3, 6, HT)
        acc_sum(7)

    block_ctx.close()


_IN_NAMES = ("x", "st", "gains", "consts", "onehot", "rel", "w_pool", "w_in0", "w_in1", "w_out0", "w_out1", "w_kv", "w_q",
             "w_o", "flips", "cmp_data", "cmp_w1", "cmp_pos", "cmp_b1", "cmp_w2", "slc_k", "slc_kv", "win_k", "win_kv", "pages")
_OUTS = (("y_out", (P, KT, NT)), ("pool_p_out", (P, KT, BUF)), ("pool_s_out", (P, KT, DB, BUF)),
         ("kv_out", (P, N_KVT, NT)), ("win_out", (DB, PAST - DS, 2 * NKV * HD)))


def bucket(dist):
    n = np.maximum(dist, 0)
    exact = NBUCK // 2
    big = exact + (np.log(np.maximum(n, 1).astype(np.float32) / exact) / np.log(np.float32(128 / exact)) * (NBUCK - exact)).astype(np.int32)
    return np.where(n < exact, n, np.minimum(big, NBUCK - 1))


def shape_constants():
    c = np.zeros((P, C_N), np.float32)
    c[:, C_ID:C_ID + P] = np.eye(P)
    row, col = np.arange(P)[:, None], np.arange(NS)[None, :]
    c[:, C_IM:C_IM + NS] = row % DS == col % DS
    for br in range(NBR):
        c[:3 * NH, C_HS + br * P:C_HS + (br + 1) * P] = np.arange(3 * NH)[:, None] == br * NH + np.arange(P)[None, :] // DS
    for g in range(NG):
        w = 2 ** (g + 1)
        c[:, C_INV + g * NT:C_INV + g * NT + SEQ] = np.float32(1) / np.minimum(w, np.arange(SEQ) + 1).astype(np.float32)
        c[:, C_INV + g * NT + SEQ:C_INV + (g + 1) * NT] = np.float32(1) / w
    c[:, C_RV] = np.arange(P) >= CB - 1
    hot = np.zeros((NBUCK + 1, NE), np.float32)
    d = PAST + DS - 1 - np.arange(NE)
    hot[np.where(d < 0, NBUCK, bucket(d)), np.arange(NE)] = 1
    flip = np.zeros((P, 2, P), np.float32)
    flip[np.arange(P), 0, P - 1 - np.arange(P)] = 1
    flip[np.arange(P), 1, np.arange(P) // DS * DS + DS - 1 - np.arange(P) % DS] = 1
    return c, hot, flip


def kernel(**inputs):
    import concourse.bacc as bacc
    from concourse.bass_utils import run_bass_kernel_spmd

    a = {k: np.asarray(v) for k, v in inputs.items()}

    def chunks(m):
        t = m.reshape(-1, KT, P).transpose(2, 1, 0)
        return t.reshape(P, KT, *m.shape[:-1])

    def panels(w, kt):
        k, n = w.shape
        return w.reshape(kt, P, n // P, P).transpose(2, 1, 0, 3).reshape(n // P, P, kt * P)

    def ffn_in(w):
        gate, up = panels(w[:, :DFF], KT), panels(w[:, DFF:], KT)
        return np.stack([gate, up], 1).reshape(2 * HT, P, PW)

    def ffn_out(w):
        return np.concatenate([panels(w[q * HQ * P:(q + 1) * HQ * P], HQ) for q in range(NQ)])

    consts, hot, flip = shape_constants()
    x_all = np.concatenate([a["x_prompt"].reshape(SEQ, D), a["x_sample"].reshape(NS, D)])
    norms = a["norms"].reshape(8, D)
    gains = np.concatenate([norms, a["pool_scale"].reshape(1, D), a["kv_norm"].reshape(1, D)])
    w_q = a["w_q"][0]
    w_q = np.concatenate([w_q, np.zeros((D, N_QT * P - w_q.shape[1]), w_q.dtype)], 1)
    cmp_rows = a["cache_cmp_kv"]
    n_pages = cmp_rows.shape[0]
    arrays = {
        "x": chunks(x_all),
        "st": chunks(a["state_pool"][0].reshape(DB * BUF, D)).reshape(P, KT, DB, BUF),
        "gains": gains.reshape(10, KT, P).transpose(2, 0, 1),
        "consts": consts, "onehot": hot, "flips": flip, "rel": a["rel_bias"],
        "w_pool": a["w_pool"][0].reshape(NG, GC, P, GC, P).transpose(0, 2, 3, 1, 4).reshape(NG, P, PW),
        "w_in0": ffn_in(a["w_ffn_in"][0]), "w_in1": ffn_in(a["w_ffn_in"][1]),
        "w_out0": ffn_out(a["w_ffn_out"][0]), "w_out1": ffn_out(a["w_ffn_out"][1]),
        "w_kv": panels(a["w_kv"], KT), "w_q": panels(w_q, KT), "w_o": panels(a["w_o"][0], KT),
        "cmp_data": cmp_rows.reshape(n_pages, PAGE // CS, CS, 2, NKV, HD).transpose(3, 0, 5, 2, 4, 1).reshape(
            2, n_pages, P, CS, NKV * PAGE // CS),
        "cmp_w1": a["cmp_w1"].transpose(0, 2, 1, 3), "cmp_pos": a["cmp_pos"].transpose(2, 0, 1),
        "cmp_b1": a["cmp_b1"].T, "cmp_w2": a["cmp_w2"].transpose(1, 0, 2),
        "slc_k": a["cache_slc_kv"][:, :, 0].transpose(0, 3, 2, 1),
        "slc_kv": a["cache_slc_kv"].reshape(n_pages, PAGE, 2, NKV * HD),
        "win_k": a["state_win_kv"][:, :, 0].transpose(0, 3, 2, 1),
        "win_kv": a["state_win_kv"].reshape(DB, PAST, 2, NKV * HD),
        "pages": a["page_table"].reshape(1, DB * NPG),
    }
    nc = bacc.Bacc("TRN2", target_bir_lowering=False, num_devices=1)
    args, sent = [], {}
    for name in _IN_NAMES:
        v = np.ascontiguousarray(arrays[name])
        sent[name + "_dram"] = v
        args.append(nc.dram_tensor(name + "_dram", v.shape, mybir.dt.from_np(v.dtype), kind="ExternalInput").ap())
    for name, shape in _OUTS:
        args.append(nc.dram_tensor(name + "_dram", shape, F32, kind="ExternalOutput").ap())
    build(nc, *args)
    got = run_bass_kernel_spmd(nc, [sent], core_ids=[0]).results[0]
    yt, pool_p, pool_s, kv, win = (got[name + "_dram"] for name, _ in _OUTS)

    y_all = yt.transpose(2, 1, 0).reshape(NT, D)
    kv = kv.transpose(2, 1, 0).reshape(NT, NBR, 2, NKV, HD)
    kv_p, kv_s = kv[:SEQ].reshape(1, SEQ, NBR, 2, NKV, HD), kv[SEQ:].reshape(DB, DS, NBR, 2, NKV, HD)
    win_s = np.concatenate([win.reshape(DB, PAST - DS, 2, NKV, HD), kv_s[:, :, 2]], 1)
    return (y_all[:SEQ].reshape(1, SEQ, D), y_all[SEQ:].reshape(DB, DS, D),
            pool_p.transpose(2, 1, 0).reshape(1, 1, BUF, D), pool_s.transpose(2, 3, 1, 0).reshape(1, DB, BUF, D),
            kv_p[:, :, 0], kv_s[:, :, 0], kv_p[:, :, 1], kv_s[:, :, 1], kv_p[:, :, 2], win_s)
```

```python
from contextlib import ExitStack

import numpy as np

import concourse.bass as bass
from concourse import mybir

F32 = mybir.dt.float32
F32R = mybir.dt.float32r
I32 = mybir.dt.int32
ALU = mybir.AluOpType
ACT = mybir.ActivationFunctionType
AX = mybir.AxisListType

P = 128
D = 2048
KT = D // P
SEQ, DB, DS = 256, 8, 8
NS = DB * DS
NT = SEQ + NS
PAST = 256
PAGE = 128
NPG = PAST // PAGE
DFF = 5632
HT = DFF // P
NQ = 4
HQ = HT // NQ
BUF = 15
EXT_P = BUF + SEQ
EXT_B = BUF + DS
EXT = EXT_P + DB * EXT_B
NG = 4
GC = KT // NG
NH, NKV, HD = 16, 4, 128
GQ = NH // NKV
NBR = 3
NBUCK = 32
CB, CS = 32, 16
NCMP = (PAST - CB) // CS + 1
NSUB = PAST // CS
NROW = (NKV - 1) * (NT // CS) + NSUB
EPS = 1e-6
SCALE = HD ** -0.5
NEG = -1e30
NEW = NS

PW = KT * P
PO = HQ * P
P_FFN0 = NG
PER_Q = 2 * HQ + KT
P_KV = P_FFN0 + NQ * PER_Q
N_KVT = NBR * 2 * NKV
P_Q = P_KV + N_KVT
N_QT = NH + 1
P_WO = P_Q + N_QT
P_FFN1 = P_WO + KT
TOFF = KT - NG

C_ID, C_IM, C_HS, C_INV, C_RV = 0, 128, 192, 192 + 3 * 128, 192 + 3 * 128 + NG * NT
C_N = C_RV + 1
G_POOL, G_KV = 8, 9
NE = SEQ + PAST + DS - 1


def plan_sbuf(nc):
    lo = (nc.sbuf_base + 31) // 32 * 32
    region = {}
    for name, size in (("H", KT * NT * 4), ("Y", KT * NT * 4), ("HID", 32768), ("X", 2 * KT * NT * 4),
                       ("RAW", 2 * PW * 4), ("LO", 2 * PW * 4), ("HI", 2 * PW * 4), ("Z", 19712), ("S", 0)):
        region[name] = lo
        lo += size
    used = {}

    def at(name, where, shape, dt=F32, off=None):
        n = int(np.prod(shape[1:])) * 4
        start = used.get(where, 0) if off is None else off
        used[where] = start + (n + 31) // 32 * 32
        return nc.alloc_sbuf_tensor_at(name, list(shape), dt, offset=region[where] + start)

    at.used = used
    return at


SW_S = PAST + NEW
SPANS_P = ((0, NCMP), (16, P), (144, P), (272, NCMP), (288, SEQ), (544, SEQ))
SPANS_S = ((0, NCMP), (16, SW_S), (16 + SW_S, SW_S))


def rep(ap, n):
    return ap.unsqueeze(1).broadcast_to([ap.shape[0], n, ap.shape[1]])


def spread(ap, n):
    return ap.unsqueeze(2).broadcast_to([ap.shape[0], ap.shape[1], n])


def pick(ap, off, step, n, w):
    return ap[:, off:off + n * step].rearrange("p (n s) -> p n s", n=n)[:, :, 0:w]


def build(nc, x, st, gains, consts, onehot, rel, w_pool, w_in0, w_in1, w_out0, w_out1, w_kv, w_q, w_o, flips,
          cmp_data, cmp_w1, cmp_pos, cmp_b1, cmp_w2, slc_k, slc_kv, win_k, win_kv, pages,
          y_out, pool_p_out, pool_s_out, kv_out, win_out):
    at = plan_sbuf(nc)
    h = at("h", "H", [P, KT, NT])
    y = at("y", "Y", [P, KT, NT])
    qT = at("qT", "Y", [P, KT, NT], off=0)
    hid_hi = at("hid_hi", "HID", [P, HQ, NT], F32R)
    hid_lo = at("hid_lo", "HID", [P, HQ, NT], F32R)
    ext = at("ext", "HID", [P, KT, EXT], off=0)
    kvT = at("kvT", "HID", [P, N_KVT, NT], off=0)
    stP = at("stP", "HID", [P, KT, BUF], off=KT * EXT * 4)
    bias_s = at("bias_s", "HID", [P, PAST + DS], off=N_KVT * NT * 4)
    bias_n = at("bias_n", "HID", [P, 2 * DB - 1, DS])
    x_hi = at("x_hi", "X", [P, KT, NT], F32R)
    x_lo = at("x_lo", "X", [P, KT, NT], F32R)
    w_raw = at("w_raw", "RAW", [P, 2, PW])
    w_lo = at("w_lo", "LO", [P, 2, PW], F32R)
    w_hi = at("w_hi", "HI", [P, 2, PW], F32R)
    NP_ALL = DB * NPG
    rowsK = at("rowsK", "RAW", [P, NP_ALL, CS, 32], off=0)
    w1K = at("w1K", "HI", [P, CB, P], off=0)
    rowsV = at("rowsV", "HID", [P, NP_ALL, CS, 32], off=0)
    stS = at("stS", "X", [P, KT, DB, BUF], off=2 * KT * NT * 4 - KT * DB * BUF * 4)
    w1V = at("w1V", "Z", [P, CB, P], off=0)
    w1Vy = at("w1Vy", "Y", [P, CB, P], off=0)
    sub1 = at("sub1", "Z", [P, DB * NKV, NSUB])
    brow = at("brow", "Z", [1, 2 * P])
    inv = at("inv", "Z", [P, NG, NT], off=0)
    winA = at("winA", "Z", [P, GC, EXT])
    winB = at("winB", "Z", [P, GC, EXT])
    w1Kp = at("w1Kp", "RAW", [P, CB, P], off=0)
    w1Vp = at("w1Vp", "Z", [P, CB, P], off=0)
    crow = at("crow", "X", [NROW, 2, 2 * P], off=KT * NT * 4)
    revP = at("revP", "X", [P, NH, SEQ], off=0)
    revS = at("revS", "X", [P, PAST + DS])
    vP = at("vP", "RAW", [P, 2, 2, NKV * HD], off=0)
    pastV = (at("pastV0", "LO", [P, 2, 2, NKV * HD], off=0), at("pastV1", "HI", [P, 2, 2, NKV * HD], off=0))
    pastK = (at("pastK0", "LO", [P, 2, NKV, PAST]), at("pastK1", "HI", [P, 2, NKV, PAST]))
    biasP = at("biasP", "HI", [P, NH, SEQ], off=0)
    SW = 816
    sc = at("sc", "Z", [P, 3, SW], off=0)
    pT = at("pT", "Z", [P, 2, 1024])
    cst = at("cst", "S", [P, C_INV])
    few = at("few", "S", [P, 8])
    rv, epsc, epsr, b1, b1e = few[:, 0:1], few[:, 1:2], few[:, 2:3], few[:, 3:5], few[:, 5:7]
    ones = at("ones", "S", [P, P])
    gn = at("gn", "S", [P, 10, KT])
    vN = at("vN", "S", [P, NKV * HD])
    norm_at = at.used["S"] - 4 * NKV * HD
    acc = at("acc", "S", [P, NT], off=norm_at)
    r = at("r", "S", [P, NT])
    root = acc
    sq = at("sq", "S", [P, 2, NT])
    gtmp = at("gtmp", "S", [P, 3, NS], off=norm_at + 2 * NT * 4)
    at.used["S"] = norm_at + 4 * NT * 4
    sg = at("sg", "Z", [P, NT], off=0)
    hb = at("hb", "Z", [P, NT])
    oh = at("oh", "Z", [NBUCK + 1, NE])
    trow = at("trow", "Z", [NH, NE], off=CB * P * 4)
    flip = at("flip", "Z", [P, 2, P])
    pos = at("pos", "S", [P, 2, CB])
    w2 = at("w2", "S", [P, 2, P])
    hcS = at("hcS", "S", [P, 2, DB * NKV * NCMP])
    kcS = at("kcS", "S", [P, DB * NKV * NCMP])
    sub0 = at("sub0", "S", [P, DB * NKV, NSUB])
    hcP = at("hcP", "S", [P, 2, NKV * NCMP])
    kcP = at("kcP", "S", [P, NKV * NCMP])
    vCP = at("vCP", "S", [NCMP, NKV * HD])
    tab = at("tab", "S", [NBUCK + 1, NH])
    biasC = at("biasC", "S", [P, 2, NH, NCMP])
    biasSC = at("biasSC", "S", [P, NCMP])
    gT = at("gT", "S", [P, NT])
    gP = at("gP", "S", [P, 2, 3 * NH])
    vC = (sub0[0:NCMP, :, :].rearrange("p n s -> p (n s)"), vCP[:, :])
    oN = at("oN", "S", [P, P])
    qS = at("qS", "S", [P, DB, NH, DS])
    gS = at("gS", "S", [P, 3, DB])
    neg = at("neg", "S", [P, 3, 6])
    tot = at("tot", "S", [P, 3, 6])
    rec = at("rec", "S", [P, 3, 6])
    pgs = at("pgs", "S", [1, NP_ALL], I32)
    ident = cst[:, C_ID:C_ID + P]

    bias_dram = nc.dram_tensor("bias_by_distance", (NH, NE), F32, kind="Internal").ap()

    ps = nc.alloc_psum_tensor("ps", [P, 8, 512], F32)
    STAT = 7

    sem = nc.alloc_semaphore
    x_in, const_in, st_in = [sem("x_in0"), sem("x_in1")], sem("const_in"), sem("st_in")
    gain_in, pos_in = sem("gain_in"), sem("pos_in")
    pages_in, cmpK_in = sem("pages_in"), [sem("cmpK_in0"), sem("cmpK_in1")]
    w1Vy_in, w1V_in, cmpV_in = sem("w1Vy_in"), sem("w1V_in"), sem("cmpV_in")
    raw_in = [sem("raw_in0"), sem("raw_in1")]
    w1Vp_in, w1Kp_in, oh_in, rev_in, trow_out = sem("w1Vp_in"), sem("w1Kp_in"), sem("oh_in"), sem("rev_in"), sem("trow_out")
    pastK_in, pastV_in = [sem("pastK_in0"), sem("pastK_in1")], [sem("pastV_in0"), sem("pastV_in1")]
    states_out, rows_out, win_stored, y_stored = sem("states_out"), sem("rows_out"), sem("win_stored"), sem("y_stored")
    hi_made, lo_made, tile_made = sem("hi_made"), sem("lo_made"), sem("tile_made")
    bank_read = [sem("bank_read0"), sem("bank_read1")]
    hid_hi_made, hid_made, y_zero = sem("hid_hi_made"), sem("hid_made"), sem("y_zero")
    set_made, acc_made = sem("set_made"), sem("acc_made")
    sq_made, sq_used, stat_made, root_made, r_made = (sem(n) for n in ("sq_made", "sq_used", "stat_made",
                                                                       "root_made", "r_made"))
    yn_made, h_made = sem("yn_made"), sem("h_made")
    y_pool, y_dve = sem("y_pool"), sem("y_dve")
    xhi_made, x_made, x_used = sem("xhi_made"), sem("x_made"), sem("x_used")
    silu_made, sgr_made = sem("silu_made"), sem("sgr_made")
    st_set, ext_made, ext_saved = sem("st_set"), sem("ext_made"), sem("ext_saved")
    mix_made, mixhi_made, mix_ready = sem("mix_made"), sem("mixhi_made"), sem("mix_ready")
    cmp_sum, cmp_pre, cmp_hid, kc_sum, kc_made = (sem(n) for n in ("cmp_sum", "cmp_pre", "cmp_hid", "kc_sum",
                                                                   "kc_made"))
    crow_sum, crow_made = sem("crow_sum"), sem("crow_made")
    brow_sum, brow_made, b1_sum, b1_made = sem("brow_sum"), sem("brow_made"), sem("b1_sum"), sem("b1_made")
    tab_made, trow_sum, trow_made, mask_set, bias_sum, bias_made = (
        sem(n) for n in ("tab_made", "trow_sum", "trow_made", "mask_set", "bias_sum", "bias_made"))
    vt_sum, vt_made = sem("vt_sum"), sem("vt_made")
    g_sum, sig_made, gates_made = sem("g_sum"), sem("sig_made"), sem("gates_made")
    s_made, s_read, max_made, exp_made, rec_made, p_made = (sem(n) for n in ("s_made", "s_read", "max_made",
                                                                             "exp_made", "rec_made", "p_made"))
    t_made, pTa_made, pTb_made, o_made, ohi_made, o_read = (sem(n) for n in ("t_made", "pTa_made", "pTb_made",
                                                                             "o_made", "ohi_made", "o_read"))
    oN_sum, oN_made = sem("oN_sum"), sem("oN_made")
    vc_sum, vc_made, qS_made = sem("vc_sum"), sem("vc_made"), sem("qS_made")
    dve_chain = sem("dve_chain")

    block = nc.Block()
    block_ctx = ExitStack()
    block_ctx.enter_context(block)

    UNITS = NH + DB
    BY_POOL = [i for i in range(KT) if i % 2 == 0 or i in (3, 7)]
    sub1p = sub0[:, 8:8 + NKV, :]

    def by_tokens(t, g):
        t = t[:, g * GC:(g + 1) * GC, :] if t.shape[1] == KT else t
        return t[:, :, 0:SEQ], t[:, :, SEQ:NT].rearrange("p c (b j) -> p c b j", b=DB)

    def by_positions(t, g):
        t = t[:, g * GC:(g + 1) * GC, :] if t.shape[1] == KT else t
        return t[:, :, BUF:EXT_P], t[:, :, EXT_P:EXT].rearrange("p c (b j) -> p c b j", b=DB)[:, :, :, BUF:EXT_B]

    def bias_at(u):
        return (u + NH // 2) % NH

    def out_bank(u):
        return 6 + (u + 1) % 2 if u < NH else 6

    ext_s = ext[:, :, EXT_P:EXT].rearrange("p c (b j) -> p c b j", b=DB)

    def tiles_before(c, half):
        if isinstance(half, int):
            n = c + 2 * half
            return n * GC if n <= NG else n + TOFF
        return half * 2 + (c + TOFF)

    @block.sync
    def _(sp):
        def panel(c, half, src, width):
            slot = c % 2
            if not isinstance(half, int) or c + 2 * half >= 2:
                sp.wait_ge(lo_made, half * 2 + (c - 1))
            sp.dma_start(w_raw[:, slot, 0:width], src).then_inc(raw_in[slot], 16)

        def section(c, n, src, width):
            with sp.Fori(0, n // 2) as i:
                for j in range(2):
                    panel(c + j, i, src[i * 2 + j], width)
            if n % 2:
                panel(c + n - 1, 0, src[n - 1], width)

        def ffn(c, w_in, w_out):
            with sp.Fori(0, NQ) as q:
                with sp.Fori(0, HQ) as i:
                    for j in range(2):
                        panel(c + j, q * (PER_Q // 2) + i, w_in[q * (2 * HQ) + i * 2 + j], PW)
                with sp.Fori(0, KT // 2) as i:
                    for j in range(2):
                        panel(c + 2 * HQ + j, q * (PER_Q // 2) + i, w_out[q * KT + i * 2 + j], PO)

        def page(p):
            return sp.value_load(pgs[0:1, p:p + 1], min_val=0, max_val=cmp_data.shape[1] - 1)

        sp.dma_start(pgs[:, :], pages[:, :]).then_inc(pages_in, 16)
        for i in range(2):
            sp.dma_start(h[:, i * KT // 2:(i + 1) * KT // 2, :], x[:, i * KT // 2:(i + 1) * KT // 2, :]).then_inc(x_in[i], 16)
        sp.dma_start(gn[:, :, :], gains[:, :, :]).then_inc(gain_in, 16)
        sp.dma_start(pos[:, :, :], cmp_pos[:, :, :]).then_inc(pos_in, 16)
        sp.dma_start(w1K[:, :, :], cmp_w1[0]).then_inc(cmpK_in[0], 16)
        sp.wait_ge(pages_in, 16)
        for p in range(NP_ALL):
            sp.dma_start(rowsK[:, p, :, :], cmp_data[0, page(p)]).then_inc(cmpK_in[p // (NP_ALL // 2)], 16)
            if p == NP_ALL // 2 - 1:
                sp.dma_start(stS[:, :, :, :], st[:, :, :, :]).then_inc(st_in, 16)
                sp.dma_start(inv[:, :, :], consts[:, C_INV:C_RV].rearrange("p (g t) -> p g t", g=NG)).then_inc(const_in, 16)
        sp.dma_start(cst[:, :], consts[:, 0:C_INV]).then_inc(const_in, 16)
        sp.dma_start(rv[:, :], consts[:, C_RV:C_RV + 1], allow_slow_non_contiguous=True).then_inc(const_in, 16)
        sp.dma_start(b1[:, :], cmp_b1[:, :]).then_inc(const_in, 16)
        sp.dma_start(w2[:, :, :], cmp_w2[:, :, :]).then_inc(const_in, 16)
        sp.dma_start(tab[0:NBUCK, :], rel[:, :]).then_inc(const_in, 16)
        sp.dma_start(w1Vy[:, :, :], cmp_w1[1]).then_inc(w1Vy_in, 16)

        sp.wait_ge(cmp_sum, 1)
        panel(0, 0, w_pool[0], PW)
        panel(1, 0, w_pool[1], PW)
        sp.wait_ge(mix_made, NG)
        sp.dma_start(w1V[:, :, :], cmp_w1[1]).then_inc(w1V_in, 16)
        panel(2, 0, w_pool[2], PW)
        sp.wait_ge(mix_ready, NG)
        sp.wait_ge(states_out, 32)
        for p in range(NP_ALL):
            if p == NP_ALL // 2:
                panel(3, 0, w_pool[3], PW)
            sp.dma_start(rowsV[:, p, :, :], cmp_data[1, page(p)]).then_inc(cmpV_in, 16)
        ffn(P_FFN0, w_in0, w_out0)
        section(P_KV, N_KVT, w_kv, PW)
        section(P_Q, N_QT, w_q, PW)
        sp.wait_ge(trow_sum, 1)
        sp.dma_start(w1Vp[:, :, :], cmp_w1[1]).then_inc(w1Vp_in, 16)
        sp.wait_ge(bank_read[(P_Q - 1) % 2], (P_Q - 1 + TOFF) // 2 + 1)
        sp.wait_ge(bank_read[P_Q % 2], (P_Q - 2 + TOFF) // 2 + 1)
        sp.dma_start(kv_out[:, :, :], kvT[:, :, :]).then_inc(rows_out, 16)

        sp.wait_ge(lo_made, P_WO)
        sp.dma_start(w1Kp[:, :, :], cmp_w1[0]).then_inc(w1Kp_in, 16)
        sp.wait_ge(trow_out, 16)
        sp.wait_ge(tile_made, P_WO + TOFF)
        t = bias_dram.tensor
        sp.dma_start(revP[:, :, :], bass.AP(t, DS, [[1, P], [NE, NH], [1, SEQ]])).then_inc(rev_in, 16)
        sp.dma_start(revS[:, :], bass.AP(t, 0, [[NE, NH], [1, DS], [1, PAST + DS]])).then_inc(rev_in, 16)

        def load_keys(b):
            if b >= 2:
                sp.wait_ge(s_made, NH + b - 1)
            for p in range(NPG):
                sp.dma_start(pastK[b % 2][:, 0, :, p * PAGE:(p + 1) * PAGE], slc_k[page(b * NPG + p)]).then_inc(pastK_in[b % 2], 16)
            sp.dma_start(pastK[b % 2][:, 1, :, :], win_k[b]).then_inc(pastK_in[b % 2], 16)

        def load_values(b):
            if b >= 2:
                sp.wait_ge(o_made, NH + b - 1)
            for p in range(NPG):
                sp.dma_start(pastV[b % 2][:, 0, p, :], slc_kv[page(b * NPG + p), :, 1, :]).then_inc(pastV_in[b % 2], 16)
            sp.dma_start(pastV[b % 2][:, 1, :, :], win_kv[b, :, 1, :].rearrange("(t p) n -> p t n", p=P)).then_inc(pastV_in[b % 2], 16)

        load_keys(0)
        load_values(0)
        sp.wait_ge(crow_sum, 2)
        panel(P_WO, 0, w_o[0], PW)
        sp.wait_ge(s_read, NH // 2)
        load_keys(1)
        sp.wait_ge(s_read, NH)
        load_values(1)
        for b in range(2, DB + 3):
            if b < DB:
                load_keys(b)
            if b == 4:
                sp.wait_ge(o_made, NH)
                panel(P_WO + 1, 0, w_o[1], PW)
            if b >= 5:
                load_values(b - 3)

        with sp.Fori(1, KT // 2) as i:
            for j in range(2):
                panel(P_WO + j, i, w_o[i * 2 + j], PW)
        ffn(P_FFN1, w_in1, w_out1)
        for i in range(0, KT, 2):
            n = sum(j < i + 2 for j in BY_POOL)
            sp.wait_ge(y_pool, n)
            sp.wait_ge(y_dve, i + 2 - n)
            sp.dma_start(y_out[:, i:i + 2, :], h[:, i:i + 2, :]).then_inc(y_stored, 16)
        sp.wait_ge(states_out, 32)
        sp.wait_ge(rows_out, 16)
        sp.wait_ge(win_stored, 16 * DB)
        sp.wait_ge(y_stored, 16 * KT // 2)

    @block.scalar
    def _(act):
        A = nc.scalar.activation

        def hi_split(c, half, width=PW):
            slot = c % 2
            act.wait_ge(raw_in[slot], half * 16 + 16 * (c // 2 + 1))
            if not isinstance(half, int) or c + 2 * half >= 2:
                act.wait_ge(tile_made, tiles_before(c - 1, half))
            nc.scalar.copy(w_hi[:, slot, 0:width], w_raw[:, slot, 0:width]).then_inc(hi_made, 1)

        def squares(m, src, ready, after=lambda i: None):
            for i in range(KT):
                ready(i)
                if i >= 2 and m % 2 == 0:
                    act.wait_ge(sq_used, (KT - 1) * (m // 2) + i - 1)
                if i >= 2 and m % 2:
                    act.wait_ge(acc_made, KT * (m // 2) + i)
                nc.scalar.square(sq[:, i % 2, :], src[:, i, :]).then_inc(sq_made, 1)
                after(i)

        def sqrt_table():
            A(epsr[:, :], epsc[:, :], ACT.Sqrt)

        def rms_root(m):
            act.wait_ge(stat_made, m + 1)
            A(root[:, :], ps[:, STAT, 0:NT], ACT.Sqrt, bias=epsc[:, 0:1], scale=1.0 / D).then_inc(root_made, 1)

        def x_high(k, g, i):
            A(x_hi[:, i, :], h[:, i, :], ACT.Copy, scale=gn[:, g, i:i + 1]).then_inc(xhi_made, 1)

        def gelu(n, c, dst):
            act.wait_ge(cmp_pre, n + 1)
            act.wait_ge(b1_made, 1)
            A(dst.rearrange("p (a s) -> p a s", s=NCMP), sub0[:, 0:dst.shape[1] // NCMP, 0:NCMP],
              ACT.Gelu_apprx_tanh, bias=b1e[:, c:c + 1]).then_inc(cmp_hid, 1)

        def ffn(c, m, next_width, free=lambda: None):
            def pair(q19, i, w):
                half = q19 + i
                act.wait_ge(bank_read[c % 2], half + ((c + TOFF) // 2 + 1))
                A(sg[:, :], sg[:, :], ACT.Silu).then_inc(silu_made, 1)
                hi_split(c + 2, half, w)
                act.wait_ge(bank_read[(c + 1) % 2], half + ((c + 1 + TOFF) // 2 + 1))
                nc.scalar.copy(hid_hi[:, i, :], hb[:, :]).then_inc(hid_hi_made, 1)
                hi_split(c + 3, half, w)

            def out_steps(q19, w_last):
                with act.Fori(0, KT // 2 - 1) as i:
                    for j in range(2):
                        hi_split(c + 2 * HQ + 2 + j, q19 + i, PO)
                if w_last:
                    for j in range(2):
                        hi_split(c + 2 * HQ + KT + j, q19, w_last)

            free()
            with act.Fori(0, NQ - 1) as q:
                with act.Fori(0, HQ - 1) as i:
                    pair(q * (PER_Q // 2), i, PW)
                pair(q * (PER_Q // 2), HQ - 1, PO)
                out_steps(q * (PER_Q // 2), PW)
            q19 = (NQ - 1) * (PER_Q // 2)
            with act.Fori(0, HQ - 1) as i:
                pair(q19, i, PW)
            pair(q19, HQ - 1, PO)
            o = c + 2 * HQ + 2 * q19

            def next_split(i):
                if i < KT - 2:
                    hi_split(o + i + 2, 0, PO)
                elif next_width and i == KT - 2:
                    hi_split(o + i + 2, 0, next_width)
            sqrt_table()
            squares(m, y, lambda i: act.wait_ge(bank_read[(o + i) % 2], (o + i + TOFF) // 2 + 1), next_split)

        def post_and_pre(a, m, k, g, second):
            rms_root(m)
            hi_split(second, 0)

            def ready(i):
                act.wait_ge(h_made, KT * a + i + 1)
            squares(m + 1, h, ready, lambda i: x_high(k, g, i))
            rms_root(m + 1)

        act.wait_ge(set_made, 1)
        sqrt_table()
        squares(0, h, lambda i: act.wait_ge(x_in[i // (KT // 2)], 16))
        rms_root(0)
        act.wait_ge(st_in, 16)
        nc.scalar.copy(ext_s[:, :, :, 0:BUF], stS[:, :, :, :]).then_inc(st_set, 1)
        act.wait_ge(ext_made, 1)
        act.wait_ge(st_set, 1)
        nc.scalar.copy(stP[:, :, :], ext[:, :, SEQ:EXT_P])
        nc.scalar.copy(stS[:, :, :, :], ext_s[:, :, :, DS:EXT_B]).then_inc(ext_saved, 1)
        for g in range(NG):
            if g == NG - 1:
                hi_split(0, 0)
                hi_split(1, 0)
            act.wait_ge(mix_made, g + 1)
            for dst, src in zip(by_tokens(x_hi, g), by_positions(ext, g)):
                last = nc.scalar.copy(dst, src)
            last.then_inc(mixhi_made, 1)

        def pool_ready(i):
            if i == 2:
                gelu(0, 0, hcS[:, 0, :])
            if i % GC == 0 and i < KT - GC:
                hi_split(i // GC + 2, 0)
            act.wait_ge(bank_read[i % 2], i // 2 + 1)
        squares(1, y, pool_ready)
        post_and_pre(0, 1, 0, 2, P_FFN0 + 1)
        gelu(1, 1, hcS[:, 1, :])
        ffn(P_FFN0, 3, PW)
        post_and_pre(1, 3, 1, G_KV, P_KV + 1)
        with act.Fori(0, N_KVT // 2 - 1) as i:
            for j in range(2):
                hi_split(P_KV + 2 + j, i)
        hi_split(P_Q, 0)
        for i in range(KT):
            if i < KT - 1:
                act.wait_ge(x_used, i + 1)
            else:
                act.wait_ge(tile_made, P_Q + TOFF)
            x_high(2, 4, i)
        hi_split(P_Q + 1, 0)
        with act.Fori(0, NH // 2 - 1) as i:
            for j in range(2):
                hi_split(P_Q + 2 + j, i)
        hi_split(P_Q + NH, 0)
        act.wait_ge(bank_read[(P_Q + NH) % 2], (P_Q + NH + TOFF) // 2 + 1)
        A(gT[:, :], gT[:, :], ACT.Sigmoid).then_inc(sig_made, 1)

        gelu(2, 1, hcP[:, 1, :])
        gelu(3, 0, hcP[:, 0, :])

        def exps(u):
            act.wait_ge(max_made, u + 1)
            if u >= 3:
                act.wait_ge(rec_made, u - 2)
            s3 = u % 3
            for n, (lo, w) in enumerate(SPANS_P if u < NH else SPANS_S):
                last = A(sc[:, s3, lo:lo + w], sc[:, s3, lo:lo + w], ACT.Exp, bias=neg[:, s3, n:n + 1],
                         accum_out=tot[:, s3, n:n + 1])
            last.then_inc(exp_made, 1)

        def copy_p(u):
            act.wait_ge(t_made, u + 1)
            if u >= 2:
                act.wait_ge(o_made, u - 1)
            nc.scalar.copy(pT[:, u % 2, 0:512], ps[:, 4, :]).then_inc(pTa_made, 1)

        def out_high(u):
            if u < NH:
                act.wait_ge(o_made, u + 1)
                nc.scalar.copy(x_hi[:, u, 0:SEQ], ps[:, out_bank(u), 0:SEQ]).then_inc(ohi_made, 1)
            else:
                o = SEQ + (u - NH) * DS
                act.wait_ge(oN_sum, u - NH + 1)
                nc.scalar.copy(x_hi[:, :, o:o + DS], ps[:, 6, P:2 * P].rearrange("p (h i) -> p h i", h=NH)).then_inc(ohi_made, 1)

        def out_rows(u):
            act.wait_ge(o_made, u + 1)
            nc.scalar.copy(oN[:, :], ps[:, 6, 0:P]).then_inc(oN_made, 1)

        for s in range(UNITS + 4):
            if s >= 4:
                out_high(s - 4)
            if 2 <= s < UNITS + 2:
                copy_p(s - 2)
            if s < UNITS:
                exps(s)
            if NH + 3 <= s < UNITS + 3:
                out_rows(s - 3)
            if s == UNITS:
                act.wait_ge(s_made, UNITS)
                hi_split(P_WO, 0)

        act.wait_ge(o_made, UNITS)
        hi_split(P_WO + 1, 0)
        sqrt_table()
        squares(5, y, lambda i: act.wait_ge(bank_read[(P_WO + i) % 2], (P_WO + i + TOFF) // 2 + 1),
                lambda i: hi_split(P_WO + i + 2, 0) if i < KT - 1 else None)
        post_and_pre(2, 5, 3, 6, P_FFN1 + 1)
        ffn(P_FFN1, 7, None, lambda: act.wait_ge(rows_out, 16))
        rms_root(7)

    @block.vector
    def _(dve):
        V = nc.vector
        chain = [0]

        def link(ins):
            chain[0] += 1
            ins.then_inc(dve_chain, 1)
            dve.wait_ge(dve_chain, chain[0])

        def lo_split(c, half, width=PW):
            slot = c % 2
            dve.wait_ge(hi_made, half * 2 + (c + 1))
            V.tensor_tensor(w_lo[:, slot, 0:width], w_raw[:, slot, 0:width],
                            w_hi[:, slot, 0:width].bitcast(F32), ALU.subtract).then_inc(lo_made, 1)

        def tile_wait(c, half):
            dve.wait_ge(tile_made, half * 2 + (c + TOFF + 1))

        def rms_recip(m):
            dve.wait_ge(root_made, m + 1)
            V.reciprocal(r[:, :], root[:, :]).then_inc(r_made, 1)
            dve.wait_ge(r_made, m + 1)

        def x_low(k, g, i):
            dve.wait_ge(xhi_made, 16 * k + i + 1)
            V.scalar_tensor_tensor(out=x_lo[:, i, :], in0=h[:, i, :], scalar=gn[:, g, i:i + 1],
                                   in1=x_hi[:, i, :].bitcast(F32), op0=ALU.mult, op1=ALU.subtract).then_inc(x_made, 1)

        def post_norm(a, m, g, lows=lambda i: None, second=None):
            rms_recip(m)
            for i in range(KT + 3):
                if i < KT:
                    V.scalar_tensor_tensor(out=y[:, i, :], in0=y[:, i, :], scalar=gn[:, g, i:i + 1], in1=r[:, :],
                                           op0=ALU.mult, op1=ALU.mult).then_inc(yn_made, 1)
                if a == 3 and i < KT and i not in BY_POOL:
                    dve.wait_ge(yn_made, 16 * a + i + 1)
                    V.tensor_tensor(h[:, i, :], h[:, i, :], y[:, i, :], ALU.add).then_inc(y_dve, 1)
                if i == 3 and second:
                    lo_split(second, 0)
                if i >= 3:
                    lows(i - 3)

        V.memset(tab[NBUCK:NBUCK + 1, :], NEG).then_inc(tab_made, 1)
        dve.wait_ge(gain_in, 16)
        dve.wait_ge(x_in[0], 16)
        dve.wait_ge(x_in[1], 16)
        rms_recip(0)
        for i in range(KT):
            V.scalar_tensor_tensor(out=ext[:, i, BUF:EXT_P], in0=h[:, i, 0:SEQ], scalar=gn[:, 0, i:i + 1],
                                   in1=r[:, 0:SEQ], op0=ALU.mult, op1=ALU.mult)
            es = ext[:, i, EXT_P:EXT].rearrange("p (b j) -> p b j", b=DB)[:, :, BUF:EXT_B]
            last = V.scalar_tensor_tensor(out=es, in0=h[:, i, SEQ:NT].rearrange("p (b j) -> p b j", b=DB),
                                          scalar=gn[:, 0, i:i + 1],
                                          in1=r[:, SEQ:NT].rearrange("p (b j) -> p b j", b=DB),
                                          op0=ALU.mult, op1=ALU.mult)
        last.then_inc(ext_made, 1)
        dve.wait_ge(ext_made, 1)
        dve.wait_ge(const_in, 16 * 6)
        dve.wait_ge(st_set, 1)

        def window_sums(g):
            e = ext[:, g * GC:(g + 1) * GC, :]
            src, at_, bufs = e, 0, (winA, winB)
            if g:
                dve.wait_ge(mix_made, g)
            for n in range(g + 1):
                w = 2 ** n
                dst = bufs[n % 2]
                o = at_ + w
                link(V.tensor_tensor(dst[:, :, o:EXT], src[:, :, o:EXT], src[:, :, o - w:EXT - w], ALU.add))
                src, at_ = dst, o
            mean = bufs[(g + 1) % 2]
            counts = (rep(inv[:, g, 0:SEQ], GC),
                      rep(inv[:, g, SEQ:NT], GC).rearrange("p c (b j) -> p c b j", b=DB))
            for dst, total, c in zip(by_tokens(mean, g), by_positions(src, g), counts):
                last = V.tensor_tensor(dst, total, c, ALU.mult)
            link(last)
            if g == 0:
                dve.wait_ge(ext_saved, 1)
            for m_, x_ in zip(by_tokens(mean, g), by_positions(ext, g)):
                last = V.tensor_tensor(x_, m_, x_, ALU.subtract)
            last.then_inc(mix_made, 1)

        def cmp_join(n, bank, nseq, pages_apart):
            dve.wait_ge(cmp_sum, n + 1)
            if n:
                dve.wait_ge(cmp_hid, n)
            if pages_apart:
                for dst, b_ in ((sub0, bank), (sub1, bank + 1)):
                    for p in range(NPG):
                        d_ = dst[:, :, :].rearrange("p (b h) s -> p b h s", h=NKV)[:, :, :, p * 8:p * 8 + 8]
                        s_ = ps[:, b_, :].rearrange("p (b g h s) -> p b g h s", b=DB, g=NPG, h=NKV)[:, :, p, :, :]
                        last = V.tensor_copy(d_, s_)
            else:
                V.tensor_copy(sub0[:, 0:nseq, :], pick(ps[:, bank, :], 0, NT // CS, NKV, NSUB))
                last = V.tensor_copy(sub1p[:, 0:nseq, :], pick(ps[:, bank, :], P, NT // CS, NKV, NSUB))
            link(last)
            s1 = sub1 if pages_apart else sub1p
            V.tensor_tensor(sub0[:, 0:nseq, 0:NCMP], sub0[:, 0:nseq, 0:NCMP], s1[:, 0:nseq, 1:NSUB],
                            ALU.add).then_inc(cmp_pre, 1)

        for g in range(NG):
            window_sums(g)
        dve.wait_ge(mix_made, NG)

        dve.wait_ge(brow_sum, 1)
        V.tensor_copy(brow[:, :], ps[0:1, 6, 0:2 * P]).then_inc(brow_made, 1)
        lo_split(0, 0)
        lo_split(1, 0)
        dve.wait_ge(b1_sum, 1)
        V.tensor_tensor(b1e[:, :], b1[:, :], ps[:, 6, 2 * P:2 * P + 2], ALU.add).then_inc(b1_made, 1)
        cmp_join(0, 2, DB * NKV, True)

        def pool_tiles(g):
            for n in range(g * GC, (g + 1) * GC):
                dve.wait_ge(tile_made, n + 1)
                V.tensor_scalar(y[:, n, :], ps[:, n % 2, 0:NT], gn[:, G_POOL, n:n + 1], None,
                                ALU.mult).then_inc(bank_read[n % 2], 1)
                if g and n % GC == 0:
                    lo_split(g + 1, 0)
        for g in range(NG):
            pool_tiles(g)
        dve.wait_ge(kc_sum, 1)
        V.tensor_copy(kcS[:, :], ps[:, 2, 0:DB * NKV * NCMP]).then_inc(kc_made, 1)
        post_norm(0, 1, 1, lambda i: x_low(0, 2, i), P_FFN0 + 1)
        rms_recip(2)
        cmp_join(1, 4, DB * NKV, True)

        def ffn(c, next_width):
            def pair(q19, i, w):
                half = q19 + i
                n = pairs_before(c, q19, i)
                tile_wait(c, half)
                V.tensor_tensor(sg[:, :], ps[:, c % 2, 0:NT], r[:, :], ALU.mult).then_inc(bank_read[c % 2], 1)
                lo_split(c + 2, half, w)
                dve.wait_ge(silu_made, n)
                V.tensor_tensor(sg[:, :], sg[:, :], r[:, :], ALU.mult).then_inc(sgr_made, 1)
                tile_wait(c + 1, half)
                dve.wait_ge(sgr_made, n)
                dve.wait_ge(hid_made, n)
                V.tensor_tensor(hb[:, :], sg[:, :], ps[:, (c + 1) % 2, 0:NT], ALU.mult).then_inc(bank_read[(c + 1) % 2], 1)
                lo_split(c + 3, half, w)

            def pairs_before(c_, q19, i):
                base = 1 if c_ == P_FFN0 else 1 + HT
                if isinstance(q19, int):
                    return i + (base + (q19 // (PER_Q // 2)) * HQ)
                return i + q_reg[0] * HQ + base

            def outs(q19, w_last, n_last=2):
                o = c + 2 * HQ

                def one(j, i, n):
                    tile_wait(o + j, q19 + i)
                    V.tensor_tensor(y[:, n, :], y[:, n, :], ps[:, (o + j) % 2, 0:NT], ALU.add).then_inc(bank_read[(o + j) % 2], 1)
                with dve.Fori(0, KT // 2 - 1) as i:
                    for j in range(2):
                        one(j, i, i * 2 + j)
                        lo_split(o + 2 + j, q19 + i, PO)
                for j in range(2):
                    one(j, KT // 2 - 1, KT - 2 + j)
                    if w_last and j < n_last:
                        lo_split(o + 2 + j, q19 + (KT // 2 - 1), w_last)

            q_reg = [0]
            dve.wait_ge(y_zero, 1 if c == P_FFN0 else 2)
            with dve.Fori(0, NQ - 1) as q:
                q_reg[0] = q
                with dve.Fori(0, HQ - 1) as i:
                    pair(q * (PER_Q // 2), i, PW)
                pair(q * (PER_Q // 2), HQ - 1, PO)
                outs(q * (PER_Q // 2), PW)
            q19 = (NQ - 1) * (PER_Q // 2)
            with dve.Fori(0, HQ - 1) as i:
                pair(q19, i, PW)
            pair(q19, HQ - 1, PO)
            outs(q19, next_width, 1)

        ffn(P_FFN0, PW)
        post_norm(1, 3, 3, lambda i: x_low(1, G_KV, i), P_KV + 1)
        rms_recip(4)

        def scaled(c, half, dst):
            tile_wait(c, half)
            V.tensor_tensor(dst, ps[:, c % 2, 0:NT], r[:, :], ALU.mult).then_inc(bank_read[c % 2], 1)

        with dve.Fori(0, N_KVT // 2 - 1) as i:
            for j in range(2):
                scaled(P_KV + j, i, kvT[:, i * 2 + j, :])
                lo_split(P_KV + 2 + j, i)
        scaled(P_Q - 2, 0, kvT[:, N_KVT - 2, :])
        lo_split(P_Q, 0)
        for i in range(KT):
            x_low(2, 4, i)
        scaled(P_Q - 1, 0, kvT[:, N_KVT - 1, :])
        lo_split(P_Q + 1, 0)
        dve.wait_ge(trow_sum, 1)
        V.tensor_copy(trow[:, 0:512], ps[0:NH, 2, :])
        V.tensor_copy(trow[:, 512:NE], ps[0:NH, 3, 0:NE - 512]).then_inc(trow_made, 1)
        with dve.Fori(0, NH // 2 - 1) as i:
            for j in range(2):
                scaled(P_Q + j, i, qT[:, i * 2 + j, :])
                lo_split(P_Q + 2 + j, i)
        scaled(P_Q + NH - 2, 0, qT[:, NH - 2, :])
        lo_split(P_Q + NH, 0)
        scaled(P_Q + NH - 1, 0, qT[:, NH - 1, :])
        scaled(P_Q + NH, 0, gT[:, :])

        for n, c in enumerate((1, 0)):
            dve.wait_ge(crow_sum, n + 1)
            V.tensor_copy(crow[:, c, :], ps[0:NROW, 2 + c, 0:2 * P]).then_inc(crow_made, 1)
        cmp_join(2, 3, NKV, False)
        for n in range(4):
            if n == 2:
                cmp_join(3, 2, NKV, False)
            dve.wait_ge(vt_sum, n + 1)
            V.tensor_copy(vP[:, n // 2, n % 2, :], ps[:, 4 + n % 2, :]).then_inc(vt_made, 1)
        dve.wait_ge(vt_sum, 5)
        V.tensor_copy(vN[:, :], ps[:, 4, :]).then_inc(vt_made, 1)

        dve.wait_ge(g_sum, 1)
        V.tensor_copy(gP[:, :, :], ps[:, 6, 0:2 * 3 * NH].rearrange("p (t n) -> p t n", t=2))
        link(V.tensor_tensor(gtmp[:, :, :], ps[:, 7, 0:3 * NS].rearrange("p (r n) -> p r n", r=3),
                             rep(cst[:, C_IM:C_IM + NS], 3), ALU.mult))
        V.tensor_scalar(gP[:, 0, 0:NH], gP[:, 0, 0:NH], rv[:, 0:1], None, ALU.mult)
        V.tensor_reduce(gS[:, :, :], gtmp[:, :, :].rearrange("p r (b i) -> p r b i", b=DB), AX.X,
                        ALU.add).then_inc(gates_made, 1)
        dve.wait_ge(gates_made, 1)

        for n in range(NH // 2):
            dve.wait_ge(bias_sum, n + 1)
            V.tensor_copy(biasP[:, bias_at(2 * n):bias_at(2 * n) + 2, :], ps[:, n % 2, :].rearrange("p (h k) -> p h k", h=2)).then_inc(bias_made, 1)
        dve.wait_ge(bias_sum, NH // 2 + 1)
        dve.wait_ge(mask_set, 1)
        V.tensor_copy(bias_s[:, :], ps[:, 2, 0:PAST + DS])
        link(V.tensor_copy(bias_n[:, DB - 1, :], ps[:, 2, PAST:PAST + DS]))
        V.tensor_copy(biasC[:, 1, :, :], biasP[:, :, CB - 1:SEQ:CS])
        n0 = len(range(P + CB - 1, SEQ, CS))
        V.tensor_copy(biasC[:, 0, :, 0:n0], biasP[:, :, P + CB - 1:SEQ:CS])
        V.tensor_copy(biasSC[:, :], bias_s[:, CB - 1:PAST:CS]).then_inc(bias_made, 1)
        dve.wait_ge(bias_made, NH // 2 + 1)

        dve.wait_ge(kc_sum, 2)
        V.tensor_copy(kcP[:, :], ps[:, 4, 0:NKV * NCMP])
        V.tensor_copy(vCP[:, :], ps[0:NCMP, 5, :]).then_inc(kc_made, 1)

        def scores_p(u):
            s3, a = u % 3, 2 * (u % 2)
            dve.wait_ge(s_made, u + 1)
            if u >= 3:
                dve.wait_ge(t_made, u - 2)
            o = sc[:, s3, :]
            V.scalar_tensor_tensor(out=o[:, 16:272].rearrange("p (r k) -> p r k", r=2),
                                   in0=ps[:, a, 0:256].rearrange("p (r k) -> p r k", r=2), scalar=SCALE,
                                   in1=rep(biasP[:, bias_at(u), P:SEQ], 2), op0=ALU.mult, op1=ALU.add)
            V.scalar_tensor_tensor(out=pick(o, 0, 272, 2, NCMP), in0=pick(ps[:, a, :], 256, 16, 2, NCMP), scalar=SCALE,
                                   in1=biasC[:, :, bias_at(u), :], op0=ALU.mult, op1=ALU.add)
            link(V.scalar_tensor_tensor(out=o[:, 288:800].rearrange("p (r k) -> p r k", r=2),
                                        in0=ps[:, a + 1, :].rearrange("p (r k) -> p r k", r=2), scalar=SCALE,
                                        in1=rep(biasP[:, bias_at(u), :], 2), op0=ALU.mult, op1=ALU.add))
            V.tensor_reduce(pick(neg[:, s3, :], 0, 3, 2, 1)[:, :, 0], pick(o, 0, 272, 2, NCMP), AX.X, ALU.max,
                            negate=True).then_inc(s_read, 1)
            V.tensor_reduce(neg[:, s3, 1:3], o[:, 16:272].rearrange("p (r k) -> p r k", r=2), AX.X, ALU.max, negate=True)
            V.tensor_reduce(neg[:, s3, 4:6], o[:, 288:800].rearrange("p (r k) -> p r k", r=2), AX.X, ALU.max,
                            negate=True).then_inc(max_made, 1)

        def scores_s(u):
            b, s3, a = u - NH, u % 3, 2 * (u % 2)
            W = PAST + NEW
            dve.wait_ge(s_made, u + 1)
            dve.wait_ge(t_made, u - 2)
            o = sc[:, s3, :]
            two = ps[:, a:a + 2, :]
            ob = o[:, 16:16 + 2 * W].rearrange("p (r k) -> p r k", r=2)
            V.scalar_tensor_tensor(out=pick(o, 16, W + NEW, 2, PAST), in0=two[:, :, 0:PAST], scalar=SCALE,
                                   in1=rep(bias_s[:, 0:PAST], 2), op0=ALU.mult, op1=ALU.add)
            bn = bias_n[:, DB - 1 - b:2 * DB - 1 - b, :].rearrange("p a j -> p (a j)")
            V.scalar_tensor_tensor(out=o[:, 16 + PAST:16 + PAST + 2 * NEW].rearrange("p (r k) -> p r k", r=2), in0=two[:, :, PAST:W], scalar=SCALE,
                                   in1=rep(bn, 2), op0=ALU.mult, op1=ALU.add)
            link(V.scalar_tensor_tensor(out=o[:, 0:NCMP], in0=ps[:, a, W:W + NCMP], scalar=SCALE,
                                        in1=biasSC[:, :], op0=ALU.mult, op1=ALU.add))
            V.tensor_reduce(neg[:, s3, 0:1], o[:, 0:NCMP], AX.X, ALU.max, negate=True).then_inc(s_read, 1)
            V.tensor_reduce(neg[:, s3, 1:3], ob, AX.X, ALU.max, negate=True).then_inc(max_made, 1)

        def recips(u):
            s3 = u % 3
            dve.wait_ge(exp_made, u + 1)
            if u >= 3:
                dve.wait_ge(p_made, u - 2)
            n = 6 if u < NH else 3
            link(V.reciprocal(rec[:, s3, 0:n], tot[:, s3, 0:n]))
            if u < NH:
                V.tensor_tensor(rec[:, s3, :].rearrange("p (t r) -> p t r", t=2), rec[:, s3, :].rearrange("p (t r) -> p t r", t=2),
                                gP[:, :, :].rearrange("p t (r h) -> p t r h", h=NH)[:, :, :, u], ALU.mult).then_inc(rec_made, 1)
            else:
                V.tensor_tensor(rec[:, s3, 0:3], rec[:, s3, 0:3], gS[:, :, u - NH], ALU.mult).then_inc(rec_made, 1)

        def copy_p(u):
            dve.wait_ge(t_made, u + 1)
            if u >= 2:
                dve.wait_ge(o_made, u - 1)
            if u < NH:
                V.tensor_copy(pT[:, u % 2, 512:768], ps[:, 5, 0:256])
                V.tensor_copy(pT[0:NCMP, u % 2, 768:1024], ps[0:NCMP, 5, 256:512]).then_inc(pTb_made, 1)
            else:
                V.tensor_copy(pT[:, u % 2, 512:640], ps[:, 5, 0:P])
                V.tensor_copy(pT[0:NCMP, u % 2, 768:896], ps[0:NCMP, 5, 256:384]).then_inc(pTb_made, 1)

        def copy_values(u):
            dve.wait_ge(vc_sum, u - NH + 1)
            V.tensor_copy(vC[u % 2], ps[0:NCMP, 7, :]).then_inc(vc_made, 1)

        def out_low(u):
            dve.wait_ge(ohi_made, u + 1)
            if u < NH:
                V.tensor_tensor(x_lo[:, u, 0:SEQ], ps[:, out_bank(u), 0:SEQ], x_hi[:, u, 0:SEQ].bitcast(F32),
                                ALU.subtract).then_inc(o_read, 1)
            else:
                o = SEQ + (u - NH) * DS
                V.tensor_tensor(x_lo[:, :, o:o + DS], ps[:, 6, P:2 * P].rearrange("p (h i) -> p h i", h=NH),
                                x_hi[:, :, o:o + DS].bitcast(F32), ALU.subtract).then_inc(o_read, 1)

        for s in range(UNITS + 4):
            if s >= NH + 4:
                out_low(s - 4)
            if s < UNITS:
                scores_p(s) if s < NH else scores_s(s)
            if 1 <= s < UNITS + 1:
                recips(s - 1)
            if 2 <= s < UNITS + 2:
                copy_p(s - 2)
            if 4 <= s < NH + 4:
                out_low(s - 4)
            if NH + 2 <= s < UNITS + 2:
                copy_values(s - 2)
            if s == UNITS:
                dve.wait_ge(s_made, UNITS)
                lo_split(P_WO, 0)

        dve.wait_ge(o_made, UNITS)
        lo_split(P_WO + 1, 0)
        for i in range(KT):
            dve.wait_ge(tile_made, P_WO + TOFF + i + 1)
            V.tensor_copy(y[:, i, :], ps[:, (P_WO + i) % 2, 0:NT]).then_inc(bank_read[(P_WO + i) % 2], 1)
            if i < KT - 1:
                lo_split(P_WO + i + 2, 0)
        post_norm(2, 5, 5, lambda i: x_low(3, 6, i), P_FFN1 + 1)
        rms_recip(6)
        ffn(P_FFN1, None)
        post_norm(3, 7, 7)

    @block.gpsimd
    def _(pool):
        G = nc.gpsimd

        def add_squares(m):
            pool.wait_ge(r_made, m)
            G.memset(acc[:, :], 0.0).then_inc(acc_made, 1)
            for i in range(KT - 1):
                pool.wait_ge(sq_made, 16 * m + i + 1)
                pool.wait_ge(acc_made, KT * (m // 2) + i + 1)
                G.tensor_tensor(acc[:, :], acc[:, :], sq[:, i % 2, :], ALU.add).then_inc(acc_made, 1)

        def residual(a):
            for i in range(KT):
                pool.wait_ge(yn_made, 16 * a + i + 1)
                G.tensor_tensor(h[:, i, :], h[:, i, :], y[:, i, :], ALU.add).then_inc(h_made, 1)

        def clear_y(n):
            pool.wait_ge(h_made, KT * n)
            G.memset(y[:, :, :], 0.0).then_inc(y_zero, 1)

        def ffn(m):
            base = a_pairs[0]

            def pair(i, before):
                pool.wait_ge(hid_hi_made, i + before + 1)
                G.tensor_tensor(hid_lo[:, i, :], hb[:, :], hid_hi[:, i, :].bitcast(F32),
                                ALU.subtract).then_inc(hid_made, 1)
            with pool.Fori(0, NQ) as q:
                with pool.Fori(0, HQ) as i:
                    pair(i, q * HQ + base)
                b = q + (0 if m == 3 else NQ)
                pool.dma_start(win_out[b], win_kv[b, DS:PAST].rearrange("t c n -> t (c n)")).then_inc(win_stored, 16)
            a_pairs[0] += HT
            add_squares(m)

        a_pairs = [0]
        G.memset(epsc[:, :], EPS).then_inc(hid_made, 1)
        G.memset(ones[:, :], 1.0)
        G.memset(ext[:, :, 0:BUF], 0.0).then_inc(set_made, 1)
        pool.wait_ge(ext_saved, 1)
        pool.dma_start(pool_p_out[:, :, :], stP[:, :, :]).then_inc(states_out, 16)
        pool.dma_start(pool_s_out[:, :, :, :], stS[:, :, :, :]).then_inc(states_out, 16)
        for g in range(NG):
            if g == 2:
                pool.wait_ge(states_out, 32)
            pool.wait_ge(mixhi_made, g + 1)
            for dst, high, src in zip(by_tokens(x_lo, g), by_tokens(x_hi, g), by_positions(ext, g)):
                last = G.tensor_tensor(dst, src, high.bitcast(F32), ALU.subtract)
            last.then_inc(mix_ready, 1)
        add_squares(1)
        residual(0)
        clear_y(1)
        pool.wait_ge(b1_sum, 1)
        pool.wait_ge(cmp_pre, 2)
        pool.dma_start(oh[:, :], onehot[:, :]).then_inc(oh_in, 16)
        pool.dma_start(flip[:, :, :], flips[:, :, :]).then_inc(oh_in, 16)
        ffn(3)
        residual(1)
        pool.wait_ge(trow_made, 1)
        pool.dma_start(bias_dram[:, :], trow[:, :]).then_inc(trow_out, 16)
        pool.wait_ge(tile_made, P_WO + TOFF)
        G.memset(bias_n[:, :, :], NEG)
        G.memset(biasC[:, :, :, :], NEG).then_inc(mask_set, 1)
        pool.wait_ge(bank_read[(P_WO - 1) % 2], (P_WO - 1 + TOFF) // 2 + 1)
        for b in range(DB):
            last = G.tensor_copy(qS[:, b, :, :], qT[:, :, SEQ + b * DS:SEQ + (b + 1) * DS])
        last.then_inc(qS_made, 1)

        for u in range(UNITS):
            s3 = u % 3
            pool.wait_ge(rec_made, u + 1)
            o, f = sc[:, s3, :], rec[:, s3, :]
            if u < NH:
                v = pick(o, 0, 272, 2, NCMP)
                G.tensor_tensor(v, v, spread(pick(f, 0, 3, 2, 1)[:, :, 0], NCMP), ALU.mult)
                v = o[:, 16:272].rearrange("p (r k) -> p r k", r=2)
                G.tensor_tensor(v, v, spread(f[:, 1:3], P), ALU.mult)
                v = o[:, 288:800].rearrange("p (r k) -> p r k", r=2)
                G.tensor_tensor(v, v, spread(f[:, 4:6], SEQ), ALU.mult).then_inc(p_made, 1)
            else:
                W = PAST + NEW
                v = o[:, 0:NCMP]
                G.tensor_tensor(v, v, f[:, 0:1].broadcast_to([P, NCMP]), ALU.mult)
                v = o[:, 16:16 + 2 * W].rearrange("p (r k) -> p r k", r=2)
                G.tensor_tensor(v, v, spread(f[:, 1:3], W), ALU.mult).then_inc(p_made, 1)
        pool.wait_ge(o_made, UNITS)
        add_squares(5)
        residual(2)
        clear_y(3)
        ffn(7)
        for i in BY_POOL:
            pool.wait_ge(yn_made, 16 * 3 + i + 1)
            G.tensor_tensor(h[:, i, :], h[:, i, :], y[:, i, :], ALU.add).then_inc(y_pool, 1)

    @block.tensor
    def _(pe):
        M = nc.tensor.matmul
        T = nc.tensor.transpose

        def tile(c, half, kt, xh, xl, ready=None, used=None):
            slot = c % 2
            pe.wait_ge(lo_made, half * 2 + (c + 1))
            if not isinstance(half, int) or c + TOFF + 2 * half >= 2:
                pe.wait_ge(bank_read[slot], half + (c + TOFF) // 2)
            out = ps[:, slot, 0:NT]
            for k in range(kt):
                if ready:
                    ready(k)
                wh, wl = w_hi[:, slot, k * P:(k + 1) * P], w_lo[:, slot, k * P:(k + 1) * P]
                M(out, wh, xh[:, k, :], start=(k == 0), stop=False)
                M(out, wh, xl[:, k, :], start=False, stop=False)
                last = M(out, wl, xh[:, k, :], start=False, stop=(k == kt - 1))
                if used and k < kt - 1:
                    last.then_inc(used, 1)
            last.then_inc(tile_made, 1)

        def first_tile(c, ready, m):
            slot = c % 2
            pe.wait_ge(lo_made, c + 1)
            pe.wait_ge(bank_read[slot], (c + TOFF) // 2)
            for k in range(KT):
                square_sum(m, k)
                ready(k)
                wh, wl = w_hi[:, slot, k * P:(k + 1) * P], w_lo[:, slot, k * P:(k + 1) * P]
                M(ps[:, slot, 0:NT], wh, x_hi[:, k, :], start=(k == 0), stop=False)
                M(ps[:, slot, 0:NT], wh, x_lo[:, k, :], start=False, stop=False)
                last = M(ps[:, slot, 0:NT], wl, x_hi[:, k, :], start=False, stop=(k == KT - 1))
            last.then_inc(tile_made, 1)

        def square_sum(m, i):
            pe.wait_ge(sq_made, 16 * m + i + 1)
            M(ps[:, STAT, 0:NT], ones[:, :], sq[:, i % 2, :], start=(i == 0),
              stop=(i == KT - 1)).then_inc(sq_used if i < KT - 1 else stat_made, 1)

        def acc_sum(m):
            pe.wait_ge(acc_made, KT * (m // 2 + 1))
            M(ps[:, STAT, 0:NT], ones[:, :], acc[:, :], start=True, stop=False)
            pe.wait_ge(sq_made, KT * (m + 1))
            M(ps[:, STAT, 0:NT], ones[:, :], sq[:, (KT - 1) % 2, :], start=False, stop=True).then_inc(stat_made, 1)

        def x_ready(k):
            return lambda i: pe.wait_ge(x_made, 16 * k + i + 1)

        def ffn(c, k, m, hid_before):
            def quarter(q19, hid_need):
                def hidden(k):
                    if k == 0:
                        pe.wait_ge(hid_made, hid_need)
                    if k == HQ - 1:
                        pe.wait_ge(hid_made, hid_need + 1)
                with pe.Fori(0, KT // 2) as i:
                    for j in range(2):
                        tile(c + 2 * HQ + j, q19 + i, HQ, hid_hi, hid_lo, None if j else hidden)
            if m == 2:
                tile(c, 0, KT, x_hi, x_lo, x_ready(k))
            else:
                first_tile(c, x_ready(k), m)
            tile(c + 1, 0, KT, x_hi, x_lo)
            with pe.Fori(1, HQ) as i:
                for j in range(2):
                    tile(c + j, i, KT, x_hi, x_lo)
            quarter(0, hid_before + HQ)
            with pe.Fori(1, NQ) as q:
                with pe.Fori(0, HQ) as i:
                    for j in range(2):
                        tile(c + j, q * (PER_Q // 2) + i, KT, x_hi, x_lo)
                quarter(q * (PER_Q // 2), q * HQ + (hid_before + HQ))

        def compress(bank, w1, rows, half, j):
            n, w = NP_ALL // 2, NP_ALL * 16
            return M(ps[:, bank + j // CS, half * w:(half + 1) * w], w1[:, j, :], rows[:, half * n:(half + 1) * n, j % CS, :],
                     start=(j % CS == 0), stop=(j % CS == CS - 1))

        def pos_bias(c, w1):
            for j in range(CB):
                last = M(ps[0:1, 6, c * P:(c + 1) * P], pos[:, c, j:j + 1], w1[:, j, :], start=(j == 0), stop=(j == CB - 1))
            return last

        pe.wait_ge(set_made, 1)
        for i in range(KT):
            square_sum(0, i)
        pe.wait_ge(pos_in, 16)
        for half in range(2):
            pe.wait_ge(cmpK_in[half], 16 * (NP_ALL // 2 + 1 - half))
            if half == 0:
                pos_bias(0, w1K)
            for j in range(CB):
                last = compress(2, w1K, rowsK, half, j)
        last.then_inc(cmp_sum, 1)

        pe.wait_ge(w1Vy_in, 16)
        pos_bias(1, w1Vy).then_inc(brow_sum, 1)
        pe.wait_ge(brow_made, 1)
        for c in range(2):
            last = M(ps[:, 6, 2 * P + c:2 * P + c + 1], brow[0:1, c * P:(c + 1) * P], ones[0:1, 0:1], start=True, stop=True)
        last.then_inc(b1_sum, 1)

        for g in range(NG):
            pe.wait_ge(lo_made, g + 1)
            pe.wait_ge(mix_ready, g + 1)
            for n in range(GC):
                t = g * GC + n
                if t >= 2:
                    pe.wait_ge(bank_read[t % 2], t // 2)
                for k in range(GC):
                    o = (n * GC + k) * P
                    wh, wl = w_hi[:, g % 2, o:o + P], w_lo[:, g % 2, o:o + P]
                    M(ps[:, t % 2, 0:NT], wh, x_hi[:, g * GC + k, :], start=(k == 0), stop=False)
                    M(ps[:, t % 2, 0:NT], wh, x_lo[:, g * GC + k, :], start=False, stop=False)
                    last = M(ps[:, t % 2, 0:NT], wl, x_hi[:, g * GC + k, :], start=False, stop=(k == GC - 1))
                last.then_inc(tile_made, 1)
        pe.wait_ge(const_in, 16 * 6)
        pe.wait_ge(cmp_hid, 1)
        M(ps[:, 2, 0:DB * NKV * NCMP], w2[:, 0, :], hcS[:, 0, :], start=True, stop=True).then_inc(kc_sum, 1)
        pe.wait_ge(w1V_in, 16)
        pe.wait_ge(cmpV_in, 16 * NP_ALL)
        steps = iter([(half, j) for half in range(2) for j in range(CB)])

        def values(n):
            for _ in range(n):
                last = compress(4, w1V, rowsV, *next(steps))
            return last
        values(10)
        acc_sum(1)
        values(14)
        for i in range(KT):
            square_sum(2, i)
            values(2)
        values(8).then_inc(cmp_sum, 1)
        ffn(P_FFN0, 0, 2, 0)
        acc_sum(3)
        first_tile(P_KV, x_ready(1), 4)
        tile(P_KV + 1, 0, KT, x_hi, x_lo)
        with pe.Fori(1, N_KVT // 2 - 1) as i:
            for j in range(2):
                tile(P_KV + j, i, KT, x_hi, x_lo)
        tile(P_Q - 2, 0, KT, x_hi, x_lo)
        tile(P_Q - 1, 0, KT, x_hi, x_lo, used=x_used)
        pe.wait_ge(oh_in, 32)
        pe.wait_ge(tab_made, 1)
        M(ps[0:NH, 2, :], tab[:, :], oh[:, 0:512], start=True, stop=True)
        M(ps[0:NH, 3, 0:NE - 512], tab[:, :], oh[:, 512:NE], start=True, stop=True).then_inc(trow_sum, 1)
        tile(P_Q, 0, KT, x_hi, x_lo, x_ready(2))
        tile(P_Q + 1, 0, KT, x_hi, x_lo)
        with pe.Fori(1, NH // 2) as i:
            for j in range(2):
                tile(P_Q + j, i, KT, x_hi, x_lo)
        tile(P_Q + NH, 0, KT, x_hi, x_lo)

        for c, w1, w1_in in ((1, w1Vp, w1Vp_in), (0, w1Kp, w1Kp_in)):
            pe.wait_ge(w1_in, 16)
            for j in range(CB):
                rows = kvT[:, c * NKV:(c + 1) * NKV, :].rearrange("p h t -> p (h t)")[:, j % CS:j % CS + NROW * CS - CS + 1:CS]
                last = M(ps[0:NROW, 2 + c, P * (j // CS):P * (j // CS) + P], rows, w1[:, j, :],
                         start=(j % CS == 0), stop=(j % CS == CS - 1))
            last.then_inc(crow_sum, 1)

        def turn_sums(n, c):
            pe.wait_ge(crow_made, n + 1)
            for half in range(2):
                last = T(ps[:, 2 + c, half * P:half * P + NROW], crow[:, c, half * P:(half + 1) * P],
                         ident[0:NROW, 0:NROW])
            last.then_inc(cmp_sum, 1)

        for n in range(4):
            br, t = n // 2, n % 2
            if n in (1, 2):
                turn_sums(n - 1, 2 - n)
            if n >= 2:
                pe.wait_ge(vt_made, n - 1)
            for v in range(NKV):
                src = kvT[:, (br + 1) * 2 * NKV + NKV + v, t * P:(t + 1) * P]
                last = T(ps[:, 4 + n % 2, v * HD:(v + 1) * HD], src, ident)
            last.then_inc(vt_sum, 1)
        pe.wait_ge(vt_made, 3)
        for br in range(2):
            for v in range(NKV):
                src = kvT[:, (br + 1) * 2 * NKV + NKV + v, SEQ:NT]
                last = M(ps[br * NS:(br + 1) * NS, 4, v * HD:(v + 1) * HD], src, ident, start=True, stop=True)
        last.then_inc(vt_sum, 1)
        pe.wait_ge(sig_made, 1)
        for t in range(2):
            T(ps[:, 6, t * 3 * NH:(t + 1) * 3 * NH], gT[0:3 * NH, t * P:(t + 1) * P], ident[0:3 * NH, 0:3 * NH])
        for br in range(NBR):
            last = M(ps[:, 7, br * NS:(br + 1) * NS], cst[0:3 * NH, C_HS + br * P:C_HS + (br + 1) * P],
                     gT[0:3 * NH, SEQ:NT], start=True, stop=True)
        last.then_inc(g_sum, 1)

        pe.wait_ge(rev_in, 32)
        for n in range(NH // 2):
            if n >= 2:
                pe.wait_ge(bias_made, n - 1)
            M(ps[:, n % 2, :], flip[:, 0, :], revP[:, 2 * n:2 * n + 2, :], start=True, stop=True).then_inc(bias_sum, 1)
        pe.wait_ge(cmp_hid, 4)
        M(ps[:, 2, 0:PAST + DS], flip[:, 1, :], revS[:, :], start=True, stop=True).then_inc(bias_sum, 1)
        pe.wait_ge(vt_made, 5)
        M(ps[:, 4, 0:NKV * NCMP], w2[:, 0, :], hcP[:, 0, :], start=True, stop=True)
        for v in range(NKV):
            last = M(ps[0:NCMP, 5, v * HD:(v + 1) * HD], hcP[:, 1, v * NCMP:(v + 1) * NCMP], w2[:, 1, :],
                     start=True, stop=True)
        last.then_inc(kc_sum, 1)
        pe.wait_ge(kc_made, 2)
        pe.wait_ge(gates_made, 1)
        pe.wait_ge(bias_made, NH // 2 + 1)
        pe.wait_ge(qS_made, 1)

        def kT(br, v):
            return kvT[:, (br + 1) * 2 * NKV + v, :]

        def scores(u):
            a = 2 * (u % 2)
            if u >= 2:
                pe.wait_ge(s_read, u - 1)
            if u < NH:
                v = u // GQ
                q0, q1 = qT[:, u, 0:P], qT[:, u, P:SEQ]
                both = kvT[:, 2 * NKV:, :].rearrange("p (r c v) t -> p r c v t", r=2, c=2)[:, :, 0, v, :]
                M(ps[:, a, 0:SEQ], q0, both[:, :, 0:P], start=True, stop=True)
                M(ps[:, a, 256:256 + NCMP], q0, kcP[:, v * NCMP:(v + 1) * NCMP], start=True, stop=True)
                M(ps[:, a, 272:272 + NCMP], q1, kcP[:, v * NCMP:(v + 1) * NCMP], start=True, stop=True)
                M(ps[:, a + 1, :], q1, both[:, :, 0:SEQ], start=True, stop=True).then_inc(s_made, 1)
                return
            b = u - NH
            pe.wait_ge(pastK_in[b % 2], 48 * (b // 2 + 1))
            for v in range(NKV):
                q = qS[:, b, v * GQ:(v + 1) * GQ, :].rearrange("p h i -> p (h i)")
                rows = slice(32 * v, 32 * v + 32)
                for br in range(2):
                    M(ps[rows, a + br, 0:PAST], q, pastK[b % 2][:, br, v, :], start=True, stop=True)
                    M(ps[rows, a + br, PAST:PAST + NEW], q, kT(br, v)[:, SEQ:NT], start=True, stop=True)
                o = (b * NKV + v) * NCMP
                last = M(ps[rows, a, PAST + NEW:PAST + NEW + NCMP], q, kcS[:, o:o + NCMP], start=True, stop=True)
            last.then_inc(s_made, 1)

        def transposes(u):
            pe.wait_ge(p_made, u + 1)
            if u:
                pe.wait_ge(pTa_made, u)
                pe.wait_ge(pTb_made, u)
            o = sc[:, u % 3, :]
            if u < NH:
                for n, lo in enumerate((16, 288, 144, 544)):
                    T(ps[:, 4, n * P:(n + 1) * P], o[:, lo:lo + P], ident)
                for n, lo in enumerate((416, 672)):
                    T(ps[:, 5, n * P:(n + 1) * P], o[:, lo:lo + P], ident)
                T(ps[0:NCMP, 5, 256:384], o[:, 0:NCMP], ident)
                T(ps[0:NCMP, 5, 384:512], o[:, 272:272 + NCMP], ident).then_inc(t_made, 1)
                return
            W = PAST + NEW
            for br in range(2):
                for t in range(2):
                    n = br * 2 + t
                    lo = 16 + br * (W + NEW) + t * P
                    T(ps[:, 4, n * P:(n + 1) * P], o[:, lo:lo + P], ident)
            T(ps[:, 5, 0:P], o[:, 16 + PAST:16 + PAST + 2 * NEW], ident)
            T(ps[0:NCMP, 5, 256:384], o[:, 0:NCMP], ident).then_inc(t_made, 1)
            b = u - NH
            if b:
                pe.wait_ge(vc_made, b)
            else:
                pe.wait_ge(o_read, NH - 1)
            for v in range(NKV):
                o_ = (b * NKV + v) * NCMP
                last = M(ps[0:NCMP, 7, v * HD:(v + 1) * HD], hcS[:, 1, o_:o_ + NCMP], w2[:, 1, :], start=True, stop=True)
            last.then_inc(vc_sum, 1)

        def outputs(u):
            pe.wait_ge(pTa_made, u + 1)
            pe.wait_ge(pTb_made, u + 1)
            if u >= 2:
                pe.wait_ge(o_read, u - 1 if u < NH else u)
            p = pT[:, u % 2, :]
            if u < NH:
                v = slice((u // GQ) * HD, (u // GQ + 1) * HD)
                O = ps[:, out_bank(u), 0:SEQ]
                M(O, vP[:, 0, 0, v], p[:, 0:256], start=True, stop=False)
                M(O, vP[:, 1, 0, v], p[:, 256:512], start=False, stop=False)
                M(O, vCP[:, v], p[0:NCMP, 768:1024], start=False, stop=False)
                M(O[:, P:SEQ], vP[:, 0, 1, v], p[:, 512:640], start=False, stop=False)
                M(O[:, P:SEQ], vP[:, 1, 1, v], p[:, 640:768], start=False, stop=True).then_inc(o_made, 1)
                return
            b = u - NH
            pe.wait_ge(pastV_in[b % 2], 48 * (b // 2 + 1))
            pe.wait_ge(vc_made, b + 1)
            for n in range(NKV):
                v = slice(n * HD, (n + 1) * HD)
                O = ps[32 * n:32 * n + 32, 6, 0:HD]
                for br in range(2):
                    for t in range(2):
                        c0 = (br * 2 + t) * P + 32 * n
                        M(O, p[:, c0:c0 + 32], pastV[b % 2][:, br, t, v], start=(br == 0 and t == 0), stop=False)
                M(O, p[:, 512 + 32 * n:544 + 32 * n], vN[:, v], start=False, stop=False)
                last = M(O, p[0:NCMP, 768 + 32 * n:800 + 32 * n], vC[u % 2][:, v], start=False, stop=True)
            last.then_inc(o_made, 1)

        def turn_outputs(b):
            pe.wait_ge(oN_made, b + 1)
            T(ps[:, 6, P:2 * P], oN[:, :], ident).then_inc(oN_sum, 1)

        for s in range(UNITS + 4):
            if s < UNITS:
                scores(s)
            if s >= NH + 4:
                turn_outputs(s - 4 - NH)
            if 2 <= s < UNITS + 2:
                transposes(s - 2)
            if 3 <= s < UNITS + 3:
                outputs(s - 3)

        pe.wait_ge(o_read, UNITS)
        with pe.Fori(0, KT // 2) as i:
            for j in range(2):
                tile(P_WO + j, i, KT, x_hi, x_lo)
        acc_sum(5)
        ffn(P_FFN1, 3, 6, HT)
        acc_sum(7)

    block_ctx.close()


_IN_NAMES = ("x", "st", "gains", "consts", "onehot", "rel", "w_pool", "w_in0", "w_in1", "w_out0", "w_out1", "w_kv", "w_q",
             "w_o", "flips", "cmp_data", "cmp_w1", "cmp_pos", "cmp_b1", "cmp_w2", "slc_k", "slc_kv", "win_k", "win_kv", "pages")
_OUTS = (("y_out", (P, KT, NT)), ("pool_p_out", (P, KT, BUF)), ("pool_s_out", (P, KT, DB, BUF)),
         ("kv_out", (P, N_KVT, NT)), ("win_out", (DB, PAST - DS, 2 * NKV * HD)))


def bucket(dist):
    n = np.maximum(dist, 0)
    exact = NBUCK // 2
    big = exact + (np.log(np.maximum(n, 1).astype(np.float32) / exact) / np.log(np.float32(128 / exact)) * (NBUCK - exact)).astype(np.int32)
    return np.where(n < exact, n, np.minimum(big, NBUCK - 1))


def shape_constants():
    c = np.zeros((P, C_N), np.float32)
    c[:, C_ID:C_ID + P] = np.eye(P)
    row, col = np.arange(P)[:, None], np.arange(NS)[None, :]
    c[:, C_IM:C_IM + NS] = row % DS == col % DS
    for br in range(NBR):
        c[:3 * NH, C_HS + br * P:C_HS + (br + 1) * P] = np.arange(3 * NH)[:, None] == br * NH + np.arange(P)[None, :] // DS
    for g in range(NG):
        w = 2 ** (g + 1)
        c[:, C_INV + g * NT:C_INV + g * NT + SEQ] = np.float32(1) / np.minimum(w, np.arange(SEQ) + 1).astype(np.float32)
        c[:, C_INV + g * NT + SEQ:C_INV + (g + 1) * NT] = np.float32(1) / w
    c[:, C_RV] = np.arange(P) >= CB - 1
    hot = np.zeros((NBUCK + 1, NE), np.float32)
    d = PAST + DS - 1 - np.arange(NE)
    hot[np.where(d < 0, NBUCK, bucket(d)), np.arange(NE)] = 1
    flip = np.zeros((P, 2, P), np.float32)
    flip[np.arange(P), 0, P - 1 - np.arange(P)] = 1
    flip[np.arange(P), 1, np.arange(P) // DS * DS + DS - 1 - np.arange(P) % DS] = 1
    return c, hot, flip


def kernel(**inputs):
    import concourse.bacc as bacc
    from concourse.bass_utils import run_bass_kernel_spmd

    a = {k: np.asarray(v) for k, v in inputs.items()}

    def chunks(m):
        t = m.reshape(-1, KT, P).transpose(2, 1, 0)
        return t.reshape(P, KT, *m.shape[:-1])

    def panels(w, kt):
        k, n = w.shape
        return w.reshape(kt, P, n // P, P).transpose(2, 1, 0, 3).reshape(n // P, P, kt * P)

    def ffn_in(w):
        gate, up = panels(w[:, :DFF], KT), panels(w[:, DFF:], KT)
        return np.stack([gate, up], 1).reshape(2 * HT, P, PW)

    def ffn_out(w):
        return np.concatenate([panels(w[q * HQ * P:(q + 1) * HQ * P], HQ) for q in range(NQ)])

    consts, hot, flip = shape_constants()
    x_all = np.concatenate([a["x_prompt"].reshape(SEQ, D), a["x_sample"].reshape(NS, D)])
    norms = a["norms"].reshape(8, D)
    gains = np.concatenate([norms, a["pool_scale"].reshape(1, D), a["kv_norm"].reshape(1, D)])
    w_q = a["w_q"][0]
    w_q = np.concatenate([w_q, np.zeros((D, N_QT * P - w_q.shape[1]), w_q.dtype)], 1)
    cmp_rows = a["cache_cmp_kv"]
    n_pages = cmp_rows.shape[0]
    arrays = {
        "x": chunks(x_all),
        "st": chunks(a["state_pool"][0].reshape(DB * BUF, D)).reshape(P, KT, DB, BUF),
        "gains": gains.reshape(10, KT, P).transpose(2, 0, 1),
        "consts": consts, "onehot": hot, "flips": flip, "rel": a["rel_bias"],
        "w_pool": a["w_pool"][0].reshape(NG, GC, P, GC, P).transpose(0, 2, 3, 1, 4).reshape(NG, P, PW),
        "w_in0": ffn_in(a["w_ffn_in"][0]), "w_in1": ffn_in(a["w_ffn_in"][1]),
        "w_out0": ffn_out(a["w_ffn_out"][0]), "w_out1": ffn_out(a["w_ffn_out"][1]),
        "w_kv": panels(a["w_kv"], KT), "w_q": panels(w_q, KT), "w_o": panels(a["w_o"][0], KT),
        "cmp_data": cmp_rows.reshape(n_pages, PAGE // CS, CS, 2, NKV, HD).transpose(3, 0, 5, 2, 4, 1).reshape(
            2, n_pages, P, CS, NKV * PAGE // CS),
        "cmp_w1": a["cmp_w1"].transpose(0, 2, 1, 3), "cmp_pos": a["cmp_pos"].transpose(2, 0, 1),
        "cmp_b1": a["cmp_b1"].T, "cmp_w2": a["cmp_w2"].transpose(1, 0, 2),
        "slc_k": a["cache_slc_kv"][:, :, 0].transpose(0, 3, 2, 1),
        "slc_kv": a["cache_slc_kv"].reshape(n_pages, PAGE, 2, NKV * HD),
        "win_k": a["state_win_kv"][:, :, 0].transpose(0, 3, 2, 1),
        "win_kv": a["state_win_kv"].reshape(DB, PAST, 2, NKV * HD),
        "pages": a["page_table"].reshape(1, DB * NPG),
    }
    nc = bacc.Bacc("TRN2", target_bir_lowering=False, num_devices=1)
    args, sent = [], {}
    for name in _IN_NAMES:
        v = np.ascontiguousarray(arrays[name])
        sent[name + "_dram"] = v
        args.append(nc.dram_tensor(name + "_dram", v.shape, mybir.dt.from_np(v.dtype), kind="ExternalInput").ap())
    for name, shape in _OUTS:
        args.append(nc.dram_tensor(name + "_dram", shape, F32, kind="ExternalOutput").ap())
    build(nc, *args)
    got = run_bass_kernel_spmd(nc, [sent], core_ids=[0]).results[0]
    yt, pool_p, pool_s, kv, win = (got[name + "_dram"] for name, _ in _OUTS)

    y_all = yt.transpose(2, 1, 0).reshape(NT, D)
    kv = kv.transpose(2, 1, 0).reshape(NT, NBR, 2, NKV, HD)
    kv_p, kv_s = kv[:SEQ].reshape(1, SEQ, NBR, 2, NKV, HD), kv[SEQ:].reshape(DB, DS, NBR, 2, NKV, HD)
    win_s = np.concatenate([win.reshape(DB, PAST - DS, 2, NKV, HD), kv_s[:, :, 2]], 1)
    return (y_all[:SEQ].reshape(1, SEQ, D), y_all[SEQ:].reshape(DB, DS, D),
            pool_p.transpose(2, 1, 0).reshape(1, 1, BUF, D), pool_s.transpose(2, 3, 1, 0).reshape(1, DB, BUF, D),
            kv_p[:, :, 0], kv_s[:, :, 0], kv_p[:, :, 1], kv_s[:, :, 1], kv_p[:, :, 2], win_s)
```
